# Optimizing a Trainium2 kernel written in Bass

```python
import math
import jax, jax.numpy as jnp
from jax import lax
import numpy as np

D_MODEL = 1024
BATCH = 1
SEQ = 256
DEPTH = 2

N_MIXERS = 2
MLA_HEADS = 8
MLA_Q_RANK = 384
MLA_KV_RANK = 256
MLA_NOPE_DIM = 128
MLA_ROPE_DIM = 64
MLA_V_DIM = 128
ROPE_THETA = 10000.0
MOBA_HEADS = 8
MOBA_HEAD_DIM = D_MODEL // MOBA_HEADS
MOBA_BLOCK = 256
MOBA_TOP_K = 3
REL_BUCKETS = 32
REL_MAX_DISTANCE = 1024
D_FF = 4 * D_MODEL
Q_BLOCK = 128
RMS_EPS = 1e-6
N_MLA_LAYERS = (DEPTH + 1) // 2
N_MOBA_LAYERS = DEPTH // 2


def rms_norm(x, g):
    xf = x.astype(jnp.float32)
    y = xf * lax.rsqrt(jnp.mean(xf * xf, axis=-1, keepdims=True) + RMS_EPS)
    return (y * g.astype(jnp.float32)).astype(x.dtype)

def rope_tables(positions):
    inv_freq = ROPE_THETA ** (-jnp.arange(0, MLA_ROPE_DIM, 2, dtype=jnp.float32) / MLA_ROPE_DIM)
    ang = positions.astype(jnp.float32)[..., None] * inv_freq
    return jnp.cos(ang), jnp.sin(ang)

def rope(x, cos, sin):
    half = x.shape[-1] // 2
    x1 = x[..., :half].astype(jnp.float32)
    x2 = x[..., half:].astype(jnp.float32)
    return jnp.concatenate([x1 * cos - x2 * sin, x2 * cos + x1 * sin], axis=-1).astype(x.dtype)

def t5_bucket(dist):
    n = jnp.maximum(dist, 0)
    max_exact = REL_BUCKETS // 2
    nf = jnp.maximum(n, 1).astype(jnp.float32)
    large = max_exact + (jnp.log(nf / max_exact) / math.log(REL_MAX_DISTANCE / max_exact)
                         * (REL_BUCKETS - max_exact)).astype(jnp.int32)
    large = jnp.minimum(large, REL_BUCKETS - 1)
    return jnp.where(n < max_exact, n, large)

def sq_relu_mlp(h, w_in, w_out):
    a = jax.nn.relu(h @ w_in)
    return (a * a) @ w_out

def mla_attention(q_nope, q_pe, k_nope, k_pe, v):
    B, H, S, _ = q_nope.shape
    nqb = S // Q_BLOCK
    scale = 1.0 / math.sqrt(MLA_NOPE_DIM + MLA_ROPE_DIM)
    k_idx = jnp.arange(S)

    def to_blocks(t):
        return jnp.moveaxis(t.reshape(B, H, nqb, Q_BLOCK, t.shape[-1]), 2, 0)

    def body(args):
        qn, qp, c = args
        logits = (jnp.einsum('bhqd,bhkd->bhqk', qn, k_nope)
                  + jnp.einsum('bhqd,bkd->bhqk', qp, k_pe)).astype(jnp.float32) * scale
        q_idx = c * Q_BLOCK + jnp.arange(Q_BLOCK)
        causal = k_idx[None, :] <= q_idx[:, None]
        logits = jnp.where(causal, logits, -jnp.inf)
        p = jax.nn.softmax(logits, axis=-1).astype(v.dtype)
        return jnp.einsum('bhqk,bhkd->bhqd', p, v)

    out = lax.map(body, (to_blocks(q_nope), to_blocks(q_pe), jnp.arange(nqb, dtype=jnp.int32)))
    return jnp.moveaxis(out, 0, 2).reshape(B, H, S, v.shape[-1])

def mla_mixer(h, w_in, q_a_norm, kv_a_norm, w_uq, w_ukv, q_nope_norm, q_rope_norm,
              k_nope_norm, k_rope_norm, w_o, cos, sin):
    B, S, _ = h.shape
    proj = h @ w_in
    c_q = proj[..., :MLA_Q_RANK]
    c_kv = proj[..., MLA_Q_RANK:MLA_Q_RANK + MLA_KV_RANK]
    k_pe = proj[..., MLA_Q_RANK + MLA_KV_RANK:]
    q = (rms_norm(c_q, q_a_norm) @ w_uq).reshape(B, S, MLA_HEADS, MLA_NOPE_DIM + MLA_ROPE_DIM)
    kv = (rms_norm(c_kv, kv_a_norm) @ w_ukv).reshape(B, S, MLA_HEADS, MLA_NOPE_DIM + MLA_V_DIM)
    q_nope = rms_norm(q[..., :MLA_NOPE_DIM], q_nope_norm)
    q_pe = rope(rms_norm(q[..., MLA_NOPE_DIM:], q_rope_norm), cos[:, :, None, :], sin[:, :, None, :])
    k_nope = rms_norm(kv[..., :MLA_NOPE_DIM], k_nope_norm)
    v = kv[..., MLA_NOPE_DIM:]
    k_pe = rope(rms_norm(k_pe, k_rope_norm), cos, sin)
    out = mla_attention(q_nope.transpose(0, 2, 1, 3), q_pe.transpose(0, 2, 1, 3),
                        k_nope.transpose(0, 2, 1, 3), k_pe, v.transpose(0, 2, 1, 3))
    return out.transpose(0, 2, 1, 3).reshape(B, S, MLA_HEADS * MLA_V_DIM) @ w_o

def moba_attention(q, k, v, positions, rel_bias_table):
    B, H, S, dh = q.shape
    nb = -(-S // MOBA_BLOCK)
    pad = nb * MOBA_BLOCK - S
    n_sel = min(MOBA_TOP_K, nb - 1)
    nqb = S // Q_BLOCK
    scale = 1.0 / math.sqrt(dh)
    kb = jnp.pad(k, ((0, 0), (0, 0), (0, pad), (0, 0))).reshape(B, H, nb, MOBA_BLOCK, dh)
    vb = jnp.pad(v, ((0, 0), (0, 0), (0, pad), (0, 0))).reshape(B, H, nb, MOBA_BLOCK, dh)
    k_mean = jnp.mean(kb.astype(jnp.float32), axis=3)
    pos_b = jnp.pad(positions, ((0, 0), (0, pad)), mode='edge').reshape(B, nb, MOBA_BLOCK)
    pos_q = jnp.moveaxis(positions.reshape(B, nqb, Q_BLOCK), 1, 0)
    q_blocks = jnp.moveaxis(q.reshape(B, H, nqb, Q_BLOCK, dh), 2, 0)
    table_h = rel_bias_table.T
    b_i = jnp.arange(B)[:, None, None]
    h_i = jnp.arange(H)[None, :, None]
    h_i4 = jnp.arange(H)[None, :, None, None]
    blk_ids = jnp.arange(nb)
    t_ids = jnp.arange(MOBA_BLOCK)

    def rel_bias(pq, pk):
        return table_h[h_i4, t5_bucket(pq - pk)].astype(jnp.float32)

    def body(args):
        qi, pq, c = args
        q_start = c * Q_BLOCK
        own = q_start // MOBA_BLOCK
        q_idx = q_start + jnp.arange(Q_BLOCK)
        pq4 = pq[:, None, :, None]
        parts = []
        sel = None
        if n_sel > 0:
            gate = jnp.einsum('bhqd,bhnd->bhqn', qi.astype(jnp.float32), k_mean)
            gate = jnp.where(blk_ids < own, gate, -jnp.inf)
            _, sel = lax.top_k(gate, n_sel)
            for r in range(n_sel):
                sel_r = sel[..., r]
                k_sel = kb[b_i, h_i, sel_r]
                lg = (jnp.einsum('bhqd,bhqtd->bhqt', qi, k_sel).astype(jnp.float32) * scale
                      + rel_bias(pq4, pos_b[b_i, sel_r]))
                parts.append(jnp.where(r < own, lg, -jnp.inf))
        k_own = lax.dynamic_index_in_dim(kb, own, axis=2, keepdims=False)
        v_own = lax.dynamic_index_in_dim(vb, own, axis=2, keepdims=False)
        pos_own = lax.dynamic_index_in_dim(pos_b, own, axis=1, keepdims=False)
        lg_own = (jnp.einsum('bhqd,bhtd->bhqt', qi, k_own).astype(jnp.float32) * scale
                  + rel_bias(pq4, pos_own[:, None, None, :]))
        causal = (own * MOBA_BLOCK + t_ids)[None, :] <= q_idx[:, None]
        parts.append(jnp.where(causal, lg_own, -jnp.inf))
        p = jax.nn.softmax(jnp.concatenate(parts, axis=-1), axis=-1).astype(v.dtype)
        p = p.reshape(B, H, Q_BLOCK, n_sel + 1, MOBA_BLOCK)
        out = jnp.einsum('bhqt,bhtd->bhqd', p[..., n_sel, :], v_own)
        for r in range(n_sel):
            v_sel = vb[b_i, h_i, sel[..., r]]
            out = out + jnp.einsum('bhqt,bhqtd->bhqd', p[..., r, :], v_sel)
        return out

    out = lax.map(body, (q_blocks, pos_q, jnp.arange(nqb, dtype=jnp.int32)))
    return jnp.moveaxis(out, 0, 2).reshape(B, H, S, dh)

def moba_mixer(h, w_qkv, q_norm, k_norm, w_o, positions, rel_bias_table):
    B, S, _ = h.shape
    qkv = (h @ w_qkv).reshape(B, S, 3, MOBA_HEADS, MOBA_HEAD_DIM)
    q = rms_norm(qkv[:, :, 0], q_norm).transpose(0, 2, 1, 3)
    k = rms_norm(qkv[:, :, 1], k_norm).transpose(0, 2, 1, 3)
    v = qkv[:, :, 2].transpose(0, 2, 1, 3)
    out = moba_attention(q, k, v, positions, rel_bias_table)
    return out.transpose(0, 2, 1, 3).reshape(B, S, MOBA_HEADS * MOBA_HEAD_DIM) @ w_o

def first_inputs(seed: int = 0) -> dict:
    key = jax.random.key(seed)
    ks = jax.random.split(key, 24)

    def nrm(k, shape, scale):
        return scale * jax.random.normal(k, shape, jnp.float32)

    def gain(k, shape):
        return 1.0 + 0.05 * jax.random.normal(k, shape, jnp.float32)

    qk_dim = MLA_NOPE_DIM + MLA_ROPE_DIM
    offset = jax.random.randint(ks[1], (BATCH,), 0, 4096, dtype=jnp.int32)
    positions = offset[:, None] + jnp.arange(SEQ, dtype=jnp.int32)[None, :]
    return {
        "x": nrm(ks[0], (BATCH, SEQ, D_MODEL), 1.0),
        "positions": positions,
        "rel_bias_table": nrm(ks[2], (REL_BUCKETS, MOBA_HEADS), 0.5),
        "attn_norm": gain(ks[3], (DEPTH, D_MODEL)),
        "mlp_norm": gain(ks[4], (DEPTH, D_MODEL)),
        "mla_w_in": nrm(ks[5], (N_MLA_LAYERS, D_MODEL, MLA_Q_RANK + MLA_KV_RANK + MLA_ROPE_DIM), D_MODEL ** -0.5),
        "mla_q_a_norm": gain(ks[6], (N_MLA_LAYERS, MLA_Q_RANK)),
        "mla_kv_a_norm": gain(ks[7], (N_MLA_LAYERS, MLA_KV_RANK)),
        "mla_w_uq": nrm(ks[8], (N_MLA_LAYERS, MLA_Q_RANK, MLA_HEADS * qk_dim), MLA_Q_RANK ** -0.5),
        "mla_w_ukv": nrm(ks[9], (N_MLA_LAYERS, MLA_KV_RANK, MLA_HEADS * (MLA_NOPE_DIM + MLA_V_DIM)), MLA_KV_RANK ** -0.5),
        "mla_q_nope_norm": gain(ks[10], (N_MLA_LAYERS, MLA_NOPE_DIM)),
        "mla_q_rope_norm": gain(ks[11], (N_MLA_LAYERS, MLA_ROPE_DIM)),
        "mla_k_nope_norm": gain(ks[12], (N_MLA_LAYERS, MLA_NOPE_DIM)),
        "mla_k_rope_norm": gain(ks[13], (N_MLA_LAYERS, MLA_ROPE_DIM)),
        "mla_w_o": nrm(ks[14], (N_MLA_LAYERS, MLA_HEADS * MLA_V_DIM, D_MODEL), (MLA_HEADS * MLA_V_DIM) ** -0.5),
        "moba_w_qkv": nrm(ks[15], (N_MOBA_LAYERS, D_MODEL, 3 * MOBA_HEADS * MOBA_HEAD_DIM), D_MODEL ** -0.5),
        "moba_q_norm": gain(ks[16], (N_MOBA_LAYERS, MOBA_HEAD_DIM)),
        "moba_k_norm": gain(ks[17], (N_MOBA_LAYERS, MOBA_HEAD_DIM)),
        "moba_w_o": nrm(ks[18], (N_MOBA_LAYERS, MOBA_HEADS * MOBA_HEAD_DIM, D_MODEL), (MOBA_HEADS * MOBA_HEAD_DIM) ** -0.5),
        "mlp_w_in": nrm(ks[19], (DEPTH, D_MODEL, D_FF), D_MODEL ** -0.5),
        "mlp_w_out": nrm(ks[20], (DEPTH, D_FF, D_MODEL), D_FF ** -0.5),
    }

def first_block(x, positions, rel_bias_table, attn_norm, mlp_norm, mla_w_in, mla_q_a_norm, mla_kv_a_norm,
              mla_w_uq, mla_w_ukv, mla_q_nope_norm, mla_q_rope_norm, mla_k_nope_norm, mla_k_rope_norm,
              mla_w_o, moba_w_qkv, moba_q_norm, moba_k_norm, moba_w_o, mlp_w_in, mlp_w_out):
    cos, sin = rope_tables(positions)
    for i in range(DEPTH):
        h = rms_norm(x, attn_norm[i])
        j = i // N_MIXERS
        if i % N_MIXERS == 0:
            x = x + mla_mixer(h, mla_w_in[j], mla_q_a_norm[j], mla_kv_a_norm[j], mla_w_uq[j], mla_w_ukv[j],
                              mla_q_nope_norm[j], mla_q_rope_norm[j], mla_k_nope_norm[j], mla_k_rope_norm[j],
                              mla_w_o[j], cos, sin)
        else:
            x = x + moba_mixer(h, moba_w_qkv[j], moba_q_norm[j], moba_k_norm[j], moba_w_o[j],
                               positions, rel_bias_table)
        h = rms_norm(x, mlp_norm[i])
        x = x + sq_relu_mlp(h, mlp_w_in[i], mlp_w_out[i])
    return x


N_A_LAYERS = DEPTH // 2
N_B_LAYERS = DEPTH - N_A_LAYERS

HEAD_DIM = 128
GDN_HEADS = D_MODEL // HEAD_DIM
GDN_DK = HEAD_DIM
GDN_DV = HEAD_DIM
GDN_WIDTH = GDN_HEADS * HEAD_DIM
CONV_K = 4
CHUNK = 64
FOX_HEADS = D_MODEL // HEAD_DIM
FOX_WIDTH = FOX_HEADS * HEAD_DIM
EPS = 1e-6


def rms_norm_2(x, g):
    xf = x.astype(jnp.float32)
    y = xf * lax.rsqrt(jnp.mean(xf * xf, axis=-1, keepdims=True) + EPS)
    return (y * g.astype(jnp.float32)).astype(x.dtype)

def l2_norm(x):
    xf = x.astype(jnp.float32)
    return (xf * lax.rsqrt(jnp.sum(xf * xf, axis=-1, keepdims=True) + EPS)).astype(x.dtype)

def causal_depthwise_conv(x, w):
    rhs = w[:, None, :].astype(x.dtype)
    return lax.conv_general_dilated(
        x, rhs, window_strides=(1,), padding=((CONV_K - 1, 0),),
        dimension_numbers=("NWC", "WIO", "NWC"), feature_group_count=x.shape[-1])

def chunk_gated_delta_rule(q, k, v, g, beta):
    B, L, H, Dk = q.shape
    Dv = v.shape[-1]
    N = L // CHUNK
    f32 = jnp.float32
    out_dtype = v.dtype

    def chunks(t):
        t = jnp.moveaxis(t.astype(f32), 2, 1)
        return t.reshape((B, H, N, CHUNK) + t.shape[3:])

    qc = chunks(q) * (Dk ** -0.5)
    kc, vc = chunks(k), chunks(v)
    gc, bc = chunks(g), chunks(beta)
    gcum = jnp.cumsum(gc, axis=-1)
    causal = jnp.tril(jnp.ones((CHUNK, CHUNK), dtype=bool))
    strict = jnp.tril(jnp.ones((CHUNK, CHUNK), dtype=bool), -1)
    diff = gcum[..., :, None] - gcum[..., None, :]
    decay = jnp.where(causal, jnp.exp(jnp.where(causal, diff, 0.0)), 0.0)

    kb = kc * bc[..., None]
    a_mat = jnp.where(strict, jnp.einsum('bhncd,bhnsd->bhncs', kb, kc) * decay, 0.0)
    rhs = jnp.concatenate([vc * bc[..., None], kb * jnp.exp(gcum)[..., None]], axis=-1)
    sol = lax.linalg.triangular_solve(a_mat, rhs, left_side=True, lower=True,
                                      unit_diagonal=True)
    u, w = sol[..., :Dv], sol[..., Dv:]
    attn = jnp.einsum('bhncd,bhnsd->bhncs', qc, kc) * decay

    def step(S, inp):
        q_i, k_i, u_i, w_i, g_i, attn_i = inp
        v_new = u_i - jnp.einsum('bhck,bhkv->bhcv', w_i, S)
        o = (jnp.einsum('bhck,bhkv->bhcv', q_i * jnp.exp(g_i)[..., None], S)
             + jnp.einsum('bhcs,bhsv->bhcv', attn_i, v_new))
        g_last = g_i[..., -1]
        k_dec = k_i * jnp.exp(g_last[..., None] - g_i)[..., None]
        S = S * jnp.exp(g_last)[..., None, None] + jnp.einsum('bhck,bhcv->bhkv', k_dec, v_new)
        return S, o

    xs = tuple(jnp.moveaxis(t, 2, 0) for t in (qc, kc, u, w, gcum, attn))
    S0 = jnp.zeros((B, H, Dk, Dv), f32)
    _, o = lax.scan(step, S0, xs)
    o = o.transpose(1, 0, 3, 2, 4).reshape(B, L, H, Dv)
    return o.astype(out_dtype)

def gdn_mixer(h, w_in, conv_w, a_log, dt_bias, o_norm, w_out):
    B, L, _ = h.shape
    W, H = GDN_WIDTH, GDN_HEADS
    proj = h @ w_in
    qkv, z, a, b = jnp.split(proj, [3 * W, 4 * W, 4 * W + H], axis=-1)
    qkv = jax.nn.silu(causal_depthwise_conv(qkv, conv_w))
    q, k, v = jnp.split(qkv, 3, axis=-1)
    q = l2_norm(q.reshape(B, L, H, GDN_DK))
    k = l2_norm(k.reshape(B, L, H, GDN_DK))
    v = v.reshape(B, L, H, GDN_DV)
    beta = jax.nn.sigmoid(b.astype(jnp.float32))
    g = -jnp.exp(a_log.astype(jnp.float32)) * jax.nn.softplus(a.astype(jnp.float32) + dt_bias.astype(jnp.float32))
    o = chunk_gated_delta_rule(q, k, v, g, beta)
    o = rms_norm_2(o, o_norm) * jax.nn.silu(z.reshape(B, L, H, GDN_DV))
    return o.reshape(B, L, W) @ w_out

def shared_kv(h, kv_norm, kv_w, kv_forget_bias, kv_k_norm):
    B, L, _ = h.shape
    u = rms_norm_2(h, kv_norm)
    k, v, f = jnp.split(u @ kv_w, [FOX_WIDTH, 2 * FOX_WIDTH], axis=-1)
    k = rms_norm_2(k.reshape(B, L, FOX_HEADS, HEAD_DIM), kv_k_norm)
    v = v.reshape(B, L, FOX_HEADS, HEAD_DIM)
    log_f = jax.nn.log_sigmoid(f.astype(jnp.float32) + kv_forget_bias.astype(jnp.float32))
    c = jnp.cumsum(log_f, axis=1)
    return k, v, c

def fox_attention(q, k, v, c):
    B, L, H, D = q.shape
    nb = L // Q_BLOCK
    qb = q.reshape(B, nb, Q_BLOCK, H, D).transpose(1, 0, 2, 3, 4)
    cT = jnp.transpose(c, (0, 2, 1))
    cb = cT.reshape(B, H, nb, Q_BLOCK).transpose(2, 0, 1, 3)
    kpos = jnp.arange(L)
    scale = D ** -0.5

    def block(args):
        i, q_i, c_i = args
        s = jnp.einsum('bqhd,bkhd->bhqk', q_i, k, preferred_element_type=jnp.float32) * scale
        s = s + (c_i[..., :, None] - cT[..., None, :])
        qpos = i * Q_BLOCK + jnp.arange(Q_BLOCK)
        s = jnp.where(kpos[None, :] <= qpos[:, None], s, -jnp.inf)
        p = jax.nn.softmax(s, axis=-1)
        return jnp.einsum('bhqk,bkhd->bqhd', p.astype(v.dtype), v)

    o = lax.map(block, (jnp.arange(nb), qb, cb))
    return o.transpose(1, 0, 2, 3, 4).reshape(B, L, H, D)

def fox_mixer(h, k, v, c, w_in, q_norm, w_out):
    B, L, _ = h.shape
    q, z = jnp.split(h @ w_in, [FOX_WIDTH], axis=-1)
    q = rms_norm_2(q.reshape(B, L, FOX_HEADS, HEAD_DIM), q_norm)
    o = fox_attention(q, k, v, c)
    o = o * jax.nn.silu(z.reshape(B, L, FOX_HEADS, HEAD_DIM))
    return o.reshape(B, L, FOX_WIDTH) @ w_out

def second_inputs(seed: int = 0) -> dict:
    key = jax.random.key(seed)
    ks = jax.random.split(key, 24)
    D, W, H = D_MODEL, GDN_WIDTH, GDN_HEADS
    nA, nB = N_A_LAYERS, N_B_LAYERS

    def nrm(k, shape, fan_in):
        return jax.random.normal(k, shape, jnp.float32) * (fan_in ** -0.5)

    def gain(k, shape):
        return 1.0 + 0.05 * jax.random.normal(k, shape, jnp.float32)

    dt = jnp.exp(jax.random.uniform(ks[5], (nA, H), jnp.float32, math.log(1e-3), math.log(1e-1)))
    return {
        "x": jax.random.normal(ks[0], (BATCH, SEQ, D), jnp.float32),
        "gdn_pre_norm": gain(ks[1], (nA, D)),
        "gdn_w_in": nrm(ks[2], (nA, D, 4 * W + 2 * H), D),
        "gdn_conv_w": nrm(ks[3], (nA, CONV_K, 3 * W), CONV_K),
        "gdn_a_log": jnp.log(jax.random.uniform(ks[4], (nA, H), jnp.float32, 1.0, 16.0)),
        "gdn_dt_bias": dt + jnp.log(-jnp.expm1(-dt)),
        "gdn_o_norm": gain(ks[6], (nA, GDN_DV)),
        "gdn_w_out": nrm(ks[7], (nA, W, D), W),
        "gdn_post_norm": gain(ks[8], (nA, D)),
        "kv_norm": gain(ks[9], (D,)),
        "kv_w": nrm(ks[10], (D, 2 * FOX_WIDTH + FOX_HEADS), D),
        "kv_forget_bias": 1.0 + 0.5 * jax.random.normal(ks[11], (FOX_HEADS,), jnp.float32),
        "kv_k_norm": gain(ks[12], (HEAD_DIM,)),
        "fox_pre_norm": gain(ks[13], (nB, D)),
        "fox_w_in": nrm(ks[14], (nB, D, 2 * FOX_WIDTH), D),
        "fox_q_norm": gain(ks[15], (nB, HEAD_DIM)),
        "fox_w_out": nrm(ks[16], (nB, FOX_WIDTH, D), FOX_WIDTH),
        "fox_post_norm": gain(ks[17], (nB, D)),
    }

def second_block(x, gdn_pre_norm, gdn_w_in, gdn_conv_w, gdn_a_log, gdn_dt_bias, gdn_o_norm,
              gdn_w_out, gdn_post_norm, kv_norm, kv_w, kv_forget_bias, kv_k_norm,
              fox_pre_norm, fox_w_in, fox_q_norm, fox_w_out, fox_post_norm):
    h = x
    k_sh = v_sh = c_sh = None
    for layer in range(DEPTH):
        if layer < N_A_LAYERS:
            i = layer
            y = gdn_mixer(rms_norm_2(h, gdn_pre_norm[i]), gdn_w_in[i], gdn_conv_w[i],
                          gdn_a_log[i], gdn_dt_bias[i], gdn_o_norm[i], gdn_w_out[i])
            h = h + rms_norm_2(y, gdn_post_norm[i])
        else:
            if layer == N_A_LAYERS:
                k_sh, v_sh, c_sh = shared_kv(h, kv_norm, kv_w, kv_forget_bias, kv_k_norm)
            i = layer - N_A_LAYERS
            y = fox_mixer(rms_norm_2(h, fox_pre_norm[i]), k_sh, v_sh, c_sh,
                          fox_w_in[i], fox_q_norm[i], fox_w_out[i])
            h = h + rms_norm_2(y, fox_post_norm[i])
    return h


def setup_inputs(seed=0):
    out = dict(first_inputs(seed))
    for name, value in second_inputs(seed + 1).items():
        if name != "x":
            out[name + "_2"] = value
    return out


def reference(
    x, positions, rel_bias_table, attn_norm, mlp_norm, mla_w_in, mla_q_a_norm, mla_kv_a_norm,
    mla_w_uq, mla_w_ukv, mla_q_nope_norm, mla_q_rope_norm, mla_k_nope_norm, mla_k_rope_norm,
    mla_w_o, moba_w_qkv, moba_q_norm, moba_k_norm, moba_w_o, mlp_w_in, mlp_w_out,
    gdn_pre_norm_2, gdn_w_in_2, gdn_conv_w_2, gdn_a_log_2, gdn_dt_bias_2, gdn_o_norm_2,
    gdn_w_out_2, gdn_post_norm_2, kv_norm_2, kv_w_2, kv_forget_bias_2, kv_k_norm_2,
    fox_pre_norm_2, fox_w_in_2, fox_q_norm_2, fox_w_out_2, fox_post_norm_2,
):
    x = first_block(
        x, positions, rel_bias_table, attn_norm, mlp_norm, mla_w_in, mla_q_a_norm,
        mla_kv_a_norm, mla_w_uq, mla_w_ukv, mla_q_nope_norm, mla_q_rope_norm, mla_k_nope_norm,
        mla_k_rope_norm, mla_w_o, moba_w_qkv, moba_q_norm, moba_k_norm, moba_w_o, mlp_w_in,
        mlp_w_out,
    )
    return second_block(
        x, gdn_pre_norm_2, gdn_w_in_2, gdn_conv_w_2, gdn_a_log_2, gdn_dt_bias_2, gdn_o_norm_2,
        gdn_w_out_2, gdn_post_norm_2, kv_norm_2, kv_w_2, kv_forget_bias_2, kv_k_norm_2,
        fox_pre_norm_2, fox_w_in_2, fox_q_norm_2, fox_w_out_2, fox_post_norm_2,
    )


_drawn_inputs = setup_inputs


def setup_inputs(seed=0):
    import zlib

    import numpy as np

    out = dict(_drawn_inputs(seed))
    spreads = {}
    factors = {'mla_q_a_norm': 3.972,
     'mla_q_nope_norm': 4.613,
     'mla_q_rope_norm': 7.641,
     'mla_k_nope_norm': 5.677,
     'mla_k_rope_norm': 7.695,
     'moba_q_norm': 8.0,
     'moba_k_norm': 8.0,
     'kv_k_norm_2': 6.261,
     'fox_q_norm_2': 8.0,
     'fox_post_norm_2': 2.824}
    for name, (base, spread) in spreads.items():
        noise = np.random.default_rng([zlib.crc32(name.encode()), seed]).standard_normal(out[name].shape)
        drawn = base * np.exp(spread * noise) if base else spread * noise
        out[name] = __import__('jax').numpy.asarray(drawn.astype(out[name].dtype))
    for name, factor in factors.items():
        out[name] = (out[name] * factor).astype(out[name].dtype)
    return out
```

```python
import numpy as np
import concourse.bass as bass
import concourse.mybir as mybir
from contextlib import ExitStack

F32 = mybir.dt.float32
F32R = mybir.dt.float32r
BF16 = mybir.dt.bfloat16
I32 = mybir.dt.int32
ALU = mybir.AluOpType
ACT = mybir.ActivationFunctionType
AX = mybir.AxisListType.X

T = 256
D = 1024
NEG = -1.0e30
EPS = 1e-6
RAW = 3
SPLIT = 3
CH = 2048

COLS = {}
_at = 0
for _n, _w in (("attn0", 8), ("attn1", 8), ("mlp0", 8), ("mlp1", 8), ("gdnpre", 8), ("kvn", 8), ("foxpre", 8),
               ("qa", 3), ("kva", 2), ("mlaqn", 1), ("mlakn", 1), ("mobaq", 1), ("mobak", 1), ("foxk", 1), ("foxq", 1),
               ("gdno", 1), ("conv", 96)):
    COLS[_n] = (_at, _w)
    _at += _w
NCOLS = _at
ROWS = {"ropeq": (0, 64), "ropek": (64, 64), "alog": (128, 8), "dt": (136, 8), "fbias": (144, 8), "invf": (152, 32)}
NROWS = 184
CST = {"ident": (0, 128), "mask": (128, 384), "tri": (512, 128), "ones": (640, 128), "tb": (768, 1),
       "negid": (769, 128)}
NCST = 897


def bc(ap, dim, n):
    shape = list(ap.shape)
    shape[dim] = n
    return ap.broadcast_to(shape)


def bass_two_blocks(nc, A, out, stop=99):
    ctx = ExitStack()
    with ctx:
        def sb(name, shape, dt=F32):
            return ctx.enter_context(nc.sbuf_tensor(name, shape, dt))

        def sem(name):
            return ctx.enter_context(nc.semaphore(name))

        queue = {e: [] for e in ("pe", "act", "dve", "pool", "sp")}
        done = {e: sem("s_" + e) for e in ("pe", "act", "dve", "pool")}
        count = {e: 0 for e in done}
        waited = {}

        def wait(eng, tokens):
            for t in tokens:
                if t is None:
                    continue
                if not (len(t) == 2 and isinstance(t[1], int)):
                    wait(eng, t)
                    continue
                s, v = t
                if waited.get((eng, id(s)), 0) < v:
                    waited[(eng, id(s))] = v
                    queue[eng].append(("wait", s, v))

        def op(eng, fn, *tokens, sig=True):
            wait(eng, tokens)
            if sig:
                count[eng] += 1
                queue[eng].append(("run", fn, done[eng], 1))
                return (done[eng], count[eng])
            queue[eng].append(("run", fn, None, 0))
            return None

        def dma(fn, s, *tokens):
            wait("sp", tokens)
            queue["sp"].append(("run", fn, s, 16))

        def act(o, i, func, *tokens, bias=0.0, scale=1.0, accum=None):
            return op("act", lambda e: e.activation(o, i, func, bias=bias, scale=scale, accum_out=accum)
                      if accum is not None else e.activation(o, i, func, bias=bias, scale=scale), *tokens)

        def tt(o, a, b, f, *tokens, eng="dve"):
            return op(eng, lambda e: e.tensor_tensor(o, a, b, f), *tokens)

        def ts(o, a, s1, s2, f1, f2, *tokens, eng="dve"):
            return op(eng, lambda e: e.tensor_scalar(o, a, s1, s2, f1, f2) if f2 is not None
                      else e.tensor_scalar(o, a, s1, None, f1), *tokens)

        def stt(o, a, s, b, f1, f2, *tokens):
            return op("dve", lambda e: e.scalar_tensor_tensor(out=o, in0=a, scalar=s, in1=b, op0=f1, op1=f2), *tokens)

        def copy(o, a, *tokens, eng="dve"):
            return op(eng, lambda e: e.tensor_copy(o, a), *tokens)

        def mm(o, l, r, start, *tokens, sig=False):
            return op("pe", lambda e: e.matmul(o, l, r, start=start, stop=True, skip_group_check=True), *tokens, sig=sig)

        def mm3(o, lh, ll, rh, rl, start, *tokens, sig=False):
            mm(o, lh, rh, start, *tokens)
            mm(o, lh, rl, False)
            return mm(o, ll, rh, False, sig=sig)

        cst = sb("cst", [128, NCST])
        cols = sb("cols", [128, NCOLS])
        rows = sb("rows", [128, NROWS])
        predi = sb("predi", [128, 2, 7, 128], mybir.dt.uint8)
        X = sb("X", [128, 2, D])
        xh = sb("xh", [128, 8, T], F32R)
        xl = sb("xl", [128, 8, T], F32R)
        raw = [sb(f"raw{i}", [128, CH]) for i in range(RAW)]
        whi = [sb(f"whi{i}", [128, CH], F32R) for i in range(SPLIT)]
        wlo = [sb(f"wlo{i}", [128, CH], F32R) for i in range(SPLIT)]
        oth = sb("oth", [128, 2048], F32R)
        otl = sb("otl", [128, 2048], F32R)
        st = sb("st", [128, 1024])
        pint = sb("pint", [128, 384])
        AR = 18400
        arena = sb("arena", [128, AR])

        P = [ctx.enter_context(nc.psum_tensor(f"ps{i}", [128, 512], F32)) for i in range(8)]
        pfree = [[] for _ in range(8)]
        ring = [4]

        def bank():
            b = ring[0]
            ring[0] = 4 + (b - 3) % 4
            return b

        def C(name, j=None):
            a, w = COLS[name]
            return cols[:, a:a + w] if j is None else cols[:, a + j:a + j + 1]

        def K(name):
            a, w = CST[name]
            return cst[:, a:a + w]

        def RW(name):
            a, w = ROWS[name]
            return rows[:, a:a + w]

        ident = K("ident")

        s_in = sem("s_in")
        s_x = sem("s_x")
        s_out = sem("s_out")
        n_in = [0]

        def small(o, i):
            dma(lambda e: e.dma_start(o, i), s_in)
            n_in[0] += 16

        dma(lambda e: e.dma_start(X[:, :, :], A["x"].rearrange("(t p) d -> p t d", p=128)), s_x)
        small(cst[:, :], A["c_cst"])
        small(cols[:, :], A["c_cols"])
        small(rows[:, :], bc(A["c_rows"].rearrange("(a d) -> a d", a=1), 0, 128))
        predf = arena[:, 14464:14464 + 1792]
        small(predf, A["c_pred"])
        posT = st[:, 0:2].bitcast(I32)
        small(posT, A["c_posT"])
        pqi = pint[:, 0:256].bitcast(I32)
        small(pqi, bc(A["positions"], 0, 128))
        pki = pint[:, 256:320].bitcast(I32)
        for kk in range(4):
            small(pki[32 * kk:32 * kk + 32, :], bc(A["positions"][:, 64 * kk:64 * kk + 64], 0, 32))
        tab = pint[:, 320:352]
        tabs = pint[:, 352:384]
        z0 = op("dve", lambda e: e.memset(pint[:, 320:384], 0.0))
        wait("sp", [z0])
        for kk in range(4):
            small(tab[32 * kk:32 * kk + 32, 8 * kk:8 * kk + 8], A["rel_bias_table"])
            small(tabs[32 * kk + 1:32 * kk + 32, 8 * kk:8 * kk + 8], A["rel_bias_table"][0:31, :])
        IN = (s_in, n_in[0])
        INX = (s_x, 16)
        t_pred = copy(predi[:, :, :, :].rearrange("p a l n -> p (a l n)"), predf, IN)

        specs = []

        def add(src, a, b):
            specs.append((src, a, b))
            return len(specs) - 1

        def kslab(w, k0, nk, c0, nc_):
            return add(w[128 * k0:128 * (k0 + nk), c0:c0 + nc_].rearrange("(k p) n -> p k n", p=128), nk, nc_)

        for k in range(0, 8, 2):
            kslab(A["mla_w_in"], k, 2, 0, 704)
        for g in range(2):
            kslab(A["mla_w_ukv"], 0, 2, 1024 * g, 1024)
            for i in range(2):
                kslab(A["mla_w_uq"], 0, 3, 768 * g + 384 * i, 384)
        for k in range(0, 8, 2):
            kslab(A["mla_w_o"], k, 2, 0, 1024)

        def mlp_specs(i):
            for g in range(9):
                if g < 8:
                    for hk in range(2):
                        kslab(A["mlp_w_in"][i], 4 * hk, 4, 512 * g, 512)
                if g > 0:
                    for k in range(4 * (g - 1), 4 * g, 2):
                        kslab(A["mlp_w_out"][i], k, 2, 0, 1024)

        mlp_specs(0)
        for g in range(2):
            for part in range(3):
                for hk in range(2):
                    kslab(A["moba_w_qkv"], 4 * hk, 4, 1024 * part + 512 * g, 512)
        for k in range(0, 8, 2):
            kslab(A["moba_w_o"], k, 2, 0, 1024)
        mlp_specs(1)
        kslab(A["gdn_w_in"], 0, 8, 4096, 16)
        for c0 in (1024, 0, 1536, 512, 2048, 2560, 3072, 3584):
            for hk in range(2):
                kslab(A["gdn_w_in"], 4 * hk, 4, c0, 512)
        for k in range(0, 8, 2):
            kslab(A["gdn_w_out"], k, 2, 0, 1024)
        kslab(A["kv_w"], 0, 8, 2048, 8)
        for w, c0 in (("kv_w", 0), ("kv_w", 1024), ("fox_w_in", 0), ("kv_w", 512), ("kv_w", 1536), ("fox_w_in", 512),
                      ("fox_w_in", 1024), ("fox_w_in", 1536)):
            for hk in range(2):
                kslab(A[w], 4 * hk, 4, c0, 512)
        for k in range(0, 8, 2):
            kslab(A["fox_w_out"], k, 2, 0, 1024)

        s_raw = [sem(f"s_raw{i}") for i in range(RAW)]
        loaded = [0]
        nsplit = [0]
        split_at = {}
        released = {}

        def load():
            c = loaded[0]
            if c >= len(specs):
                return
            loaded[0] += 1
            src, a, b = specs[c]
            dst = raw[c % RAW][:, 0:a * b].rearrange("p (k n) -> p k n", k=a)
            dma(lambda e: e.dma_start(dst, src), s_raw[c % RAW], *(split_at[c - RAW] if c >= RAW else ()))

        def split():
            c = nsplit[0]
            if c >= len(specs):
                return
            nsplit[0] += 1
            if loaded[0] <= c:
                load()
            _, a, b = specs[c]
            n = a * b
            r, h, l = raw[c % RAW][:, 0:n], whi[c % SPLIT][:, 0:n], wlo[c % SPLIT][:, 0:n]
            free = released.get(c - SPLIT)
            t1 = op("act", lambda e: e.activation(h, r, ACT.Copy), (s_raw[c % RAW], 16 * (c // RAW + 1)), free)
            t2 = tt(l, r, h, ALU.subtract, t1, free)
            split_at[c] = (t1, t2)
            load()

        for _ in range(RAW):
            load()
        cur = [-1]

        def use():
            cur[0] += 1
            c = cur[0]
            while nsplit[0] < min(c + SPLIT, len(specs)) and (nsplit[0] - SPLIT < 0 or (nsplit[0] - SPLIT) in released):
                split()
            _, a, b = specs[c]
            v = [w[c % SPLIT][:, 0:a * b].rearrange("p (k n) -> p k n", k=a) for w in (whi, wlo)]
            return c, v[0], v[1], split_at[c]

        def release(c, tok):
            released[c] = tok

        sti = [2]

        def small_tile(n):
            if sti[0] + n > 1024:
                sti[0] = 2
            a = sti[0]
            sti[0] += n
            return st[:, a:a + n]

        def rsqrt(ss, n, scale, *tokens, eps=EPS):
            m, l, r, u, v, w = (small_tile(n) for _ in range(6))
            t = ts(m, ss, scale, eps, ALU.mult, ALU.add, *tokens)
            t = act(l, m, ACT.Ln, t)
            t = act(r, l, ACT.Exp, t, scale=-0.5)
            t = stt(u, r, -0.5, m, ALU.mult, ALU.mult, t)
            t = tt(v, u, r, ALU.mult, t)
            t = stt(w, v, 1.5, r, ALU.add, ALU.mult, t)
            return w, t

        def transposed(src, gain, h, l, *tokens, free=()):
            toks = []
            for j2 in range(4):
                b = bank()
                for j in (2 * j2, 2 * j2 + 1):
                    for t in range(2):
                        o = P[b][:, 256 * (j % 2) + 128 * t:256 * (j % 2) + 128 * t + 128]
                        i = src[:, t, 128 * j:128 * j + 128]
                        tk = op("pe", lambda e, o=o, i=i: e.transpose(o, i, ident), IN, *tokens, pfree[b],
                                sig=(j % 2 == 1 and t == 1))
                for j in (2 * j2, 2 * j2 + 1):
                    ta = act(h[:, j, :], P[b][:, 256 * (j % 2):256 * (j % 2) + 256], ACT.Copy, tk, IN, *free,
                             scale=C(gain, j))
                for j in (2 * j2, 2 * j2 + 1):
                    tv = stt(l[:, j, :], P[b][:, 256 * (j % 2):256 * (j % 2) + 256], C(gain, j), h[:, j, :],
                             ALU.mult, ALU.subtract, ta, IN, *free)
                pfree[b] = [ta, tv]
                toks.append(tv)
            return toks[-1]

        def mean_squares(src, junk, *tokens):
            ss = small_tile(2)
            for t in range(2):
                tk = act(junk, src[:, t, :], ACT.Square, *tokens, accum=ss[:, t:t + 1])
                tokens = (tk,)
            return ss, tk

        def proj_x(pair, groups, th, tl, k0, w, first, last, *tokens):
            c, wh, wl, tk = use()
            nk = specs[c][1]
            n = specs[c][2]
            for t in range(2):
                b = pair + t
                for k in range(nk):
                    s = slice(128 * t, 128 * t + 128)
                    tok = mm3(P[b][:, 0:n], th[:, k0 + k, s], tl[:, k0 + k, s], wh[:, k, :], wl[:, k, :],
                              first and k == 0, tk, tokens, pfree[b], sig=(k == nk - 1))
            release(c, tok)
            return tok

        def proj_w(pair, th, tl, k0, first, *tokens):
            c, wh, wl, tk = use()
            for m in range(4):
                b = pair + m // 2
                o = P[b][:, 256 * (m % 2):256 * (m % 2) + 256]
                for k in range(4):
                    s = slice(128 * m, 128 * m + 128)
                    fst = first and k == 0 and m % 2 == 0
                    mm(o, wh[:, k, s], th[:, k0 + k, :], fst, tk, tokens, pfree[b])
                    mm(o, wh[:, k, s], tl[:, k0 + k, :], False)
                    tok = mm(o, wl[:, k, s], th[:, k0 + k, :], False, sig=(k == 3 and m % 2 == 1))
            release(c, tok)
            return tok

        def back(k0, hh, hl, first, last, *tokens):
            c, wh, wl, tk = use()
            toks = []
            for t in range(2):
                for ch in range(2):
                    b = 2 * t + ch
                    for k in range(2):
                        tok = mm3(P[b][:, :], hh(k0 + k, t), hl(k0 + k, t), wh[:, k, 512 * ch:512 * ch + 512],
                                  wl[:, k, 512 * ch:512 * ch + 512], first and k == 0, tk, tokens, pfree[b],
                                  sig=(k == 1))
                    toks.append(tok)
            release(c, tok)
            return toks

        def residual(toks, scale=None):
            out_ = []
            for t in range(2):
                for ch in range(2):
                    b = 2 * t + ch
                    xs = X[:, t, 512 * ch:512 * ch + 512]
                    if scale is None:
                        tk = tt(xs, P[b][:, :], xs, ALU.add, toks[b])
                    else:
                        tk = stt(xs, P[b][:, :], scale[0][:, t:t + 1], xs, ALU.mult, ALU.add, toks[b], scale[1])
                    pfree[b] = [tk]
                    out_.append(tk)
            return out_[-1]

        def interleave(a, b, ratio=1):
            a, b = iter(a), iter(b)
            live = True
            for _ in b:
                for _ in range(ratio):
                    next(a, None)
            for _ in a:
                pass

        def fence():
            return [(done[e], count[e]) for e in done]

        def attention(heads, qT, kT, V, scale, bias, bufs, emit, extra=None, after=(), ready=lambda h: ()):
            Sx, Pn, PT, sm = bufs
            used = attention.used

            def score(h):
                b = bank()
                i = h % 2
                for t, (c0, n) in enumerate(((0, 128), (128, 256))):
                    s = slice(128 * t, 128 * t + 128)
                    o = P[b][:, c0:c0 + n]
                    tk = mm(o, qT(h)[:, s], kT(h)[:, 0:n], True, pfree[b], ready(h), sig=(extra is None and t == 1))
                    if extra is not None:
                        q2, k2 = extra(h)
                        tk = mm(o, q2[:, s], k2[:, 0:n], False, sig=(t == 1))
                bt = bias(h)
                if isinstance(scale, float):
                    tk = stt(Sx[i], P[b][:, 0:384], scale, bt[0], ALU.mult, ALU.add, tk, bt[1], used.get(("S", i)), after)
                else:
                    sc, sct = scale(h)
                    stt(Sx[i][:, 0:128], P[b][:, 0:128], sc[0], bt[0][:, 0:128], ALU.mult, ALU.add, tk, bt[1], sct,
                        used.get(("S", i)), after)
                    tk = stt(Sx[i][:, 128:384], P[b][:, 128:384], sc[1], bt[0][:, 128:384], ALU.mult, ALU.add)
                if len(bt) > 2:
                    bt[2](tk)
                pfree[b] = [tk]
                mx = small_tile(2)
                ng = small_tile(2)
                op("dve", lambda e: e.reduce_max(mx[:, 0:1], Sx[i][:, 0:128], AX), tk)
                tk = op("dve", lambda e: e.reduce_max(mx[:, 1:2], Sx[i][:, 128:384], AX))
                tk = ts(ng, mx, -1.0, None, ALU.mult, None, tk)
                su = small_tile(2)
                act(Pn[i][:, 0:128], Sx[i][:, 0:128], ACT.Exp, tk, used.get(("P", i)), after, bias=ng[:, 0:1],
                    accum=su[:, 0:1])
                tk = act(Pn[i][:, 128:384], Sx[i][:, 128:384], ACT.Exp, bias=ng[:, 1:2], accum=su[:, 1:2])
                used[("S", i)] = tk
                rc = small_tile(2)
                tk = op("dve", lambda e: e.reciprocal(rc, su), tk)
                ts(Pn[i][:, 0:128], Pn[i][:, 0:128], rc[:, 0:1], None, ALU.mult, None, tk)
                return ts(Pn[i][:, 128:384], Pn[i][:, 128:384], rc[:, 1:2], None, ALU.mult, None)

            def turn(h, tk):
                b = bank()
                i = h % 2
                for j in range(3):
                    o, a = P[b][:, 128 * j:128 * j + 128], Pn[i][:, 128 * j:128 * j + 128]
                    tk = op("pe", lambda e, o=o, a=a: e.transpose(o, a, ident), tk, pfree[b], sig=(j == 2))
                used[("P", i)] = tk
                tk = copy(PT[i], P[b][:, 0:384], tk, used.get(("T", i)), after)
                pfree[b] = [tk]
                return tk

            def value(h, tk):
                b = bank()
                i = h % 2
                mm(P[b][:, 0:256], V(h, 0), PT[i][:, 0:256], True, tk, pfree[b])
                tk = mm(P[b][:, 128:256], V(h, 1), PT[i][:, 256:384], False, sig=True)
                used[("T", i)] = tk
                pfree[b] = emit(h, b, tk)

            prob = {}
            n = len(heads)
            prob[0] = score(heads[0])
            yield
            for j in range(n):
                if j + 1 < n:
                    prob[j + 1] = score(heads[j + 1])
                    yield
                tk = turn(heads[j], prob.pop(j))
                yield
                value(heads[j], tk)
                yield

        attention.used = {}

        def abufs(a):
            return ([arena[:, a + 384 * i:a + 384 * i + 384] for i in range(2)],
                    [arena[:, a + 768 + 384 * i:a + 768 + 384 * i + 384] for i in range(2)],
                    [arena[:, a + 1536 + 384 * i:a + 1536 + 384 * i + 384] for i in range(2)], None)

        def o_split(h, b, tk, *tokens):
            a = act(oth[:, 256 * h:256 * h + 256], P[b][:, 0:256], ACT.Copy, tk, *tokens)
            v = tt(otl[:, 256 * h:256 * h + 256], P[b][:, 0:256], oth[:, 256 * h:256 * h + 256], ALU.subtract, a, *tokens)
            return [a, v]

        def oh(k, t):
            return oth[:, 256 * k + 128 * t:256 * k + 128 * t + 128]

        def ol(k, t):
            return otl[:, 256 * k + 128 * t:256 * k + 128 * t + 128]

        def view(a, n, s=None, **kw):
            v = arena[:, a:a + n]
            return v.rearrange(s, **kw) if s else v

        A_PROJ, A_KV, A_Q, A_KT, A_QT, A_QPT, A_KPT, A_SQ, A_AT, A_TR = (0, 1408, 5504, 8576, 10624, 12672, 13696,
                                                                        13952, 14464, 16768)
        projS = view(A_PROJ, 1408, "p (t n) -> p t n", t=2)
        kvtok = view(A_KV, 4096, "p (t h n) -> p t h n", t=2, h=8)
        qtok = view(A_Q, 3072, "p (t h n) -> p t h n", t=2, h=8)
        kT = view(A_KT, 2048, "p (h n) -> p h n", h=8)
        qT = view(A_QT, 2048, "p (h n) -> p h n", h=8)
        qpT = view(A_QPT, 1024, "p (h n) -> p h n", h=4)
        kpT = view(A_KPT, 256)
        sq = view(A_SQ, 512)
        rt = view(A_TR, 900)

        posf = small_tile(2)
        tp = copy(posf, posT, IN)
        ang, nn, rr, hf, sn, cs, s2 = (rt[:, 64 * i:64 * i + 64].rearrange("p (t n) -> p t n", t=2) for i in range(7))
        for t in range(2):
            tk = ts(ang[:, t, :], RW("invf"), posf[:, t:t + 1], None, ALU.mult, None, tp)
        MAGIC = 12582912.0
        C1 = 6.28125
        C2 = float(np.float32(2 * np.pi - C1))
        C3 = float(2 * np.pi - C1 - C2)
        tk = ts(nn, ang, float(1 / (2 * np.pi)), MAGIC, ALU.mult, ALU.add, tk)
        tk = ts(nn, nn, MAGIC, None, ALU.subtract, None, tk)
        tk = stt(rr, nn, -C1, ang, ALU.mult, ALU.add, tk)
        tk = stt(rr, nn, -C2, rr, ALU.mult, ALU.add, tk)
        tk = stt(rr, nn, -C3, rr, ALU.mult, ALU.add, tk)
        tk = ts(rr, rr, 3.1415925, -3.1415925, ALU.min, ALU.max, tk)
        tk = act(sn, rr, ACT.Sin, tk)
        tk2 = act(s2, rr, ACT.Sin, scale=0.5)
        tk = tt(s2, s2, s2, ALU.mult, tk2)
        tk = ts(cs, s2, -2.0, 1.0, ALU.mult, ALU.add, tk)
        rope_t = {}
        for n_, nm in enumerate(("ropeq", "ropek")):
            for j, (src, half) in enumerate(((cs, 0), (sn, 1), (cs, 1), (sn, 0))):
                d = rt[:, 448 + 256 * n_ + 64 * j - 448 * 0:448 + 256 * n_ + 64 * j + 64] if False else None
                a0 = 16768 + 448 + 64 * (4 * n_ + j)
                d = arena[:, a0:a0 + 64].rearrange("p (t n) -> p t n", t=2)
                g = bc(RW(nm)[:, 32 * half:32 * half + 32].unsqueeze(1), 1, 2)
                tk = tt(d, src, g, ALU.mult, tk)
                rope_t[nm, j] = d
        t_rope = tk

        def rope(nm, src, dst, t, nh, tmp, *tokens):
            x1, x2 = src[:, :, 0:32], src[:, :, 32:64]
            f = [bc(rope_t[nm, j][:, t, :].unsqueeze(1), 1, nh) for j in range(4)]
            ta = tmp.rearrange("p (a h n) -> p a h n", a=4, h=nh)
            tt(ta[:, 0], x1, f[0], ALU.mult, t_rope, *tokens)
            tt(ta[:, 1], x2, f[1], ALU.mult)
            tt(ta[:, 2], x2, f[2], ALU.mult)
            tk = tt(ta[:, 3], x1, f[3], ALU.mult)
            tt(dst[:, :, 0:32], ta[:, 0], ta[:, 1], ALU.subtract, tk)
            return tt(dst[:, :, 32:64], ta[:, 2], ta[:, 3], ALU.add)

        xT = transposed(X, "attn0", xh, xl, INX)
        ss, tk = mean_squares(X, view(A_QT, 1024), INX)
        r0, tr0 = rsqrt(ss, 2, 1.0 / D, tk)
        for c_ in range(4):
            c, wh, wl, tk = use()
            for t in range(2):
                s = slice(128 * t, 128 * t + 128)
                for ch, (a, n) in enumerate(((0, 512), (512, 192))):
                    for k in range(2):
                        tok = mm3(P[2 * t + ch][:, 0:n], xh[:, 2 * c_ + k, s], xl[:, 2 * c_ + k, s],
                                  wh[:, k, a:a + n], wl[:, k, a:a + n], c_ == 0 and k == 0, tk, xT,
                                  sig=(k == 1 and ch == 1))
            release(c, tok)
        t_in = tok
        for t in range(2):
            for ch, (a, n) in enumerate(((0, 512), (512, 192))):
                tk = act(projS[:, t, a:a + n], P[2 * t + ch][:, 0:n], ACT.Copy, t_in, tr0, scale=r0[:, t:t + 1])
                pfree[2 * t + ch] = [tk]
        ssm = small_tile(6)
        for t in range(2):
            for i, (a, n) in enumerate(((0, 384), (384, 256), (640, 64))):
                tk = act(sq[:, 0:n], projS[:, t, a:a + n], ACT.Square, tk, accum=ssm[:, 2 * i + t:2 * i + t + 1])
        ssn = small_tile(6)
        for i, n in enumerate((384, 256, 64)):
            t2 = ts(ssn[:, 2 * i:2 * i + 2], ssm[:, 2 * i:2 * i + 2], 1.0 / n, None, ALU.mult, None, tk)
        rm, trm = rsqrt(ssn, 6, 1.0, t2)
        for j in range(5):
            b = bank()
            for t in range(2):
                o, i = P[b][:, 128 * t:128 * t + 128], projS[:, t, 128 * j:128 * j + 128]
                tk = op("pe", lambda e, o=o, i=i: e.transpose(o, i, ident), tk, pfree[b], sig=(t == 1))
            g = C("qa", j) if j < 3 else C("kva", j - 3)
            ta = act(xh[:, j, :], P[b][:, 0:256], ACT.Copy, tk, t_in, scale=g)
            tv = stt(xl[:, j, :], P[b][:, 0:256], g, xh[:, j, :], ALU.mult, ALU.subtract, ta, t_in)
            pfree[b] = [ta, tv]
            tk = ta
        cT = tv
        kp = view(A_QPT, 256, "p (t n) -> p t n", t=2)
        kn = view(A_QPT + 256, 128, "p (t n) -> p t n", t=2)
        for t in range(2):
            ts(kn[:, t, :], projS[:, t, 640:704], rm[:, 4 + t:5 + t], None, ALU.mult, None, trm)
        tk = (done["dve"], count["dve"])
        for t in range(2):
            tk = rope("ropek", kn[:, t:t + 1, :], kp[:, t:t + 1, 0:64], t, 1, sq[:, 128 * t:128 * t + 128], tk,
                      (done["act"], count["act"]))
        tk = copy(kp[:, :, 64:128], kp[:, :, 0:64], tk)
        b = bank()
        for t in range(2):
            o, i = P[b][:, 128 * t:128 * t + 128], kp[:, t, :]
            tk = op("pe", lambda e, o=o, i=i: e.transpose(o, i, ident), tk, pfree[b], sig=(t == 1))
        t_kp = copy(kpT, P[b][:, 0:256], tk)
        pfree[b] = [t_kp]
        gk = small_tile(1)
        t_gk = tt(gk, C("mlaqn"), C("mlakn"), ALU.mult, IN)

        sqf = [(None)]

        def head_rstd(src, nh, n, tok, sqb=None):
            s_ = (sqb if sqb is not None else sq)[:, 0:nh * n].rearrange("p (h n) -> p h n", h=nh)
            ta = act(s_, src, ACT.Square, tok, sqf[0])
            o = small_tile(nh)
            tv = op("dve", lambda e: e.reduce_sum(o, s_, AX), ta)
            sqf[0] = tv
            return rsqrt(o, nh, 1.0 / n, tv)

        def heads_T(dst, src, h0, gain, tok, *tokens):
            b = bank()
            for j in range(2):
                for t in range(2):
                    o, i = P[b][:, 256 * j + 128 * t:256 * j + 128 * t + 128], src(t, h0 + j)
                    tk = op("pe", lambda e, o=o, i=i: e.transpose(o, i, ident), tok, pfree[b],
                            sig=(j == 1 and t == 1))
            d = dst[:, h0:h0 + 2, :]
            i = P[b][:, :].rearrange("p (h n) -> p h n", h=2)
            if gain is None:
                tk = act(d, i, ACT.Copy, tk, *tokens)
            else:
                tk = act(d, i, ACT.Copy, tk, *tokens, scale=gain)
            pfree[b] = [tk]
            return tk

        ready = {}

        def mla_up(g):
            c, wh, wl, tk = use()
            for ch in range(2):
                for t in range(2):
                    b = 2 * ch + t
                    for k in range(2):
                        s = slice(128 * t, 128 * t + 128)
                        tok = mm3(P[b][:, :], xh[:, 3 + k, s], xl[:, 3 + k, s], wh[:, k, 512 * ch:512 * ch + 512],
                                  wl[:, k, 512 * ch:512 * ch + 512], k == 0, tk, cT, pfree[b], sig=(k == 1))
                    h0 = 4 * g + 2 * ch
                    ta = act(kvtok[:, t, h0:h0 + 2, :], P[b][:, :].rearrange("p (h n) -> p h n", h=2), ACT.Copy, tok, trm,
                             scale=rm[:, 2 + t:3 + t])
                    pfree[b] = [ta]
                    yield
            release(c, tok)
            for t in range(2):
                ks = kvtok[:, t, 4 * g:4 * g + 4, 0:128]
                r_, tr = head_rstd(ks, 4, 128, (done["act"], count["act"]))
                tkk = tt(ks, ks, bc(r_.unsqueeze(2), 2, 128), ALU.mult, tr)
            tkk2 = {}
            for h0 in (4 * g, 4 * g + 2):
                tkk2[h0] = heads_T(kT, lambda t, h: kvtok[:, t, h, 0:128], h0, gk, tkk, t_gk)
                yield
            for i in range(2):
                h0 = 4 * g + 2 * i
                c, wh, wl, tk = use()
                for t in range(2):
                    b = t + 2 * i
                    s = slice(128 * t, 128 * t + 128)
                    for k in range(3):
                        tok = mm3(P[b][:, 0:384], xh[:, k, s], xl[:, k, s], wh[:, k, :], wl[:, k, :], k == 0, tk, cT,
                                  pfree[b], sig=(k == 2))
                    ta = act(qtok[:, t, h0:h0 + 2, :], P[b][:, 0:384].rearrange("p (h n) -> p h n", h=2), ACT.Copy,
                             tok, trm, scale=rm[:, t:t + 1])
                    pfree[b] = [ta]
                    yield
                release(c, tok)
                for t in range(2):
                    qn, qp = qtok[:, t, h0:h0 + 2, 0:128], qtok[:, t, h0:h0 + 2, 128:192]
                    r_, tr = head_rstd(qn, 2, 128, ta)
                    tq = tt(qn, qn, bc(r_.unsqueeze(2), 2, 128), ALU.mult, tr)
                    r_, tr = head_rstd(qp, 2, 64, ta)
                    tp_ = tt(qp, qp, bc(r_.unsqueeze(2), 2, 64), ALU.mult, tr)
                    tmp = view(A_TR + 448 + 512, 256)
                    tp_ = rope("ropeq", qp, qp, t, 2, tmp, tp_)
                tkq = heads_T(qT, lambda t, h: qtok[:, t, h, 0:128], h0, None, tq)
                b = bank()
                for t in range(2):
                    o = P[b][:, 128 * t:128 * t + 128]
                    pr = view(A_TR + 448 + 768 + 0, 128)
                    tp_ = copy(pr.rearrange("p (h n) -> p h n", h=2), qtok[:, t, h0:h0 + 2, 128:192], tp_, t_gk)
                    tp_ = op("pe", lambda e, o=o, i=pr: e.transpose(o, i, ident), tp_, pfree[b])
                tkp = act(qpT[:, h0 // 2, :], P[b][:, 0:256], ACT.Copy, tp_, t_kp)
                pfree[b] = [tkp]
                ready[h0] = ready[h0 + 1] = [tkk2[h0], tkq, tkp, t_kp]
                yield

        def mla_extra(h):
            s = slice(64 * (h % 2), 64 * (h % 2) + 64)
            return qpT[s, h // 2, :], kpT[s, :]

        mscale = float(1.0 / np.sqrt(192.0))
        ot_t = {}

        def keep_o(h, b, tk):
            ot_t[h] = o_split(h, b, tk)
            return ot_t[h]

        def mla_attn(heads):
            return attention(heads, lambda h: qT[:, h, :], lambda h: kT[:, h, :], lambda h, t: kvtok[:, t, h, 128:256],
                             mscale, lambda h: (K("mask"), IN), abufs(A_AT), keep_o, extra=mla_extra, after=(t_pred,),
                             ready=lambda h: ready[h])

        final = {}

        def o_product(first_pair, pairs, hh=oh, hl=ol):
            for p_ in pairs:
                while 2 * p_ + 1 not in ot_t:
                    yield
                final["t"] = back(2 * p_, hh, hl, p_ == first_pair, False, ot_t[2 * p_], ot_t[2 * p_ + 1])
                yield

        def o_phase(attn_gen):
            gen = o_product(0, range(4))
            for _ in attn_gen:
                next(gen, None)
            for _ in gen:
                pass

        for _ in mla_up(0):
            pass
        interleave(mla_attn(range(0, 4)), mla_up(1), 1)
        o_phase(mla_attn(range(4, 8)))
        tX = residual(final["t"])

        def finish(tok):
            dma(lambda e: e.dma_start(out.rearrange("(t p) d -> p t d", p=128), X[:, :, :]), s_out, tok)
            wait("sp", [(s_out, 16)])

        def mlp(i, tok, extra=()):
            F = fence()
            ot_t.clear()
            xt = transposed(X, f"mlp{i}", xh, xl, tok, free=F)
            ss, tk = mean_squares(X, view(4096, 1024), tok, F)
            m = small_tile(2)
            r2 = small_tile(2)
            tk = ts(m, ss, 1.0 / D, EPS, ALU.mult, ALU.add, tk)
            tr2 = op("dve", lambda e: e.reciprocal(r2, m), tk)
            rel = [view(2048 * i_, 1024) for i_ in range(2)]
            sqr = [view(2048 * i_ + 1024, 1024) for i_ in range(2)]
            ex = iter(extra)
            for g in range(9):
                if g < 8:
                    for hk in range(2):
                        tok = None
                        c, wh, wl, tk = use()
                        mtok = []
                        for m_ in range(4):
                            b = 4 + 2 * (g % 2) + m_ // 2
                            o = P[b][:, 256 * (m_ % 2):256 * (m_ % 2) + 256]
                            s = slice(128 * m_, 128 * m_ + 128)
                            for k in range(4):
                                mm(o, wh[:, k, s], xh[:, 4 * hk + k, :], hk == 0 and k == 0 and m_ % 2 == 0, tk, xt, pfree[b])
                                mm(o, wh[:, k, s], xl[:, 4 * hk + k, :], False)
                                tok = mm(o, wl[:, k, s], xh[:, 4 * hk + k, :], False, sig=(k == 3 and m_ % 2 == 1))
                            if m_ % 2 == 1:
                                mtok.append(tok)
                        release(c, tok)
                        next(ex, None)
                    v = g % 2
                    tl_ = []
                    for half in range(2):
                        b = 4 + 2 * v + half
                        hs = slice(512 * half, 512 * half + 512)
                        os_ = slice(1024 * v + 512 * half, 1024 * v + 512 * half + 512)
                        prev = act_free.get((v, half))
                        ta = act(rel[v][:, hs], P[b][:, :], ACT.Relu, mtok[half], prev, F)
                        pfree[b] = [ta]
                        ta = act(sqr[v][:, hs], rel[v][:, hs], ACT.Square, ta)
                        th = copy(oth[:, os_], sqr[v][:, hs], ta, mlp_used.get(v), F)
                        tv = tt(otl[:, os_], sqr[v][:, hs], oth[:, os_], ALU.subtract, th)
                        act_free[(v, half)] = tv
                        tl_.append(tv)
                    next_t[g] = tl_
                if g > 0:
                    v = (g - 1) % 2
                    for kk in range(2):
                        f = lambda q, k, t, v=v: q[:, 1024 * v + 256 * k + 128 * t:1024 * v + 256 * k + 128 * t + 128]
                        toks = back(2 * kk, lambda k, t: f(oth, k, t), lambda k, t: f(otl, k, t), g == 1 and kk == 0,
                                    False, next_t[g - 1][kk], F)
                        next(ex, None)
                    mlp_used[v] = toks[-1]
            for _ in ex:
                pass
            ring[0] = 4
            return residual(toks, (r2, tr2))

        act_free, mlp_used, next_t = {}, {}, {}

        AB = 8192
        biasM = view(AB, 3072, "p (h n) -> p h n", h=8)
        A_IND = 11264

        def bias_steps():
            F = fence()
            pq = view(AR - 900, 256)
            pkf = view(AR - 1000, 64)
            Aq = pq
            t1 = copy(pq, pqi, IN, F)
            t1 = ts(Aq, pq, K("tb"), None, ALU.subtract, None, t1)
            t2 = copy(pkf, pki, IN, F)
            tb = arena[:, AR - 256:AR - 208].bitcast(BF16).rearrange("p (a n) -> p a n", a=3)
            dd = arena[:, AR - 208:AR - 176]
            de = arena[:, AR - 176:AR - 144]
            tk = tt(dd, tab, tabs, ALU.subtract, IN, F)
            tk = copy(tb[:, 0, :], dd, tk)
            tk = tt(de, dd, tb[:, 0, :], ALU.subtract, tk)
            tk = copy(tb[:, 1, :], de, tk)
            tk = tt(dd, de, tb[:, 1, :], ALU.subtract, tk)
            t_tb = copy(tb[:, 2, :], dd, tk)
            yield
            ind = [arena[:, A_IND + 2048 * i:A_IND + 2048 * i + 2048].bitcast(BF16).rearrange("p (g q) -> p g q", g=16)
                   for i in range(2)]
            usedi = {}
            for q_ in range(4):
                iv = ind[q_ % 2]
                a_ = bc(Aq.unsqueeze(1), 1, 16)
                b_ = bc(pkf[:, 16 * q_:16 * q_ + 16].unsqueeze(2), 2, 256)
                ti = tt(iv, a_, b_, ALU.is_ge, t1, t2, usedi.get(q_ % 2))
                for _ in range(3):
                    yield
                for t in range(2):
                    nk = 2 + 2 * t
                    b = bias_bank
                    n = 8 * nk
                    for g_ in range(16):
                        for p_ in range(3):
                            tk = mm(P[b][:, n * g_:n * g_ + n], iv[0:32 * nk, g_, 128 * t:128 * t + 128],
                                    tb[0:32 * nk, p_, 0:n], p_ == 0, ti, t_tb, pfree[b], sig=(g_ == 15 and p_ == 2))
                    base = 0 if t == 0 else 128
                    for k_ in range(nk):
                        d = biasM[:, :, base + 64 * k_ + 16 * q_:base + 64 * k_ + 16 * q_ + 16]
                        s_ = P[b][:, 0:16 * n].rearrange("p (g k h) -> p k h g", g=16, k=nk)[:, k_]
                        m_ = K("mask")[:, base + 64 * k_ + 16 * q_:base + 64 * k_ + 16 * q_ + 16]
                        tv = tt(d, s_, bc(m_.unsqueeze(1), 1, 8), ALU.add, tk, F)
                    pfree[b] = [tv]
                    yield
                usedi[q_ % 2] = tk
            biasdone.append(tv)

        biasdone = []
        bias_bank = 7
        if stop >= 2:
            for _ in bias_steps():
                pass
            tX = mlp(0, tX)

        def tok_heads(g, pair, dst, tok, scale=None, sct=()):
            tks = []
            for t in range(2):
                if scale is None:
                    ta = act(dst(t), P[pair + t][:, :], ACT.Copy, tok, sct)
                else:
                    ta = act(dst(t), P[pair + t][:, :], ACT.Copy, tok, sct, scale=scale[:, t:t + 1])
                pfree[pair + t] = [ta]
                tks.append(ta)
            return tks[-1]

        def proj_heads(xs, g, which, pair, r, tr, bufs, V, kT_, qT_, gain, rq, F, xt):
            th, tl = xs
            for hk in range(2):
                c, wh, wl, tk = use()
                for t in range(2):
                    s = slice(128 * t, 128 * t + 128)
                    for k in range(4):
                        tok = mm3(P[pair + t][:, :], th[:, 4 * hk + k, s], tl[:, 4 * hk + k, s], wh[:, k, :], wl[:, k, :],
                                  hk == 0 and k == 0, tk, xt, pfree[pair + t], sig=(k == 3))
                    yield
                release(c, tok)
            if which == "v":
                ready[("v", g)] = tok_heads(g, pair, lambda t: V[:, t, 512 * g:512 * g + 512], tok, r, [tr, F])
                yield
                return
            buf = bufs[which]
            prev = qk_used.get(which)
            ta = tok_heads(g, pair, lambda t: buf[:, t, :], tok, r, [tr, F, prev])
            for t in range(2):
                v4 = buf[:, t, :].rearrange("p (h n) -> p h n", h=4)
                r_, tr_ = head_rstd(v4, 4, 128, ta, sqb)
                if which == "k":
                    tk = tt(v4, v4, bc(r_.unsqueeze(2), 2, 128), ALU.mult, tr_)
                else:
                    tk = ts(rq[:, t, 4 * g:4 * g + 4], r_, float(128 ** -0.5), None, ALU.mult, None, tr_, F)
                    ready[("rq", g)] = tk
            yield
            for j in range(2):
                h0 = 4 * g + 2 * j
                src = lambda t, h: buf[:, t, 128 * (h - 4 * g):128 * (h - 4 * g) + 128]
                tk2 = heads_T(kT_ if which == "k" else qT_, src, h0, gain if which == "k" else None,
                              tk if which == "k" else ta, F)
                ready[(which, h0)] = ready[(which, h0 + 1)] = tk2
                yield
            qk_used[which] = (done["pe"], count["pe"])

        qk_used = {}
        sqb = None
        if stop >= 3:
            F = fence()
            ready.clear()
            qk_used.clear()
            attention.used.clear()
            ot_t.clear()
            V = view(0, 2048, "p (t n) -> p t n", t=2)
            kT = view(2048, 2048, "p (h n) -> p h n", h=8)
            qT = view(4096, 2048, "p (h n) -> p h n", h=8)
            bufs = {"q": view(6144, 1024, "p (t n) -> p t n", t=2), "k": view(7168, 1024, "p (t n) -> p t n", t=2)}
            rq = view(11264, 16, "p (t h) -> p t h", t=2)
            sqb = view(11300, 512)
            ab = abufs(11900)
            xt = transposed(X, "attn1", xh, xl, tX, free=F)
            ss, tk = mean_squares(X, view(11900, 1024), tX, F)
            r1, tr1 = rsqrt(ss, 2, 1.0 / D, tk)
            gm = small_tile(1)
            t_gm = tt(gm, C("mobaq"), C("mobak"), ALU.mult, IN)
            sqf[0] = F

            def moba_proj(g):
                for i_, w_ in enumerate(("q", "k", "v")):
                    yield from proj_heads((xh, xl), g, w_, 2 * (i_ % 2), r1, tr1, bufs, V, kT, qT, gm, rq, [F, t_gm], xt)

            def moba_attn(heads):
                return attention(heads, lambda h: qT[:, h, :], lambda h: kT[:, h, :],
                                 lambda h, t: V[:, t, 128 * h:128 * h + 128],
                                 lambda h: ([rq[:, t, h:h + 1] for t in range(2)], ready[("rq", h // 4)]),
                                 lambda h: (biasM[:, h, :], biasdone[0]), ab, keep_o, after=F,
                                 ready=lambda h: [ready[("q", h)], ready[("k", h)], ready[("v", h // 4)]])

            for _ in moba_proj(0):
                pass
            interleave(moba_attn(range(0, 4)), moba_proj(1), 1)
            o_phase(moba_attn(range(4, 8)))
            tX = residual(final["t"])
        if stop >= 4:
            tX = mlp(1, tX)

        def normalised(dst, tok, F):
            ss, tk = mean_squares(X, dst[:, 0, :], tok, F)
            r_, tr = rsqrt(ss, 2, 1.0 / D, tk)
            for t in range(2):
                tk = ts(dst[:, t, :], X[:, t, :], r_[:, t:t + 1], None, ALU.mult, None, tr, tk)
            return tk

        s_pn = sem("s_pn")
        npn = [0]

        def post_row(name, a, F):
            g = view(a, 1024)
            dma(lambda e: e.dma_start(g, bc(A[name].rearrange("(a d) -> a d", a=1), 0, 128)), s_pn, F)
            npn[0] += 16
            return g, (s_pn, npn[0])

        def post_norm(toks, grow, tg, a):
            ss = small_tile(4)
            tmp = view(a, 2048, "p (t n) -> p t n", t=2)
            for b in range(4):
                tk = act(tmp[:, b // 2, 512 * (b % 2):512 * (b % 2) + 512], P[b][:, :], ACT.Square, toks[b],
                         accum=ss[:, b:b + 1])
            s2_ = small_tile(2)
            sv = ss.rearrange("p (t c) -> p t c", t=2)
            tk = tt(s2_.unsqueeze(2), sv[:, :, 0:1], sv[:, :, 1:2], ALU.add, tk)
            r_, tr = rsqrt(s2_, 2, 1.0 / D, tk)
            for b in range(4):
                d = tmp[:, b // 2, 512 * (b % 2):512 * (b % 2) + 512]
                tk = stt(d, P[b][:, :], r_[:, b // 2:b // 2 + 1], grow[:, 512 * (b % 2):512 * (b % 2) + 512],
                         ALU.mult, ALU.mult, tr, tg)
                pfree[b] = [tk]
            for t in range(2):
                tk = tt(X[:, t, :], X[:, t, :], tmp[:, t, :], ALU.add, tk)
            return tk

        if stop >= 5:
            F = fence()
            ot_t.clear()
            kS = view(0, 2048, "p (h n) -> p h n", h=8)
            qS = view(2048, 2048, "p (h n) -> p h n", h=8)
            BA = view(4096, 6144, "p (h n) -> p h n", h=8)
            Vt = view(10240, 2048, "p (t h n) -> p t h n", t=2, h=8)
            zT = view(12288, 2048, "p (h n) -> p h n", h=8)
            cva = [view(14336 + 512 * i, 512) for i in range(3)]
            vS = view(14336 + 1536, 1024, "p (h n) -> p h n", h=4)
            XY = 16896
            Xi, Yi, W1, X2 = (view(XY, 512), None, None, None)
            Xn = view(4096, 2048, "p (t n) -> p t n", t=2)
            tk = normalised(Xn, tX, F)
            xt = transposed(Xn, "gdnpre", xh, xl, tk, free=F)
            c, wh, wl, tk = use()
            for t in range(2):
                s = slice(128 * t, 128 * t + 128)
                for k in range(8):
                    tok = mm3(P[t][:, 0:16], xh[:, k, s], xl[:, k, s], wh[:, k, :], wl[:, k, :], k == 0, tk, xt,
                              pfree[t], sig=(k == 7))
            release(c, tok)
            ab_ = small_tile(32).rearrange("p (t n) -> p t n", t=2)
            for t in range(2):
                tab_ = copy(ab_[:, t, :], P[t][:, 0:16], tok)
                pfree[t] = [tab_]
            conv_o = COLS["conv"][0]
            cvf = {}
            cvi = [0]

            def conv_silu(pair, m0, dst, tok):
                for half in range(2):
                    b = pair + half
                    i = cvi[0] % len(cva)
                    cvi[0] += 1
                    acc = cva[i].rearrange("p (m n) -> p m n", m=2)
                    for j in range(2):
                        wj = lambda tap: cols[:, conv_o + 4 * (m0 + 2 * half + j) + tap:conv_o + 4 * (m0 + 2 * half + j) + tap + 1]
                        ta = act(acc[:, j, :], P[b][:, 256 * j:256 * j + 256], ACT.Copy, tok, cvf.get(i), F, scale=wj(3))
                    for tap in (2, 1, 0):
                        d = 3 - tap
                        for j in range(2):
                            sc = cols[:, conv_o + 4 * (m0 + 2 * half + j) + tap:conv_o + 4 * (m0 + 2 * half + j) + tap + 1]
                            tv = stt(acc[:, j, d:256], P[b][:, 256 * j:256 * j + 256 - d], sc, acc[:, j, d:256],
                                     ALU.mult, ALU.add, ta if tap == 2 else last[j])
                            last[j] = tv
                    pfree[b] = [tv]
                    dd = dst[:, 2 * half:2 * half + 2, :]
                    cvf[i] = act(dd, acc, ACT.Silu, tv, F)
                return cvf[i]

            last = [None, None]
            gt = {}

            def gdn_in(name, g, i):
                pair = 2 * (i % 2)
                for hk in range(2):
                    tok = proj_w(pair, xh, xl, 4 * hk, hk == 0, xt)
                    yield
                if name == "z":
                    for half in range(2):
                        tk = act(zT[:, 4 * g + 2 * half:4 * g + 2 * half + 2, :],
                                 P[pair + half][:, :].rearrange("p (m n) -> p m n", m=2), ACT.Silu, tok, F)
                        pfree[pair + half] = [tk]
                    gt[("z", g)] = tk
                    yield
                    return
                if name == "v":
                    tk = conv_silu(pair, 16 + 4 * g, vS, tok)
                    yield
                    for hp in range(2):
                        b = bank()
                        for j in range(2):
                            for t in range(2):
                                o = P[b][:, 256 * j + 128 * t:256 * j + 128 * t + 128]
                                i_ = vS[:, 2 * hp + j, 128 * t:128 * t + 128]
                                tp2 = op("pe", lambda e, o=o, i_=i_: e.transpose(o, i_, ident), tk, pfree[b],
                                         sig=(j == 1 and t == 1))
                        h0 = 4 * g + 2 * hp
                        for j in range(2):
                            for t in range(2):
                                tv = ts(Vt[:, t, h0 + j, :], P[b][:, 256 * j + 128 * t:256 * j + 128 * t + 128],
                                        beta[:, t, h0 + j:h0 + j + 1], None, ALU.mult, None, tp2, t_beta, F)
                        pfree[b] = [tv]
                        gt[("v", h0)] = gt[("v", h0 + 1)] = tv
                        yield
                    return
                dst = (kS if name == "k" else qS)[:, 4 * g:4 * g + 4, :]
                gt[(name, g)] = conv_silu(pair, (8 if name == "k" else 0) + 4 * g, dst, tok)
                yield

            for i, (nm, g) in enumerate((("k", 0), ("q", 0), ("k", 1), ("q", 1))):
                for _ in gdn_in(nm, g, i):
                    pass
            b_ss = bank()
            sqp = [view(14336 + 1536 + 256 * i, 256) for i in range(4)]
            spf = {}
            for h in range(8):
                for qi, (src, nm) in enumerate(((kS, "k"), (qS, "q"))):
                    i = (2 * h + qi) % 4
                    tq = tt(sqp[i], src[:, h, :], src[:, h, :], ALU.mult, gt[(nm, h // 4)], spf.get(i), F, eng="pool")
                    for t in range(2):
                        o = P[b_ss][:, 16 * t + 8 * qi + h:16 * t + 8 * qi + h + 1]
                        tk = mm(o, sqp[i][:, 128 * t:128 * t + 128], K("ones")[:, 0:1], True, tq, pfree[b_ss], sig=(t == 1))
                    spf[i] = tk
            sst = small_tile(32)
            t_ss = ts(sst, P[b_ss][:, 0:32], EPS, None, ALU.add, None, tk)
            pfree[b_ss] = [t_ss]
            lnr = small_tile(32)
            t_ln = act(lnr, sst, ACT.Ln, t_ss)
            xx = small_tile(32).rearrange("p (t n) -> p t n", t=2)
            tt(xx[:, :, 0:8], ab_[:, :, 0:8], bc(RW("dt").unsqueeze(1), 1, 2), ALU.add, IN, tab_)
            tk = ts(xx[:, :, 8:16], ab_[:, :, 8:16], -1.0, None, ALU.mult, None)
            e0, e1, e2, sp = (small_tile(32).rearrange("p (t n) -> p t n", t=2) for _ in range(4))
            ta = act(e0, xx, ACT.Abs, tk)
            ta = act(e1, e0, ACT.Exp, ta, scale=-1.0)
            ta = act(e2, e1, ACT.Ln, ta, bias=1.0)
            tk = stt(sp, xx, 0.0, e2, ALU.max, ALU.add, ta)
            ea = small_tile(8)
            ta = act(ea, RW("alog"), ACT.Exp, IN)
            gg = small_tile(16).rearrange("p (t n) -> p t n", t=2)
            nb_ = small_tile(16).rearrange("p (t n) -> p t n", t=2)
            tg_ = stt(gg, sp[:, :, 0:8], -1.0, bc(ea.unsqueeze(1), 1, 2), ALU.mult, ALU.mult, ta, tk)
            tn_ = ts(nb_, sp[:, :, 8:16], -1.0, None, ALU.mult, None, tk)
            beta = small_tile(16).rearrange("p (t n) -> p t n", t=2)
            t_beta = act(beta, nb_, ACT.Exp, tn_)
            b = bank()
            for t in range(2):
                mm(P[b][:, 8 * t:8 * t + 8], K("tri"), gg[:, t, :], True, tg_, pfree[b])
            tk = mm(P[b][:, 16:24], K("ones"), gg[:, 0, :], True, sig=True)
            cum = small_tile(24)
            t_cum = copy(cum, P[b][:, 0:24], tk)
            pfree[b] = [t_cum]
            cu = cum[:, 0:16].rearrange("p (t n) -> p t n", t=2)
            lr = lnr.rearrange("p (t n) -> p t n", t=2)
            cb = small_tile(24)
            cbv = cb[:, 0:16].rearrange("p (t n) -> p t n", t=2)
            rw = small_tile(32).rearrange("p (t n) -> p t n", t=2)
            tmpc = small_tile(16).rearrange("p (t n) -> p t n", t=2)
            tk = stt(cbv, lr[:, :, 0:8], -0.5, cu, ALU.mult, ALU.subtract, t_cum, t_ln)
            t_cb = tt(cb[:, 16:24], cb[:, 0:8], cum[:, 16:24], ALU.add, tk)
            tk = tt(tmpc, cu, nb_, ALU.add, tn_)
            tk = stt(rw[:, :, 0:8], lr[:, :, 0:8], -0.5, tmpc, ALU.mult, ALU.add, tk)
            tk = stt(tmpc, lr[:, :, 8:16], -0.5, cu, ALU.mult, ALU.add, tk)
            t_rw = ts(rw[:, :, 8:16], tmpc, float(-0.5 * np.log(128.0)), None, ALU.add, None, tk)
            b = bank()
            for t in range(2):
                o, i = P[b][0:16, 128 * t:128 * t + 128], rw[:, t, :]
                tk = op("pe", lambda e, o=o, i=i: e.transpose(o, i, ident), t_rw, pfree[b], sig=(t == 1))
            rT = small_tile(256)
            t_rT = copy(rT[0:16, :], P[b][0:16, 0:256], tk)
            pfree[b] = [t_rT]

            Dring = [view(14336 + 1536 + 0, 768)]
            dfree = [spf[i] for i in range(4)] + [cvf[i] for i in range(3)]
            Dt = [view(14336 + 768 * i, 768) for i in range(2)]
            dused = {}
            for h in range(8):
                rb = bank()
                for j in range(2):
                    o = P[rb][:, :].rearrange("p (t a n) -> p t a n", t=2, a=2)[:, :, j, :]
                    l = bc(ident[0:16, h + 8 * j:h + 8 * j + 1], 1, 128)
                    tk = mm(o, l, rT[0:16, :].rearrange("p (t n) -> p t n", t=2), True, t_rT, pfree[rb], sig=(j == 1))
                dt_ = Dt[h % 2]
                fr = [dused.get(h % 2), dfree]
                ts(dt_[:, 0:256], P[rb][:, 0:256], cb[:, h:h + 1], 80.0, ALU.add, ALU.min, tk, t_cb, *fr)
                ts(dt_[:, 256:512], P[rb][:, 256:512], cb[:, 16 + h:17 + h], 80.0, ALU.add, ALU.min)
                ta = ts(dt_[:, 512:768], P[rb][:, 256:512], cb[:, 8 + h:9 + h], 80.0, ALU.add, ALU.min)
                pfree[rb] = [ta]
                ta = act(dt_, dt_, ACT.Exp, ta)
                for o_, strict in ((0, 1), (128, 0), (512, 1), (640, 0)):
                    d = dt_[:, o_:o_ + 128]
                    tp3 = op("pool", lambda e, d=d, s=strict: e.affine_select(
                        out=d, in_=d, pattern=[[1, 128]], compare_op=ALU.is_ge, fill=0.0, base=-s,
                        channel_multiplier=-1), ta)
                kb = bank()
                kb2 = bank()
                for j, src in enumerate((kS, qS)):
                    o = P[kb][:, :].rearrange("p (t a n) -> p t a n", t=2, a=2)[:, :, j, :]
                    mm(o, kS[:, h, 0:128], src[:, h, :].rearrange("p (t n) -> p t n", t=2), True, pfree[kb],
                       gt[("k", h // 4)], gt[("q", h // 4)])
                    tk = mm(P[kb2][:, 128 * j:128 * j + 128], kS[:, h, 128:256], src[:, h, 128:256], True, pfree[kb2],
                            sig=(j == 1))
                t1 = stt(BA[:, h, 0:512], P[kb][:, :], -1.0, dt_[:, 0:512], ALU.mult, ALU.mult, tk, tp3, F, xt)
                t2 = stt(BA[:, h, 512:768], P[kb2][:, 0:256], -1.0, dt_[:, 512:768], ALU.mult, ALU.mult)
                pfree[kb], pfree[kb2] = [t1], [t2]
                dused[h % 2] = t2
                gt[("B", h)] = t2

            Ya = view(0, 4096, "p (g n) -> p g n", g=8)
            t_kq = fence()

            def invert(g, sl):
                Xb = view(4 * 0 + 16384 + 0, 512) if False else arena[:, 15872 + 1024 * sl:15872 + 1024 * sl + 512]
                Wb = arena[:, 15872 + 1024 * sl + 512:15872 + 1024 * sl + 1024]
                Yb = Ya[:, g, :]
                blk = lambda i: BA[:, 2 * g + i // 2, 512 * (i % 2):512 * (i % 2) + 128]
                bt = [gt[("B", 2 * g)], gt[("B", 2 * g + 1)]]
                v4 = lambda a: a.rearrange("p (b n) -> p b n", b=4)
                idb = bc(ident.unsqueeze(1), 1, 4)
                msk = lambda w, l: bc(predi[:, w, l, :].unsqueeze(1), 1, 4)
                ty = copy(v4(Yb), idb, t_kq, eng="pool")
                tx = copy(v4(Xb), idb, t_kq, inv_used.get(sl), eng="pool")
                for i in range(2):
                    bv = BA[:, 2 * g + i, :].rearrange("p (z n) -> p z n", z=6)[:, 0:5:4, :]
                    ty = op("dve", lambda e, i=i, bv=bv: e.copy_predicated(
                        Yb[:, 256 * i:256 * i + 256].rearrange("p (b n) -> p b n", b=2),
                        bc(predi[:, 0, 0, :].unsqueeze(1), 1, 2), bv), ty, bt)
                b = bank()
                for i in range(4):
                    tk = op("pe", lambda e, i=i, b=b: e.transpose(P[b][:, 128 * i:128 * i + 128], blk(i), ident), bt,
                            pfree[b], sig=(i == 3))
                tx = op("dve", lambda e, b=b: e.copy_predicated(v4(Xb), msk(1, 0), v4(P[b][:, :])), tx, tk)
                pfree[b] = [tx]
                yield
                for l in range(1, 7):
                    b = bank()
                    for i in range(4):
                        s = slice(128 * i, 128 * i + 128)
                        tk = mm(P[b][:, s], blk(i), Xb[:, s], True, tx, bt, pfree[b], sig=(i == 3))
                    tw = act(Wb, P[b][:, :], ACT.Copy, tk, inv_used.get(sl))
                    pfree[b] = [tw]
                    yield
                    b = bank()
                    for i in range(4):
                        s = slice(128 * i, 128 * i + 128)
                        tk = mm(P[b][:, s], Wb[:, s], Yb[:, s], True, tw, ty, pfree[b], sig=(i == 3))
                    if l < 6:
                        b2 = bank()
                        for i in range(4):
                            s = slice(128 * i, 128 * i + 128)
                            tk2 = mm(P[b2][:, s], Yb[:, s], Wb[:, s], True, tw, ty, pfree[b2], sig=(i == 3))
                    ty = op("dve", lambda e, b=b, l=l: e.copy_predicated(v4(Yb), msk(0, l), v4(P[b][:, :])), tk,
                            tk2 if l < 6 else None)
                    pfree[b] = [ty]
                    if l < 6:
                        tx = op("dve", lambda e, b=b2, l=l: e.copy_predicated(v4(Xb), msk(1, l), v4(P[b][:, :])), tk2)
                        pfree[b2] = [tx]
                    yield
                inv_used[sl] = tk
                gt[("Y", g)] = ty

            inv_used = {}
            ob_t = {}
            otok = view(4096 - 4096 + 4096, 0) if False else None

            def solve(h, Ub, osb):
                g, i = h // 2, 2 * (h % 2)
                Y0, Y1 = Ya[:, g, 128 * i:128 * i + 128], Ya[:, g, 128 * i + 128:128 * i + 256]
                b = bank()
                tk = mm(P[b][:, 0:128], Y0, Vt[:, 0, h, :], True, gt[("Y", g)], gt[("v", h)], pfree[b], sig=True)
                tu = act(Ub[:, 0:128], P[b][:, 0:128], ACT.Copy, tk, sol_used.get(h % 2))
                pfree[b] = [tu]
                yield
                b = bank()
                tk = mm(P[b][:, 0:128], BA[:, h, 256:384], Ub[:, 0:128], True, tu, pfree[b], sig=True)
                tr_ = tt(Ub[:, 128:256], P[b][:, 0:128], Vt[:, 1, h, :], ALU.add, tk, sol_used.get(h % 2))
                pfree[b] = [tr_]
                yield
                b = bank()
                tk = mm(P[b][:, 0:128], Y1, Ub[:, 128:256], True, tr_, pfree[b], sig=True)
                tu1 = act(Ub[:, 128:256], P[b][:, 0:128], ACT.Copy, tk)
                pfree[b] = [tu1]
                yield
                b = bank()
                mm(P[b][:, 0:128], BA[:, h, 128:256], Ub[:, 0:128], True, tu, pfree[b])
                mm(P[b][:, 128:256], BA[:, h, 384:512], Ub[:, 0:128], True)
                tk = mm(P[b][:, 128:256], BA[:, h, 640:768], Ub[:, 128:256], False, tu1, sig=True)
                sol_used[h % 2] = tk
                ta = act(BA[:, h, 0:256], P[b][:, 0:256], ACT.Copy, tk, scale=-1.0)
                pfree[b] = [ta]
                gt[("o", h)] = ta
                yield

            sol_used = {}

            def interleave_many(gens):
                gens = [iter(x) for x in gens]
                while gens:
                    gens = [x for x in gens if next(x, gens) is not gens]
                    yield

            def inversions():
                for g0 in (0, 2):
                    yield from interleave_many([invert(g0, 0), invert(g0 + 1, 1)])

            def rest_in():
                for i, (nm, g) in enumerate((("v", 0), ("v", 1), ("z", 0), ("z", 1))):
                    yield from gdn_in(nm, g, i)

            F = [F, (done["dve"], count["dve"]), (done["act"], count["act"]), (done["pool"], count["pool"])]
            vS = view(14336, 1024, "p (h n) -> p h n", h=4)
            cva = [view(14336 + 1024, 512)]
            cvf_all = {}
            cvi[0] = 0

            interleave(inversions(), rest_in(), 3)
            gn, t_gn = post_row("gdn_post_norm_2", 14336, fence())
            Ub = [arena[:, 15872 + 1024 * i:15872 + 1024 * i + 256] for i in range(2)]
            for h0 in range(0, 8, 2):
                for _ in interleave_many([solve(h0, Ub[0], None), solve(h0 + 1, Ub[1], None)]):
                    pass
                ov = BA[:, h0:h0 + 2, 0:256]
                tko = [gt[("o", h0)], gt[("o", h0 + 1)]]
                sqv = arena[:, 15872 + 256:15872 + 256 + 256]
                ss4 = small_tile(4)
                sq5 = arena[:, 15360:15872]
                ta = act(sq5.rearrange("p (h n) -> p h n", h=2), ov, ACT.Square, *tko, sqf[0], t_gn)
                tv = op("dve", lambda e, ss4=ss4, sq5=sq5: e.reduce_sum(ss4, sq5.rearrange("p (a n) -> p a n", a=4), AX), ta)
                sqf[0] = tv
                r4, tr4 = rsqrt(ss4, 4, 1.0 / 128, tv)
                for j in range(2):
                    o2 = BA[:, h0 + j, 0:256].rearrange("p (t n) -> p t n", t=2)
                    tk = tt(o2, o2, bc(r4[:, 2 * j:2 * j + 2].unsqueeze(2), 2, 128), ALU.mult, tr4, ta)
                b = bank()
                for j in range(2):
                    for t in range(2):
                        o = P[b][:, 256 * j + 128 * t:256 * j + 128 * t + 128]
                        i_ = BA[:, h0 + j, 128 * t:128 * t + 128]
                        tq = op("pe", lambda e, o=o, i_=i_: e.transpose(o, i_, ident), tk, pfree[b], sig=(j == 1 and t == 1))
                dz = zT[:, h0:h0 + 2, :]
                tz = stt(dz, P[b][:, :].rearrange("p (h n) -> p h n", h=2), C("gdno"), dz, ALU.mult, ALU.mult, tq,
                         gt[("z", 0)], gt[("z", 1)])
                pfree[b] = [tz]
                zf = zT[:, h0:h0 + 2, :]
                oo = lambda q: q[:, 256 * h0:256 * h0 + 512].rearrange("p (h n) -> p h n", h=2)
                ta = act(oo(oth), zf, ACT.Copy, tz, F)
                tv = tt(oo(otl), zf, oo(oth), ALU.subtract, ta, F)
                ot_t[h0] = ot_t[h0 + 1] = [ta, tv]
                toks = back(h0, oh, ol, h0 == 0, False, ta, tv)
            tX = post_norm(toks, gn, t_gn, 4096) if False else None
            Fp = fence()
            wait("act", Fp)
            wait("dve", Fp)
            tX = post_norm(toks, gn, t_gn, 0)

        if stop >= 6:
            F = fence()
            ready.clear()
            qk_used.clear()
            attention.used.clear()
            ot_t.clear()
            V = view(0, 2048, "p (t n) -> p t n", t=2)
            kT = view(2048, 2048, "p (h n) -> p h n", h=8)
            qT = view(4096, 2048, "p (h n) -> p h n", h=8)
            bufs = {"q": view(6144, 1024, "p (t n) -> p t n", t=2), "k": view(7168, 1024, "p (t n) -> p t n", t=2)}
            zT = view(8192, 2048, "p (h n) -> p h n", h=8)
            rq = view(10240, 16, "p (t h) -> p t h", t=2)
            sqb = view(10260, 512)
            ab = abufs(10800)
            bb = [view(13104 + 384 * i, 384) for i in range(2)]
            xh2 = oth[:, :].rearrange("p (k n) -> p k n", k=8)
            xl2 = otl[:, :].rearrange("p (k n) -> p k n", k=8)
            Xn = view(13900, 2048, "p (t n) -> p t n", t=2)
            gnf, t_gnf = post_row("fox_post_norm_2", 15960, F)
            gz = view(16984, 512)
            sqf[0] = F
            tk = normalised(Xn, tX, F)
            xt = transposed(Xn, "kvn", xh, xl, tk, free=F)
            xt2 = transposed(Xn, "foxpre", xh2, xl2, tk, free=F)
            c, wh, wl, tk = use()
            for t in range(2):
                s = slice(128 * t, 128 * t + 128)
                for k in range(8):
                    tok = mm3(P[t][:, 0:8], xh[:, k, s], xl[:, k, s], wh[:, k, :], wl[:, k, :], k == 0, tk, xt,
                              pfree[t], sig=(k == 7))
            release(c, tok)
            fx, e0, e1, e2, lf = (small_tile(16).rearrange("p (t n) -> p t n", t=2) for _ in range(5))
            for t in range(2):
                tk = tt(fx[:, t, :], P[t][:, 0:8], RW("fbias"), ALU.add, tok, IN)
                pfree[t] = [tk]
            ta = act(e0, fx, ACT.Abs, tk)
            ta = act(e1, e0, ACT.Exp, ta, scale=-1.0)
            ta = act(e2, e1, ACT.Ln, ta, bias=1.0)
            t_lf = stt(lf, fx, 0.0, e2, ALU.min, ALU.subtract, ta)
            b = bank()
            mm(P[b][:, 0:8], K("tri"), lf[:, 0, :], True, t_lf, pfree[b])
            mm(P[b][:, 8:16], K("ones"), lf[:, 0, :], True)
            tk = mm(P[b][:, 8:16], K("tri"), lf[:, 1, :], False, sig=True)
            cc, cn = small_tile(16), small_tile(16)
            copy(cc, P[b][:, 0:16], tk)
            t_c = ts(cn, P[b][:, 0:16], -1.0, None, ALU.mult, None, tk)
            pfree[b] = [t_c]
            b = bank()
            for t in range(2):
                o, i = P[b][0:8, 128 * t:128 * t + 128], cn[:, 8 * t:8 * t + 8]
                tk = op("pe", lambda e, o=o, i=i: e.transpose(o, i, ident), t_c, pfree[b], sig=(t == 1))
            cT_ = small_tile(256)
            t_cT = copy(cT_[0:8, :], P[b][0:8, 0:256], tk)
            pfree[b] = [t_cT]
            gf = small_tile(1)
            t_gf = tt(gf, C("foxq"), C("foxk"), ALU.mult, IN)
            bb_used = {}

            def fox_bias(h):
                b = bank()
                tk = mm(P[b][:, 0:256], bc(ident[0:8, h:h + 1], 1, 128), cT_[0:8, :], True, t_cT, pfree[b], sig=True)
                d = bb[h % 2]
                m = K("mask")
                stt(d[:, 0:128], P[b][:, 0:128], cc[:, h:h + 1], m[:, 0:128], ALU.add, ALU.add, tk, F, bb_used.get(h % 2))
                tk = stt(d[:, 128:384], P[b][:, 0:256], cc[:, 8 + h:9 + h], m[:, 128:384], ALU.add, ALU.add)
                pfree[b] = [tk]
                return d, tk, lambda t_: bb_used.__setitem__(h % 2, t_)

            def fox_proj(g):
                for i_, w_ in enumerate(("k", "v", "q")):
                    xs, xq = ((xh, xl), xt) if w_ != "q" else ((xh2, xl2), xt2)
                    yield from proj_heads(xs, g, w_, 2 * (i_ % 2), None, None, bufs, V, kT, qT, gf, rq, [F, t_gf], xq)

            def fox_z():
                for g in range(2):
                    for hk in range(2):
                        tok = proj_w(2 * (g % 2), xh2, xl2, 4 * hk, hk == 0, xt2)
                        yield
                    for half in range(2):
                        b = 2 * (g % 2) + half
                        tk = act(zT[:, 4 * g + 2 * half:4 * g + 2 * half + 2, :],
                                 P[b][:, :].rearrange("p (m n) -> p m n", m=2), ACT.Silu, tok, F)
                        pfree[b] = [tk]
                    zt_t.append(tk)
                    yield

            zt_t = []
            og = xh, xl

            def fox_keep(h, b, tk):
                g_ = gz[:, 256 * (h % 2):256 * (h % 2) + 256]
                tv0 = tt(g_, P[b][:, 0:256], zT[:, h, :], ALU.mult, tk, zt_t, gz_used.get(h % 2), F)
                ta = act(xh[:, h, :], g_, ACT.Copy, tv0, fkv)
                tv = tt(xl[:, h, :], g_, xh[:, h, :], ALU.subtract, ta, fkv)
                gz_used[h % 2] = tv
                ot_t[h] = [ta, tv]
                return [tv0]

            gz_used = {}

            def fox_attn(heads):
                return attention(heads, lambda h: qT[:, h, :], lambda h: kT[:, h, :],
                                 lambda h, t: V[:, t, 128 * h:128 * h + 128],
                                 lambda h: ([rq[:, t, h:h + 1] for t in range(2)], ready[("rq", h // 4)]),
                                 fox_bias, ab, fox_keep, after=F,
                                 ready=lambda h: [ready[("q", h)], ready[("k", h)], ready[("v", h // 4)]])

            for g in range(2):
                for _ in fox_proj(g):
                    pass
            for _ in fox_z():
                pass
            fkv = [(done["pe"], count["pe"])]
            gen = o_product(0, range(4), lambda k, t: xh[:, k, 128 * t:128 * t + 128],
                            lambda k, t: xl[:, k, 128 * t:128 * t + 128])
            for _ in fox_attn(range(8)):
                next(gen, None)
            for _ in gen:
                pass
            Fp = fence()
            wait("act", Fp)
            wait("dve", Fp)
            tX = post_norm(final["t"], gnf, t_gnf, 0)
        finish(tX)

        block = ctx.enter_context(nc.Block())

        def play(eng, entries):
            for kind, a, b, *n in entries:
                if kind == "wait":
                    eng.wait_ge(a, b)
                else:
                    ins = a(eng)
                    if b is not None:
                        ins.then_inc(b, n[0])

        @block.sync
        def _(eng):
            play(eng, queue["sp"])

        @block.scalar
        def _(eng):
            play(eng, queue["act"])

        @block.vector
        def _(eng):
            play(eng, queue["dve"])

        @block.gpsimd
        def _(eng):
            play(eng, queue["pool"])

        @block.tensor
        def _(eng):
            play(eng, queue["pe"])


def constants():
    c = np.zeros((128, NCST), np.float32)
    p = np.arange(128)
    c[:, 0:128] = np.eye(128, dtype=np.float32)
    causal = np.where(p[None, :] <= p[:, None], 0.0, NEG)
    c[:, 128:256] = causal
    c[:, 384:512] = causal
    c[:, 512:640] = p[:, None] <= p[None, :]
    c[:, 640:768] = 1.0
    limits = [-1.0e9] + list(range(1, 17)) + [21, 27, 35, 46, 59, 77, 99, 128, 166, 216, 280, 363, 470, 609, 790]
    c[:, 768] = np.tile(np.array(limits, np.float32), 4)
    pred = np.zeros((128, 2, 7, 128), np.float32)
    for l in range(7):
        s = 1 << l
        m = ((p[:, None] // (2 * s)) == (p[None, :] // (2 * s))) & ((p[:, None] // s) % 2 == 0) & ((p[None, :] // s) % 2 == 1)
        pred[:, 0, l] = m
        pred[:, 1, l] = m.T
    return c, pred.reshape(128, 1792)


def kernel(**inputs):
    import numpy as _np
    import concourse.bacc as _bacc
    from concourse import mybir as _mybir
    from concourse.bass_utils import run_bass_kernel_spmd as _run

    a = {k: _np.ascontiguousarray(v) for k, v in inputs.items()}
    col = lambda v: v.reshape(-1, 128).T
    cols = _np.ascontiguousarray(_np.concatenate([
        col(a["attn_norm"][0]), col(a["attn_norm"][1]), col(a["mlp_norm"][0]), col(a["mlp_norm"][1]),
        col(a["gdn_pre_norm_2"][0]), col(a["kv_norm_2"]), col(a["fox_pre_norm_2"][0]), col(a["mla_q_a_norm"][0]),
        col(a["mla_kv_a_norm"][0]), col(a["mla_q_nope_norm"][0]), col(a["mla_k_nope_norm"][0]),
        col(a["moba_q_norm"][0]), col(a["moba_k_norm"][0]), col(a["kv_k_norm_2"]), col(a["fox_q_norm_2"][0]),
        col(a["gdn_o_norm_2"][0]),
        a["gdn_conv_w_2"][0].reshape(4, 24, 128).transpose(2, 1, 0).reshape(128, 96)], axis=1))
    invf = _np.float32(10000.0) ** (-_np.arange(0, 64, 2, dtype=_np.float32) / _np.float32(64))
    rows = _np.concatenate([a["mla_q_rope_norm"][0], a["mla_k_rope_norm"][0], a["gdn_a_log_2"][0],
                            a["gdn_dt_bias_2"][0], a["kv_forget_bias_2"], invf.astype(_np.float32)])
    cst, pred = constants()
    arrays = {
        "x": a["x"][0], "positions": a["positions"], "rel_bias_table": a["rel_bias_table"],
        "mla_w_in": a["mla_w_in"][0], "mla_w_uq": a["mla_w_uq"][0], "mla_w_ukv": a["mla_w_ukv"][0],
        "mla_w_o": a["mla_w_o"][0], "moba_w_qkv": a["moba_w_qkv"][0], "moba_w_o": a["moba_w_o"][0],
        "mlp_w_in": a["mlp_w_in"], "mlp_w_out": a["mlp_w_out"], "gdn_w_in": a["gdn_w_in_2"][0],
        "gdn_w_out": a["gdn_w_out_2"][0], "kv_w": a["kv_w_2"], "fox_w_in": a["fox_w_in_2"][0],
        "fox_w_out": a["fox_w_out_2"][0], "gdn_post_norm_2": a["gdn_post_norm_2"][0],
        "fox_post_norm_2": a["fox_post_norm_2"][0],
        "c_cols": cols, "c_rows": rows, "c_cst": cst, "c_pred": pred,
        "c_posT": _np.ascontiguousarray(a["positions"].reshape(2, 128).T),
    }
    arrays = {k + "_dram": _np.ascontiguousarray(v) for k, v in arrays.items()}
    nc = _bacc.Bacc("TRN2", target_bir_lowering=False, num_devices=1)
    aps = {k[:-5]: nc.dram_tensor(k, v.shape, _mybir.dt.from_np(v.dtype), kind="ExternalInput").ap()
           for k, v in arrays.items()}
    out = nc.dram_tensor("out_dram", (256, 1024), _mybir.dt.float32, kind="ExternalOutput").ap()
    bass_two_blocks(nc, aps, out)
    r = _run(nc, [arrays], core_ids=[0])
    return r.results[0]["out_dram"].reshape(1, 256, 1024)
```

```python
import numpy as np
import concourse.bass as bass
import concourse.mybir as mybir
from contextlib import ExitStack

F32 = mybir.dt.float32
F32R = mybir.dt.float32r
BF16 = mybir.dt.bfloat16
I32 = mybir.dt.int32
ALU = mybir.AluOpType
ACT = mybir.ActivationFunctionType
AX = mybir.AxisListType.X

T = 256
D = 1024
NEG = -1.0e30
EPS = 1e-6
RAW = 3
SPLIT = 3
CH = 2048

COLS = {}
_at = 0
for _n, _w in (("attn0", 8), ("attn1", 8), ("mlp0", 8), ("mlp1", 8), ("gdnpre", 8), ("kvn", 8), ("foxpre", 8),
               ("qa", 3), ("kva", 2), ("mlaqn", 1), ("mlakn", 1), ("mobaq", 1), ("mobak", 1), ("foxk", 1), ("foxq", 1),
               ("gdno", 1), ("conv", 96)):
    COLS[_n] = (_at, _w)
    _at += _w
NCOLS = _at
ROWS = {"ropeq": (0, 64), "ropek": (64, 64), "alog": (128, 8), "dt": (136, 8), "fbias": (144, 8), "invf": (152, 32)}
NROWS = 184
CST = {"ident": (0, 128), "mask": (128, 384), "tri": (512, 128), "ones": (640, 128), "tb": (768, 1),
       "negid": (769, 128)}
NCST = 897


def bc(ap, dim, n):
    shape = list(ap.shape)
    shape[dim] = n
    return ap.broadcast_to(shape)


def bass_two_blocks(nc, A, out, stop=99):
    ctx = ExitStack()
    with ctx:
        def sb(name, shape, dt=F32):
            return ctx.enter_context(nc.sbuf_tensor(name, shape, dt))

        def sem(name):
            return ctx.enter_context(nc.semaphore(name))

        queue = {e: [] for e in ("pe", "act", "dve", "pool", "sp")}
        done = {e: sem("s_" + e) for e in ("pe", "act", "dve", "pool")}
        count = {e: 0 for e in done}
        waited = {}

        def wait(eng, tokens):
            for t in tokens:
                if t is None:
                    continue
                if not (len(t) == 2 and isinstance(t[1], int)):
                    wait(eng, t)
                    continue
                s, v = t
                if waited.get((eng, id(s)), 0) < v:
                    waited[(eng, id(s))] = v
                    queue[eng].append(("wait", s, v))

        def op(eng, fn, *tokens, sig=True):
            wait(eng, tokens)
            if sig:
                count[eng] += 1
                queue[eng].append(("run", fn, done[eng], 1))
                return (done[eng], count[eng])
            queue[eng].append(("run", fn, None, 0))
            return None

        def dma(fn, s, *tokens):
            wait("sp", tokens)
            queue["sp"].append(("run", fn, s, 16))

        def act(o, i, func, *tokens, bias=0.0, scale=1.0, accum=None):
            return op("act", lambda e: e.activation(o, i, func, bias=bias, scale=scale, accum_out=accum)
                      if accum is not None else e.activation(o, i, func, bias=bias, scale=scale), *tokens)

        def table(name):
            queue["act"].append(("run", lambda e: e.preload_act_table_set(name), None, 0))

        def tt(o, a, b, f, *tokens, eng="dve"):
            return op(eng, lambda e: e.tensor_tensor(o, a, b, f), *tokens)

        def ts(o, a, s1, s2, f1, f2, *tokens, eng="dve"):
            return op(eng, lambda e: e.tensor_scalar(o, a, s1, s2, f1, f2) if f2 is not None
                      else e.tensor_scalar(o, a, s1, None, f1), *tokens)

        def stt(o, a, s, b, f1, f2, *tokens):
            return op("dve", lambda e: e.scalar_tensor_tensor(out=o, in0=a, scalar=s, in1=b, op0=f1, op1=f2), *tokens)

        def copy(o, a, *tokens, eng="dve"):
            return op(eng, lambda e: e.tensor_copy(o, a), *tokens)

        def mm(o, l, r, start, *tokens, sig=False):
            return op("pe", lambda e: e.matmul(o, l, r, start=start, stop=True, skip_group_check=True), *tokens, sig=sig)

        def mm3(o, lh, ll, rh, rl, start, *tokens, sig=False):
            mm(o, lh, rh, start, *tokens)
            mm(o, lh, rl, False)
            return mm(o, ll, rh, False, sig=sig)

        cst = sb("cst", [128, NCST])
        cols = sb("cols", [128, NCOLS])
        rows = sb("rows", [128, NROWS])
        level_mask = sb("level_mask", [128, 7, 128], BF16)[:, :, :]
        identr = sb("identr", [128, 128], F32R)[:, :]
        X = sb("X", [128, 2, D])
        xh = sb("xh", [128, 8, T], F32R)
        xl = sb("xl", [128, 8, T], F32R)
        raw = [sb(f"raw{i}", [128, CH]) for i in range(RAW)]
        whi = [sb(f"whi{i}", [128, CH], F32R) for i in range(SPLIT)]
        wlo = [sb(f"wlo{i}", [128, CH], F32R) for i in range(SPLIT)]
        oth = sb("oth", [128, 2048], F32R)
        otl = sb("otl", [128, 2048], F32R)
        st = sb("st", [128, 1024])
        pint = sb("pint", [128, 384])
        AR = 20600
        arena = sb("arena", [128, AR])

        P = [ctx.enter_context(nc.psum_tensor(f"ps{i}", [128, 512], F32)) for i in range(8)]
        pfree = [[] for _ in range(8)]
        ring = [4]

        def bank():
            b = ring[0]
            ring[0] = 4 + (b - 3) % 4
            return b

        def C(name, j=None):
            a, w = COLS[name]
            return cols[:, a:a + w] if j is None else cols[:, a + j:a + j + 1]

        def K(name):
            a, w = CST[name]
            return cst[:, a:a + w]

        def RW(name):
            a, w = ROWS[name]
            return rows[:, a:a + w]

        ident = K("ident")

        s_in = sem("s_in")
        s_x = sem("s_x")
        s_out = sem("s_out")
        n_in = [0]

        def small(o, i):
            dma(lambda e: e.dma_start(o, i), s_in)
            n_in[0] += 16

        dma(lambda e: e.dma_start(X[:, :, :], A["x"].rearrange("(t p) d -> p t d", p=128)), s_x)
        small(cst[:, :], A["c_cst"])
        small(cols[:, :], A["c_cols"])
        small(rows[:, :], bc(A["c_rows"].rearrange("(a d) -> a d", a=1), 0, 128))
        posT = st[:, 0:2].bitcast(I32)
        small(posT, A["c_posT"])
        pqi = pint[:, 0:256].bitcast(I32)
        small(pqi, bc(A["positions"], 0, 128))
        pki = pint[:, 256:320].bitcast(I32)
        for kk in range(4):
            small(pki[32 * kk:32 * kk + 32, :], bc(A["positions"][:, 64 * kk:64 * kk + 64], 0, 32))
        tab = pint[:, 320:352]
        tabs = pint[:, 352:384]
        z0 = op("dve", lambda e: e.memset(pint[:, 320:384], 0.0))
        wait("sp", [z0])
        for kk in range(4):
            small(tab[32 * kk:32 * kk + 32, 8 * kk:8 * kk + 8], A["rel_bias_table"])
            small(tabs[32 * kk + 1:32 * kk + 32, 8 * kk:8 * kk + 8], A["rel_bias_table"][0:31, :])
        IN = (s_in, n_in[0])
        t_idr = op("dve", lambda e: e.tensor_copy(identr, ident), IN)
        INX = (s_x, 16)

        specs = []

        def add(src, a, b):
            specs.append((src, a, b))
            return len(specs) - 1

        def kslab(w, k0, nk, c0, nc_):
            return add(w[128 * k0:128 * (k0 + nk), c0:c0 + nc_].rearrange("(k p) n -> p k n", p=128), nk, nc_)

        def columns(w, *starts):
            for c0 in starts:
                for hk in range(2):
                    kslab(w, 4 * hk, 4, c0, 512)

        def down(w):
            for k in range(0, 8, 2):
                kslab(w, k, 2, 0, 1024)

        for k in range(0, 8, 2):
            kslab(A["mla_w_in"], k, 2, 0, 704)
        for g in range(2):
            kslab(A["mla_w_ukv"], 0, 2, 1024 * g, 1024)
            for i in range(2):
                kslab(A["mla_w_uq"], 0, 3, 768 * g + 384 * i, 384)
        down(A["mla_w_o"])

        def mlp_specs(i):
            for g in range(9):
                if g < 8:
                    columns(A["mlp_w_in"][i], 512 * g)
                if g > 0:
                    for k in range(4 * (g - 1), 4 * g, 2):
                        kslab(A["mlp_w_out"][i], k, 2, 0, 1024)

        mlp_specs(0)
        columns(A["moba_w_qkv"], 0, 1024, 2048, 512, 1536, 2560)
        down(A["moba_w_o"])
        mlp_specs(1)
        kslab(A["gdn_w_in"], 0, 8, 4096, 16)
        columns(A["gdn_w_in"], 1024, 0, 1536, 512, 2048, 2560, 3072, 3584)
        down(A["gdn_w_out"])
        columns(A["fox_w_in"], 1024, 1536)
        kslab(A["kv_w"], 0, 8, 2048, 8)
        columns(A["kv_w"], 0, 1024)
        columns(A["fox_w_in"], 0, 512)
        columns(A["kv_w"], 512, 1536)
        down(A["fox_w_out"])

        s_raw = [sem(f"s_raw{i}") for i in range(RAW)]
        loaded = [0]
        nsplit = [0]
        split_at = {}
        released = {}

        def load():
            c = loaded[0]
            if c >= len(specs):
                return
            loaded[0] += 1
            src, a, b = specs[c]
            dst = raw[c % RAW][:, 0:a * b].rearrange("p (k n) -> p k n", k=a)
            dma(lambda e: e.dma_start(dst, src), s_raw[c % RAW], *(split_at[c - RAW] if c >= RAW else ()))

        def split():
            c = nsplit[0]
            if c >= len(specs):
                return
            nsplit[0] += 1
            if loaded[0] <= c:
                load()
            _, a, b = specs[c]
            n = a * b
            r, h, l = raw[c % RAW][:, 0:n], whi[c % SPLIT][:, 0:n], wlo[c % SPLIT][:, 0:n]
            free = released.get(c - SPLIT)
            t1 = op("act", lambda e: e.activation(h, r, ACT.Copy), (s_raw[c % RAW], 16 * (c // RAW + 1)), free)
            t2 = tt(l, r, h, ALU.subtract, t1, free)
            split_at[c] = (t1, t2)
            load()

        for _ in range(RAW):
            load()
        cur = [-1]

        def use():
            cur[0] += 1
            c = cur[0]
            while nsplit[0] < min(c + SPLIT, len(specs)) and (nsplit[0] - SPLIT < 0 or (nsplit[0] - SPLIT) in released):
                split()
            _, a, b = specs[c]
            v = [w[c % SPLIT][:, 0:a * b].rearrange("p (k n) -> p k n", k=a) for w in (whi, wlo)]
            return c, v[0], v[1], split_at[c]

        def release(c, tok):
            released[c] = tok

        at = {"turn": 0, "keep": 512}

        def small_tile(n):
            if at["turn"] + n > 512:
                at["turn"] = 0
            a = at["turn"]
            at["turn"] += n
            return st[:, a:a + n]

        def keep_tile(n):
            a = at["keep"]
            at["keep"] += n
            assert at["keep"] <= 1024
            return st[:, a:a + n]

        def rsqrt(ss, n, scale, *tokens, eps=EPS, out_=None):
            m, l, r, u, v = (small_tile(n) for _ in range(5))
            w = small_tile(n) if out_ is None else out_
            t = ts(m, ss, scale, eps, ALU.mult, ALU.add, *tokens)
            t = act(l, m, ACT.Ln, t)
            t = act(r, l, ACT.Exp, t, scale=-0.5)
            t = stt(u, r, -0.5, m, ALU.mult, ALU.mult, t)
            t = tt(v, u, r, ALU.mult, t)
            t = stt(w, v, 1.5, r, ALU.add, ALU.mult, t)
            return w, t

        def pe_turn(o, i, *tokens, sig=False):
            return op("pe", lambda e: e.transpose(o, i, ident), *tokens, sig=sig)

        def transposed(tX, *sets, free=()):
            banks, res = [], []
            for j2 in range(4):
                b = bank()
                for j in (2 * j2, 2 * j2 + 1):
                    for t in range(2):
                        a = 256 * (j % 2) + 128 * t
                        tk = pe_turn(P[b][:, a:a + 128], X[:, t, 128 * j:128 * j + 128], IN, tX[j2 // 2], pfree[b],
                                     sig=(j % 2 == 1 and t == 1))
                banks.append((b, tk))
            for gain, h, l in sets:
                toks = []
                for j2, (b, tk) in enumerate(banks):
                    for j in (2 * j2, 2 * j2 + 1):
                        ta = act(h[:, j, :], P[b][:, 256 * (j % 2):256 * (j % 2) + 256], ACT.Copy, tk, IN, free,
                                 pfree[b] if toks is None else None, scale=C(gain, j))
                    for j in (2 * j2, 2 * j2 + 1):
                        tv = stt(l[:, j, :], P[b][:, 256 * (j % 2):256 * (j % 2) + 256], C(gain, j), h[:, j, :],
                                 ALU.mult, ALU.subtract, ta, IN, free)
                    banks[j2] = (b, tv)
                    pfree[b] = [ta, tv]
                    toks.append(tv)
                res.append(toks)
            return res

        def mean_squares(junk, *tokens):
            ss = small_tile(2)
            for t in range(2):
                tk = act(junk, X[:, t, :], ACT.Square, *tokens, accum=ss[:, t:t + 1])
                tokens = (tk,)
            return ss, tk

        def proj_x(pair, th, tl, xt, done_):
            for hk in range(2):
                c, wh, wl, tk = use()
                for t in range(2):
                    s = slice(128 * t, 128 * t + 128)
                    for k in range(4):
                        kk = 4 * hk + k
                        tok = mm3(P[pair + t][:, :], th[:, kk, s], tl[:, kk, s], wh[:, k, :], wl[:, k, :], kk == 0, tk,
                                  xt[kk // 2], pfree[pair + t], sig=(k == 3))
                    done_[t] = tok
                    if t == 1:
                        release(c, tok)
                    yield True

        def proj_w(pair, th, tl, xt, done_):
            for hk in range(2):
                c, wh, wl, tk = use()
                for half in range(2):
                    for m in (2 * half, 2 * half + 1):
                        o = P[pair + half][:, 256 * (m % 2):256 * (m % 2) + 256]
                        s = slice(128 * m, 128 * m + 128)
                        for k in range(4):
                            kk = 4 * hk + k
                            mm(o, wh[:, k, s], th[:, kk, :], kk == 0 and m % 2 == 0, tk, xt[kk // 2], pfree[pair + half])
                            mm(o, wh[:, k, s], tl[:, kk, :], False)
                            tok = mm(o, wl[:, k, s], th[:, kk, :], False, sig=(k == 3 and m % 2 == 1))
                    done_[half] = tok
                    if half == 1:
                        release(c, tok)
                    yield True

        def proj_few(n, th, tl, xt):
            c, wh, wl, tk = use()
            for t in range(2):
                s = slice(128 * t, 128 * t + 128)
                for k in range(8):
                    tok = mm3(P[t][:, 0:n], th[:, k, s], tl[:, k, s], wh[:, k, :], wl[:, k, :], k == 0, tk, xt[k // 2],
                              pfree[t], sig=(k == 7))
            release(c, tok)
            return tok

        def back(k0, hh, hl, first, toks, *tokens):
            c, wh, wl, tk = use()
            for ch in range(2):
                for t in range(2):
                    b = 2 * t + ch
                    for k in range(2):
                        tok = mm3(P[b][:, :], hh(k0 + k, t), hl(k0 + k, t), wh[:, k, 512 * ch:512 * ch + 512],
                                  wl[:, k, 512 * ch:512 * ch + 512], first and k == 0, tk, tokens, pfree[b],
                                  sig=(k == 1))
                    toks[b] = tok
                if ch == 1:
                    release(c, tok)
                yield True

        def residual(toks, scale=None):
            res = []
            for ch in range(2):
                for t in range(2):
                    b = 2 * t + ch
                    xs = X[:, t, 512 * ch:512 * ch + 512]
                    if scale is None:
                        tk = tt(xs, P[b][:, :], xs, ALU.add, toks[b])
                    else:
                        tk = stt(xs, P[b][:, :], scale[0][:, t:t + 1], xs, ALU.mult, ALU.add, toks[b], scale[1])
                    pfree[b] = [tk]
                res.append(tk)
            return res

        def weave(main, *sides):
            live = [[main, 1]] + [list(x) for x in sides]
            stuck = 0
            while live:
                moved = False
                for entry in list(live):
                    for _ in range(entry[1]):
                        r = next(entry[0], None)
                        if r is None:
                            live.remove(entry)
                            moved = True
                            break
                        moved = moved or r
                        if not r:
                            break
                stuck = 0 if moved else stuck + 1
                assert stuck < 3

        def chain(*gens):
            for g_ in gens:
                yield from g_

        def fence():
            return [(done[e], count[e]) for e in done]

        ready, ot_t, final = {}, {}, {}

        def attention(heads, qT, kT, V, scale, bias, a0, emit, extra=None, after=()):
            Sx = [view(a0 + 384 * i, 384) for i in range(2)]
            Pn = [view(a0 + 768 + 384 * i, 384) for i in range(3)]
            PT = [view(a0 + 1920 + 384 * i, 384) for i in range(2)]
            used, sums, prob, turned = {}, {}, {}, {}

            def score(j, h):
                b = bank()
                S, Q = Sx[j % 2], Pn[j % 3]
                for t, (c0, n) in enumerate(((0, 128), (128, 256))):
                    s = slice(128 * t, 128 * t + 128)
                    o = P[b][:, c0:c0 + n]
                    tk = mm(o, qT(h)[:, s], kT(h)[:, 0:n], True, pfree[b], ready[h], sig=(extra is None and t == 1))
                    if extra is not None:
                        q2, k2 = extra(h)
                        tk = mm(o, q2[:, s], k2[:, 0:n], False, sig=(t == 1))
                bt = bias(h)
                if isinstance(scale, float):
                    tk = stt(S, P[b][:, 0:384], scale, bt[0], ALU.mult, ALU.add, tk, bt[1], used.get(("S", j % 2)), after)
                else:
                    sc, sct = scale(h)
                    stt(S[:, 0:128], P[b][:, 0:128], sc[0], bt[0][:, 0:128], ALU.mult, ALU.add, tk, bt[1], sct,
                        used.get(("S", j % 2)), after)
                    tk = stt(S[:, 128:384], P[b][:, 128:384], sc[1], bt[0][:, 128:384], ALU.mult, ALU.add)
                if len(bt) > 2:
                    bt[2](tk)
                pfree[b] = [tk]
                mx, ng, su = small_tile(2), small_tile(2), small_tile(2)
                op("dve", lambda e: e.reduce_max(mx[:, 0:1], S[:, 0:128], AX), tk)
                tk = op("dve", lambda e: e.reduce_max(mx[:, 1:2], S[:, 128:384], AX))
                tk = ts(ng, mx, -1.0, None, ALU.mult, None, tk)
                act(Q[:, 0:128], S[:, 0:128], ACT.Exp, tk, used.get(("P", j % 3)), after, bias=ng[:, 0:1],
                    accum=su[:, 0:1])
                tk = act(Q[:, 128:384], S[:, 128:384], ACT.Exp, bias=ng[:, 1:2], accum=su[:, 1:2])
                used[("S", j % 2)] = tk
                sums[j] = (su, tk)

            def divide(j):
                su, tk = sums.pop(j)
                Q = Pn[j % 3]
                rc = small_tile(2)
                tk = op("dve", lambda e: e.reciprocal(rc, su), tk)
                ts(Q[:, 0:128], Q[:, 0:128], rc[:, 0:1], None, ALU.mult, None, tk)
                prob[j] = ts(Q[:, 128:384], Q[:, 128:384], rc[:, 1:2], None, ALU.mult, None)

            def turn(j):
                b = bank()
                for n in range(3):
                    tk = pe_turn(P[b][:, 128 * n:128 * n + 128], Pn[j % 3][:, 128 * n:128 * n + 128], prob[j], pfree[b],
                                 sig=(n == 2))
                used[("P", j % 3)] = tk
                tk = act(PT[j % 2], P[b][:, 0:384], ACT.Copy, tk, used.get(("T", j % 2)), after)
                pfree[b] = [tk]
                turned[j] = tk

            def value(j, h):
                b = bank()
                mm(P[b][:, 0:256], V(h, 0), PT[j % 2][:, 0:256], True, turned[j], pfree[b])
                tk = mm(P[b][:, 128:256], V(h, 1), PT[j % 2][:, 256:384], False, sig=True)
                used[("T", j % 2)] = tk
                pfree[b] = emit(h, b, tk)

            n = len(heads)
            for j in range(n + 3):
                if j < n:
                    while heads[j] not in ready:
                        yield False
                    score(j, heads[j])
                if 0 <= j - 1 < n:
                    divide(j - 1)
                if j < n + 1:
                    yield True
                if 0 <= j - 2 < n:
                    turn(j - 2)
                    yield True
                if 0 <= j - 3 < n:
                    value(j - 3, heads[j - 3])
                    yield True

        def o_split(h, b, tk, *tokens):
            a = act(oth[:, 256 * h:256 * h + 256], P[b][:, 0:256], ACT.Copy, tk, *tokens)
            v = tt(otl[:, 256 * h:256 * h + 256], P[b][:, 0:256], oth[:, 256 * h:256 * h + 256], ALU.subtract, a, *tokens)
            return [a, v]

        def keep_o(h, b, tk):
            ot_t[h] = o_split(h, b, tk)
            return ot_t[h]

        def oh(k, t):
            return oth[:, 256 * k + 128 * t:256 * k + 128 * t + 128]

        def ol(k, t):
            return otl[:, 256 * k + 128 * t:256 * k + 128 * t + 128]

        def view(a, n, s=None, **kw):
            v = arena[:, a:a + n]
            return v.rearrange(s, **kw) if s else v

        def o_product(hh=oh, hl=ol):
            for p_ in range(4):
                while 2 * p_ + 1 not in ot_t:
                    yield False
                yield from back(2 * p_, hh, hl, p_ == 0, final, ot_t[2 * p_], ot_t[2 * p_ + 1])

        def stage():
            at["keep"] = 512
            ready.clear()
            ot_t.clear()
            final.clear()
            qk_used.clear()
            return fence()

        qk_used = {}

        A_PROJ, A_KV, A_Q, A_KT, A_QT, A_QPT, A_KPT, A_SQ, A_AT, A_TR, AB = (
            0, 1408, 5504, 7040, 9088, 11136, 12160, 12416, 13440, 16128, 17528)
        A_IND = 0
        projS = view(A_PROJ, 1408, "p (t n) -> p t n", t=2)
        kvtok = view(A_KV, 4096, "p (t h n) -> p t h n", t=2, h=8)
        qtoks = [view(A_Q + 768 * i, 768, "p (t h n) -> p t h n", t=2, h=2) for i in range(2)]
        kT = view(A_KT, 2048, "p (h n) -> p h n", h=8)
        qT = view(A_QT, 2048, "p (h n) -> p h n", h=8)
        qpT = view(A_QPT, 1024, "p (h n) -> p h n", h=4)
        kpT = view(A_KPT, 256)
        sq = [view(A_SQ + 512 * i, 512) for i in range(2)]
        rt = view(A_TR, 448)

        table("silu_and_others")
        posf = keep_tile(2)
        tp = copy(posf, posT, IN)
        ang, nn, rr, sn, cs, s2 = (rt[:, 64 * i:64 * i + 64].rearrange("p (t n) -> p t n", t=2) for i in range(6))
        for t in range(2):
            tk = ts(ang[:, t, :], RW("invf"), posf[:, t:t + 1], None, ALU.mult, None, tp)
        MAGIC = 12582912.0
        C1 = 6.28125
        C2 = float(np.float32(2 * np.pi - C1))
        C3 = float(2 * np.pi - C1 - C2)
        tk = ts(nn, ang, float(1 / (2 * np.pi)), MAGIC, ALU.mult, ALU.add, tk)
        tk = ts(nn, nn, MAGIC, None, ALU.subtract, None, tk)
        tk = stt(rr, nn, -C1, ang, ALU.mult, ALU.add, tk)
        tk = stt(rr, nn, -C2, rr, ALU.mult, ALU.add, tk)
        tk = stt(rr, nn, -C3, rr, ALU.mult, ALU.add, tk)
        tk = ts(rr, rr, 3.1415925, -3.1415925, ALU.min, ALU.max, tk)
        tk = act(sn, rr, ACT.Sin, tk)
        tk2 = act(s2, rr, ACT.Sin, scale=0.5)
        tk = tt(s2, s2, s2, ALU.mult, tk2)
        tk = ts(cs, s2, -2.0, 1.0, ALU.mult, ALU.add, tk)
        table("natural_log_exp_and_others")
        rope_t = {}
        for n_, nm in enumerate(("ropeq", "ropek")):
            for j, (src, half) in enumerate(((cs, 0), (sn, 1), (cs, 1), (sn, 0))):
                d = view(A_TR + 448 + 64 * (4 * n_ + j), 64, "p (t n) -> p t n", t=2)
                g = bc(RW(nm)[:, 32 * half:32 * half + 32].unsqueeze(1), 1, 2)
                tk = tt(d, src, g, ALU.mult, tk)
                rope_t[nm, j] = d
        t_rope = tk

        def rope(nm, src, dst, t, nh, tmp, *tokens):
            x1, x2 = src[:, :, 0:32], src[:, :, 32:64]
            f = [bc(rope_t[nm, j][:, t, :].unsqueeze(1), 1, nh) for j in range(4)]
            ta = tmp.rearrange("p (a h n) -> p a h n", a=4, h=nh)
            tt(ta[:, 0], x1, f[0], ALU.mult, t_rope, *tokens)
            tt(ta[:, 1], x2, f[1], ALU.mult)
            tt(ta[:, 2], x2, f[2], ALU.mult)
            tk = tt(ta[:, 3], x1, f[3], ALU.mult)
            tt(dst[:, :, 0:32], ta[:, 0], ta[:, 1], ALU.subtract, tk)
            return tt(dst[:, :, 32:64], ta[:, 2], ta[:, 3], ALU.add)

        (xT,) = transposed([INX, INX], ("attn0", xh, xl))
        ss, tk = mean_squares(view(A_QT, 1024), INX)
        r0, tr0 = rsqrt(ss, 2, 1.0 / D, tk, out_=keep_tile(2))
        t_in = {}
        for c_ in range(4):
            c, wh, wl, tk = use()
            for t in range(2):
                s = slice(128 * t, 128 * t + 128)
                for ch, (a, n) in enumerate(((0, 512), (512, 192))):
                    for k in range(2):
                        tok = mm3(P[2 * t + ch][:, 0:n], xh[:, 2 * c_ + k, s], xl[:, 2 * c_ + k, s],
                                  wh[:, k, a:a + n], wl[:, k, a:a + n], c_ == 0 and k == 0, tk, xT[c_],
                                  sig=(k == 1))
                    t_in[t, ch] = tok
            release(c, tok)
        t_x = tok
        ssm = small_tile(6)
        for t in range(2):
            for ch, (a, n) in enumerate(((0, 512), (512, 192))):
                tk = act(projS[:, t, a:a + n], P[2 * t + ch][:, 0:n], ACT.Copy, t_in[t, ch], tr0, scale=r0[:, t:t + 1])
                pfree[2 * t + ch] = [tk]
        t_ps = tk
        for j in (3, 4, 0, 1, 2):
            b = bank()
            for t in range(2):
                tk = pe_turn(P[b][:, 128 * t:128 * t + 128], projS[:, t, 128 * j:128 * j + 128], t_ps, pfree[b],
                             sig=(t == 1))
            g = C("qa", j) if j < 3 else C("kva", j - 3)
            ta = act(xh[:, j, :], P[b][:, 0:256], ACT.Copy, tk, t_x, scale=g)
            tv = stt(xl[:, j, :], P[b][:, 0:256], g, xh[:, j, :], ALU.mult, ALU.subtract, ta, t_x)
            pfree[b] = [ta, tv]
        cT = tv
        for t in range(2):
            for i, (a, n) in enumerate(((0, 384), (384, 256), (640, 64))):
                tk = act(sq[(3 * t + i) % 2][:, 0:n], projS[:, t, a:a + n], ACT.Square, t_ps,
                         accum=ssm[:, 2 * i + t:2 * i + t + 1])
                t_ps = tk
        ssn = small_tile(6)
        for i, n in enumerate((384, 256, 64)):
            t2 = ts(ssn[:, 2 * i:2 * i + 2], ssm[:, 2 * i:2 * i + 2], 1.0 / n, None, ALU.mult, None, tk)
        rm, trm = rsqrt(ssn, 6, 1.0, t2, out_=keep_tile(6))
        gk = keep_tile(1)
        t_gk = tt(gk, C("mlaqn"), C("mlakn"), ALU.mult, IN)
        sq_used = {}
        sqi = [0]

        def head_rstd(srcs, nh, n, tok, sqs):
            o = small_tile(nh * len(srcs))
            for i, src in enumerate(srcs):
                q_ = sqi[0] % len(sqs)
                sqi[0] += 1
                s_ = sqs[q_][:, 0:nh * n].rearrange("p (h n) -> p h n", h=nh)
                ta = act(s_, src, ACT.Square, tok, sq_used.get(q_))
                tv = op("dve", lambda e, i=i, s_=s_: e.reduce_sum(o[:, nh * i:nh * i + nh], s_, AX), ta)
                sq_used[q_] = tv
            return rsqrt(o, nh * len(srcs), 1.0 / n, tv)

        def heads_T(dst, src, h0, gain, tok, *tokens):
            b = bank()
            for j in range(2):
                for t in range(2):
                    tk = pe_turn(P[b][:, 256 * j + 128 * t:256 * j + 128 * t + 128], src(t, h0 + j), tok, pfree[b],
                                 sig=(j == 1 and t == 1))
            d = dst[:, h0:h0 + 2, :]
            i = P[b][:, :].rearrange("p (h n) -> p h n", h=2)
            if gain is None:
                tk = act(d, i, ACT.Copy, tk, *tokens)
            else:
                tk = act(d, i, ACT.Copy, tk, *tokens, scale=gain)
            pfree[b] = [tk]
            return tk

        kv_t, q_t, kT_t, t_kp = {}, {}, {}, []

        def mla_kv(g):
            c, wh, wl, tk = use()
            for ch in range(2):
                for t in range(2):
                    b = 2 * ch + t
                    for k in range(2):
                        s = slice(128 * t, 128 * t + 128)
                        tok = mm3(P[b][:, :], xh[:, 3 + k, s], xl[:, 3 + k, s], wh[:, k, 512 * ch:512 * ch + 512],
                                  wl[:, k, 512 * ch:512 * ch + 512], k == 0, tk, cT, pfree[b], sig=(k == 1))
                    h0 = 4 * g + 2 * ch
                    ta = act(kvtok[:, t, h0:h0 + 2, :], P[b][:, :].rearrange("p (h n) -> p h n", h=2), ACT.Copy, tok, trm,
                             scale=rm[:, 2 + t:3 + t])
                    pfree[b] = [ta]
                    if ch == 1 and t == 1:
                        release(c, tok)
                        kv_t[g] = ta
                    yield True

        def mla_q(i):
            c, wh, wl, tk = use()
            for t in range(2):
                b = t + 2 * (i % 2)
                s = slice(128 * t, 128 * t + 128)
                for k in range(3):
                    tok = mm3(P[b][:, 0:384], xh[:, k, s], xl[:, k, s], wh[:, k, :], wl[:, k, :], k == 0, tk, cT,
                              pfree[b], sig=(k == 2))
                ta = act(qtoks[i % 2][:, t], P[b][:, 0:384].rearrange("p (h n) -> p h n", h=2), ACT.Copy,
                         tok, trm, qk_used.get(("q", i % 2)), scale=rm[:, t:t + 1])
                pfree[b] = [ta]
                if t == 1:
                    release(c, tok)
                    q_t[i] = ta
                yield True

        def mla_kpe():
            kp = view(A_AT, 256, "p (t n) -> p t n", t=2)
            kn = view(A_AT + 256, 128, "p (t n) -> p t n", t=2)
            for t in range(2):
                tk = ts(kn[:, t, :], projS[:, t, 640:704], rm[:, 4 + t:5 + t], None, ALU.mult, None, trm)
            for t in range(2):
                tk = rope("ropek", kn[:, t:t + 1, :], kp[:, t:t + 1, 0:64], t, 1, view(A_AT + 384 + 128 * t, 128), tk)
            tk = copy(kp[:, :, 64:128], kp[:, :, 0:64], tk)
            yield True
            b = bank()
            for t in range(2):
                tk = pe_turn(P[b][:, 128 * t:128 * t + 128], kp[:, t, :], tk, pfree[b], sig=(t == 1))
            tk = copy(kpT, P[b][:, 0:256], tk)
            pfree[b] = [tk]
            t_kp.append(tk)
            yield True

        def mla_kpost(g):
            while g not in kv_t:
                yield False
            ks = [kvtok[:, t, 4 * g:4 * g + 4, 0:128] for t in range(2)]
            r_, tr = head_rstd(ks, 4, 128, kv_t[g], sq)
            for t in range(2):
                tkk = tt(ks[t], ks[t], bc(r_[:, 4 * t:4 * t + 4].unsqueeze(2), 2, 128), ALU.mult, tr)
            yield True
            for h0 in (4 * g, 4 * g + 2):
                kT_t[h0] = heads_T(kT, lambda t, h: kvtok[:, t, h, 0:128], h0, gk, tkk, t_gk)
                yield True

        def mla_qpost(i):
            while i not in q_t or 2 * i not in kT_t or not t_kp:
                yield False
            h0 = 2 * i
            qt = qtoks[i % 2]
            qn = [qt[:, t, :, 0:128] for t in range(2)]
            qp = [qt[:, t, :, 128:192] for t in range(2)]
            r_, tr = head_rstd(qn, 2, 128, q_t[i], sq)
            r2_, tr2 = head_rstd(qp, 2, 64, q_t[i], sq)
            for t in range(2):
                tq = tt(qn[t], qn[t], bc(r_[:, 2 * t:2 * t + 2].unsqueeze(2), 2, 128), ALU.mult, tr)
            yield True
            for t in range(2):
                tp_ = tt(qp[t], qp[t], bc(r2_[:, 2 * t:2 * t + 2].unsqueeze(2), 2, 64), ALU.mult, tr2)
            for t in range(2):
                tp_ = rope("ropeq", qp[t], qp[t], t, 2, view(A_TR + 1016, 256), tp_)
            pr = view(A_TR, 256, "p (t n) -> p t n", t=2)
            for t in range(2):
                tp_ = copy(pr[:, t, :].rearrange("p (h n) -> p h n", h=2), qp[t], tp_, qk_used.get("pr"))
            tkq = heads_T(qT, lambda t, h: qt[:, t, h - h0, 0:128], h0, None, tq)
            yield True
            b = bank()
            for t in range(2):
                tk = pe_turn(P[b][:, 128 * t:128 * t + 128], pr[:, t, :], tp_, pfree[b], sig=(t == 1))
            qk_used["pr"] = tk
            qk_used[("q", i % 2)] = [tk, tp_]
            tkp = act(qpT[:, i, :], P[b][:, 0:256], ACT.Copy, tk)
            pfree[b] = [tkp]
            ready[h0] = ready[h0 + 1] = [kT_t[h0], tkq, tkp, t_kp[0]]
            yield True

        def mla_extra(h):
            s = slice(64 * (h % 2), 64 * (h % 2) + 64)
            return qpT[s, h // 2, :], kpT[s, :]

        biasM = view(AB, 3072, "p (h n) -> p h n", h=8)
        biasdone = []

        def bias_steps():
            pq = view(A_IND + 1024, 256)
            pkf = keep_bias[:, :]
            t1 = copy(pq, pqi, IN, trm, cT)
            t1 = ts(pq, pq, K("tb"), None, ALU.subtract, None, t1)
            t2 = copy(pkf, pki, IN)
            tb = pint[:, 0:48].bitcast(BF16).rearrange("p (a n) -> p a n", a=3)
            dd, de = pint[:, 64:96], pint[:, 96:128]
            tk = tt(dd, tab, tabs, ALU.subtract, IN, t1)
            tk = copy(tb[:, 0, :], dd, tk)
            tk = tt(de, dd, tb[:, 0, :], ALU.subtract, tk)
            tk = copy(tb[:, 1, :], de, tk)
            tk = tt(dd, de, tb[:, 1, :], ALU.subtract, tk)
            t_tb = copy(tb[:, 2, :], dd, tk)
            yield True
            ind = [view(A_IND + 512 * i, 512).bitcast(BF16).rearrange("p (g q) -> p g q", g=4) for i in range(2)]
            usedi = {}
            tis = {}

            def make(q_):
                a_ = bc(pq.unsqueeze(1), 1, 4)
                b_ = bc(pkf[:, 4 * q_:4 * q_ + 4].unsqueeze(2), 2, 256)
                tis[q_] = tt(ind[q_ % 2], a_, b_, ALU.is_ge, t1, t2, usedi.get(q_ % 2))

            make(0)
            yield True
            for q_ in range(16):
                iv = ind[q_ % 2]
                if q_ + 1 < 16:
                    make(q_ + 1)
                b = bank()
                for t in range(2):
                    nk = 2 + 2 * t
                    n = 8 * nk
                    for g_ in range(4):
                        for p_ in range(3):
                            a = 128 * t + n * g_
                            tk = mm(P[b][:, a:a + n], iv[0:32 * nk, g_, 128 * t:128 * t + 128], tb[0:32 * nk, p_, 0:n],
                                    p_ == 0, tis[q_], t_tb, pfree[b], sig=(t == 1 and g_ == 3 and p_ == 2))
                usedi[q_ % 2] = tk
                for t in range(2):
                    nk = 2 + 2 * t
                    base = 128 * t
                    d = biasM[:, :, base:base + 64 * nk].rearrange("p h (k g) -> p h k g", k=nk)[:, :, :, 4 * q_:4 * q_ + 4]
                    s_ = P[b][:, base:base + 32 * nk].rearrange("p (g k h) -> p h k g", g=4, k=nk)
                    m_ = K("mask")[:, base:base + 64 * nk].rearrange("p (k g) -> p k g", k=nk)[:, :, 4 * q_:4 * q_ + 4]
                    for k_ in range(nk):
                        tv = tt(d[:, :, k_], s_[:, :, k_], bc(m_[:, k_].unsqueeze(1), 1, 8), ALU.add, tk)
                pfree[b] = [tv]
                yield True
            biasdone.append(tv)

        keep_bias = sb("pkf", [128, 64])
        mla_main = chain(mla_kv(0), mla_q(0), mla_q(1), mla_kv(1), mla_q(2), mla_q(3), o_product())
        mla_post = chain(mla_kpe(), mla_kpost(0), mla_qpost(0), mla_qpost(1), mla_kpost(1), mla_qpost(2), mla_qpost(3))
        mla_attn = attention(range(8), lambda h: qT[:, h, :], lambda h: kT[:, h, :],
                             lambda h, t: kvtok[:, t, h, 128:256], float(1.0 / np.sqrt(192.0)),
                             lambda h: (K("mask"), IN), A_AT, keep_o, extra=mla_extra)

        def after_kpe(gen):
            while not t_kp:
                yield False
            yield from gen

        weave(mla_main, (mla_post, 1), (after_kpe(mla_attn), 2), (bias_steps(), 1))
        tX = residual(final)

        s_pr = sem("s_pr")

        def finish(tX):
            for t in range(2):
                dma(lambda e, t=t: e.dma_start(out[128 * t:128 * t + 128, :], X[:, t, :]), s_out, tX)
            wait("sp", [(s_out, 32)])

        def mlp(i, tX):
            F = stage()
            (xt,) = transposed(tX, (f"mlp{i}", xh, xl), free=F)
            ss, tk = mean_squares(view(4096, 1024), tX, F)
            m = small_tile(2)
            r2 = keep_tile(2)
            tk = ts(m, ss, 1.0 / D, EPS, ALU.mult, ALU.add, tk)
            tr2 = op("dve", lambda e: e.reciprocal(r2, m), tk, F)
            if i == 0:
                predf = view(6144, 896)
                dma(lambda e: e.dma_start(predf, A["c_pred"]), s_pr, F)
                copy(level_mask.rearrange("p l n -> p (l n)"), predf, (s_pr, 16))
            rel = [view(2048 * i_, 1024) for i_ in range(2)]
            sqr = [view(2048 * i_ + 1024, 1024) for i_ in range(2)]
            freed, used, hid, toks = {}, {}, {}, {}
            for g in range(9):
                if g < 8:
                    v = g % 2
                    mtok = {}
                    for _ in proj_w(4 + 2 * v, xh, xl, xt, mtok):
                        pass
                    tl_ = []
                    for half in range(2):
                        b = 4 + 2 * v + half
                        hs = slice(512 * half, 512 * half + 512)
                        os_ = slice(1024 * v + 512 * half, 1024 * v + 512 * half + 512)
                        ta = act(rel[v][:, hs], P[b][:, :], ACT.Relu, mtok[half], freed.get((v, half)), F)
                        pfree[b] = [ta]
                        ta = act(sqr[v][:, hs], rel[v][:, hs], ACT.Square, ta)
                        th = copy(oth[:, os_], sqr[v][:, hs], ta, used.get(v), F)
                        tv = tt(otl[:, os_], sqr[v][:, hs], oth[:, os_], ALU.subtract, th)
                        freed[(v, half)] = tv
                        tl_.append(tv)
                    hid[g] = tl_
                if g > 0:
                    v = (g - 1) % 2
                    f = lambda q, k, t, v=v: q[:, 1024 * v + 256 * k + 128 * t:1024 * v + 256 * k + 128 * t + 128]
                    for kk in range(2):
                        for _ in back(2 * kk, lambda k, t: f(oth, k, t), lambda k, t: f(otl, k, t), g == 1 and kk == 0,
                                      toks, hid[g - 1][kk], F):
                            pass
                    used[v] = toks[3]
            ring[0] = 4
            return residual(toks, (r2, tr2))

        if stop >= 2:
            tX = mlp(0, tX)

        def token_major(pair, dst, toks, scale, *tokens):
            for t in range(2):
                ta = act(dst(t), P[pair + t][:, :], ACT.Copy, toks[t], *tokens, scale=scale[:, t:t + 1])
                pfree[pair + t] = [ta]
            return ta

        def heads_main(g, which, pair, th, tl, xt, r, bufs, V, F):
            toks = {}
            yield from proj_x(pair, th, tl, xt, toks)
            if which == "v":
                evac[("v", g)] = token_major(pair, lambda t: V[:, t, 512 * g:512 * g + 512], toks, r[0], r[1], F)
            else:
                evac[(which, g)] = token_major(pair, lambda t: bufs[which][:, t, :], toks, r[0], r[1], F,
                                               qk_used.get(which))
            evac[("pe", which, g)] = toks[1]

        evac = {}

        def heads_post(g, which, bufs, qT_, kT_, gain, rq, sqs, F):
            while (which, g) not in evac:
                yield False
            buf = bufs[which]
            ta = evac[(which, g)]
            v4 = [buf[:, t, :].rearrange("p (h n) -> p h n", h=4) for t in range(2)]
            r_, tr_ = head_rstd(v4, 4, 128, ta, sqs)
            if which == "k":
                for t in range(2):
                    tk = tt(v4[t], v4[t], bc(r_[:, 4 * t:4 * t + 4].unsqueeze(2), 2, 128), ALU.mult, tr_)
            else:
                tk = ts(rq[:, :, 4 * g:4 * g + 4], r_.rearrange("p (t h) -> p t h", t=2), float(128 ** -0.5), None,
                        ALU.mult, None, tr_, F)
                ready[("rq", g)] = tk
            yield True
            for j in range(2):
                h0 = 4 * g + 2 * j
                src = lambda t, h: buf[:, t, 128 * (h - 4 * g):128 * (h - 4 * g) + 128]
                tk2 = heads_T(kT_ if which == "k" else qT_, src, h0, gain if which == "k" else None,
                              tk if which == "k" else ta, F)
                qk_used[which] = [(done["pe"], count["pe"]), tk2]
                ready[(which, h0)] = ready[(which, h0 + 1)] = tk2
                yield True

        def when_ready(g):
            for j in range(4):
                h = 4 * g + j
                while not all(x in ready for x in (("q", h), ("k", h), ("rq", g))) or ("v", g) not in evac:
                    yield False
                ready[h] = [ready[("q", h)], ready[("k", h)], evac[("v", g)]]
            yield True

        if stop >= 3:
            F = stage()
            evac.clear()
            V = view(0, 2048, "p (t n) -> p t n", t=2)
            kT = view(2048, 2048, "p (h n) -> p h n", h=8)
            qT = view(4096, 2048, "p (h n) -> p h n", h=8)
            bufs = {"q": view(6144, 1024, "p (t n) -> p t n", t=2), "k": view(7168, 1024, "p (t n) -> p t n", t=2)}
            sqs = [view(8192 + 512 * i, 512) for i in range(2)]
            rq = view(9216, 16, "p (t h) -> p t h", t=2)
            (xt,) = transposed(tX, ("attn1", xh, xl), free=F)
            ss, tk = mean_squares(view(10000, 1024), tX, F)
            r1 = rsqrt(ss, 2, 1.0 / D, tk, F, out_=keep_tile(2))
            gm = keep_tile(1)
            t_gm = tt(gm, C("mobaq"), C("mobak"), ALU.mult, IN, F)
            sq_used.clear()
            sq_used.update({0: F, 1: F})
            bufF = [F, t_gm]
            main = chain(*[heads_main(g, w_, 2 * (i_ % 2), xh, xl, xt, r1, bufs, V, bufF)
                           for i_, (g, w_) in enumerate([(g, w_) for g in range(2) for w_ in "qkv"])], o_product())
            post = chain(*[heads_post(g, w_, bufs, qT, kT, gm, rq, sqs, bufF) for g in range(2) for w_ in "qk"])
            gate = chain(when_ready(0), when_ready(1))
            attn = attention(range(8), lambda h: qT[:, h, :], lambda h: kT[:, h, :],
                             lambda h, t: V[:, t, 128 * h:128 * h + 128],
                             lambda h: ([rq[:, t, h:h + 1] for t in range(2)], ready[("rq", h // 4)]),
                             lambda h: (biasM[:, h, :], biasdone[0]), 11024, keep_o, after=F)
            weave(main, (post, 1), (gate, 1), (attn, 2))
            tX = residual(final)
        if stop >= 4:
            tX = mlp(1, tX)

        s_pn = sem("s_pn")
        npn = [0]

        def post_row(name, a, F):
            g = view(a, 1024)
            dma(lambda e: e.dma_start(g, bc(A[name].rearrange("(a d) -> a d", a=1), 0, 128)), s_pn, F)
            npn[0] += 16
            return g, (s_pn, npn[0])

        def post_norm(toks, grow, tg, a, F):
            ss = small_tile(4)
            for b in (0, 2, 1, 3):
                d = view(a + 512 * b, 512)
                tk = act(d, P[b][:, :], ACT.Square, toks[b], F, accum=ss[:, b:b + 1])
            s2_ = small_tile(2)
            sv = ss.rearrange("p (t c) -> p t c", t=2)
            tk = tt(s2_.unsqueeze(2), sv[:, :, 0:1], sv[:, :, 1:2], ALU.add, tk)
            r_, tr = rsqrt(s2_, 2, 1.0 / D, tk)
            res = []
            for ch in range(2):
                for b in (ch, 2 + ch):
                    d = view(a + 512 * b, 512)
                    tk = stt(d, P[b][:, :], r_[:, b // 2:b // 2 + 1], grow[:, 512 * ch:512 * ch + 512], ALU.mult,
                             ALU.mult, tr, tg)
                    pfree[b] = [tk]
                for b in (ch, 2 + ch):
                    xs = X[:, b // 2, 512 * ch:512 * ch + 512]
                    tk = tt(xs, xs, view(a + 512 * b, 512), ALU.add, tk)
                res.append(tk)
            return res

        def across(r, dst, tr, *tokens):
            b = bank()
            for t in range(2):
                tk = pe_turn(P[b][:, 128 * t:128 * t + 128], bc(r[:, t:t + 1], 1, 128), tr, IN, pfree[b], sig=(t == 1))
            tk = copy(dst, P[b][:, 0:256], tk, *tokens)
            pfree[b] = [tk]
            return tk

        if stop >= 5:
            F = stage()
            kS = view(0, 2048, "p (h n) -> p h n", h=8)
            qS = view(2048, 2048, "p (h n) -> p h n", h=8)
            BA = view(4096, 6144, "p (h n) -> p h n", h=8)
            Vt = view(10240, 2048, "p (t h n) -> p t h n", t=2, h=8)
            zT = view(12288, 2048, "p (h n) -> p h n", h=8)
            pre = [view(14336 + 512 * i, 512) for i in range(2)]
            vS = [view(15360 + 1024 * i, 1024, "p (h n) -> p h n", h=4) for i in range(2)]
            acc2 = [view(15360 + 512 * i, 512) for i in range(4)]
            Dt = [view(17408 + 768 * i, 768) for i in range(2)]
            sqp = [view(18944 + 256 * i, 256) for i in range(4)]
            rT = view(19968, 256)
            rbc = view(20224, 256)
            Ya = view(0, 4096, "p (g n) -> p g n", g=8)

            (xt,) = transposed(tX, ("gdnpre", xh, xl), free=F)
            ss, tk = mean_squares(view(0, 1024), tX, F)
            r1, tr1 = rsqrt(ss, 2, 1.0 / D, tk, F, out_=keep_tile(2))
            tok = proj_few(16, xh, xl, xt)
            t_rbc = across(r1, rbc, tr1, F)
            ab_ = keep_tile(32).rearrange("p (t n) -> p t n", t=2)
            for t in range(2):
                tab_ = ts(ab_[:, t, :], P[t][:, 0:16], r1[:, t:t + 1], None, ALU.mult, None, tok, tr1, F)
                pfree[t] = [tab_]
            conv_o = COLS["conv"][0]
            gt, preu, accu = {}, {}, {}
            cnt = {"pre": 0, "acc": 0}

            def gdn_proj(name, g, pair):
                toks = {}
                yield from proj_w(pair, xh, xl, xt, toks)
                gt[("p", name, g)] = (pair, toks)

            def gdn_conv(name, g):
                while ("p", name, g) not in gt:
                    yield False
                pair, toks = gt[("p", name, g)]
                for half in range(2):
                    b = pair + half
                    rb = bc(rbc.unsqueeze(1), 1, 2)
                    src = P[b][:, :].rearrange("p (m n) -> p m n", m=2)
                    if name == "z":
                        tk = tt(zT[:, 4 * g + 2 * half:4 * g + 2 * half + 2, :], src, rb, ALU.mult, toks[half], t_rbc, F)
                        pfree[b] = [tk]
                        gt[("z", g)] = tk
                        yield True
                        continue
                    i = cnt["pre"] % 2
                    cnt["pre"] += 1
                    px = pre[i].rearrange("p (m n) -> p m n", m=2)
                    t0 = tt(px, src, rb, ALU.mult, toks[half], t_rbc, preu.get(i), F)
                    pfree[b] = [t0]
                    if name == "v":
                        acc = vS[g][:, 2 * half:2 * half + 2, :]
                        free = vfree
                    else:
                        ai = cnt["acc"] % 4
                        cnt["acc"] += 1
                        acc = acc2[ai].rearrange("p (m n) -> p m n", m=2)
                        free = accu.get(ai)
                    m0 = {"q": 0, "k": 8, "v": 16}[name] + 4 * g + 2 * half
                    w = lambda j, tap: cols[:, conv_o + 4 * (m0 + j) + tap:conv_o + 4 * (m0 + j) + tap + 1]
                    tj = [act(acc[:, j, :], px[:, j, :], ACT.Copy, t0, free, F, scale=w(j, 3)) for j in range(2)]
                    for tap in (2, 1, 0):
                        d = 3 - tap
                        tj = [stt(acc[:, j, d:256], px[:, j, 0:256 - d], w(j, tap), acc[:, j, d:256], ALU.mult, ALU.add,
                                  tj[j]) for j in range(2)]
                    preu[i] = tj[1]
                    if name != "v":
                        dst = (kS if name == "k" else qS)[:, 4 * g + 2 * half:4 * g + 2 * half + 2, :]
                        ta = act(dst, acc, ACT.Silu, tj[1], F)
                        accu[ai] = ta
                        gt[(name, g)] = ta
                    else:
                        gt[("vc", g)] = tj[1]
                    yield True
                gt[("done", name, g)] = True

            def gdn_stats():
                for nm in "kq":
                    for g in range(2):
                        while ("done", nm, g) not in gt:
                            yield False
                b_ss = bank()
                o_ss = P[b_ss]
                spf = {}
                for h in range(8):
                    for qi, (src, nm) in enumerate(((kS, "k"), (qS, "q"))):
                        i = (2 * h + qi) % 4
                        tq = tt(sqp[i], src[:, h, :], src[:, h, :], ALU.mult, gt[(nm, h // 4)], spf.get(i), F,
                                eng="pool" if h % 2 else "dve")
                        for t in range(2):
                            a = 16 * t + 8 * qi + h
                            tk = mm(o_ss[:, a:a + 1], sqp[i][:, 128 * t:128 * t + 128], K("ones")[:, 0:1], True, tq,
                                    pfree[b_ss], sig=(t == 1))
                        spf[i] = tk
                sst = keep_tile(32)
                t_ss = ts(sst, o_ss[:, 0:32], EPS, None, ALU.add, None, tk, F)
                pfree[b_ss] = [t_ss]
                lnr = keep_tile(32)
                table("natural_log")
                t_ln = act(lnr, sst, ACT.Ln, t_ss, F)
                xx = keep_tile(32).rearrange("p (t n) -> p t n", t=2)
                tt(xx[:, :, 0:8], ab_[:, :, 0:8], bc(RW("dt").unsqueeze(1), 1, 2), ALU.add, IN, tab_, F)
                tk = ts(xx[:, :, 8:16], ab_[:, :, 8:16], -1.0, None, ALU.mult, None)
                e0, e1, e2, sp = (small_tile(32).rearrange("p (t n) -> p t n", t=2) for _ in range(4))
                ta = act(e0, xx, ACT.Abs, tk)
                table("natural_log_exp_and_others")
                ta = act(e1, e0, ACT.Exp, ta, scale=-1.0)
                ta = act(e2, e1, ACT.Ln, ta, bias=1.0)
                yield True
                tk = stt(sp, xx, 0.0, e2, ALU.max, ALU.add, ta)
                ea = keep_tile(8)
                ta = act(ea, RW("alog"), ACT.Exp, IN, F)
                gg = keep_tile(16).rearrange("p (t n) -> p t n", t=2)
                nb_ = keep_tile(16).rearrange("p (t n) -> p t n", t=2)
                tg_ = stt(gg, sp[:, :, 0:8], -1.0, bc(ea.unsqueeze(1), 1, 2), ALU.mult, ALU.mult, ta, tk)
                tn_ = ts(nb_, sp[:, :, 8:16], -1.0, None, ALU.mult, None, tk)
                gt["t_beta"] = act(beta, nb_, ACT.Exp, tn_, F)
                yield True
                b = bank()
                for t in range(2):
                    mm(P[b][:, 8 * t:8 * t + 8], K("tri"), gg[:, t, :], True, tg_, pfree[b])
                tk = mm(P[b][:, 16:24], K("ones"), gg[:, 0, :], True, sig=True)
                cum = keep_tile(24)
                t_cum = copy(cum, P[b][:, 0:24], tk)
                pfree[b] = [t_cum]
                cu = cum[:, 0:16].rearrange("p (t n) -> p t n", t=2)
                lr = lnr.rearrange("p (t n) -> p t n", t=2)
                cbv = cb[:, 0:16].rearrange("p (t n) -> p t n", t=2)
                rw = keep_tile(32).rearrange("p (t n) -> p t n", t=2)
                tmpc = keep_tile(32).rearrange("p (a t n) -> p a t n", a=2, t=2)
                tk = stt(cbv, lr[:, :, 0:8], -0.5, cu, ALU.mult, ALU.subtract, t_cum, t_ln, F)
                gt["t_cb"] = tt(cb[:, 16:24], cb[:, 0:8], cum[:, 16:24], ALU.add, tk)
                tk = tt(tmpc[:, 0], cu, nb_, ALU.add, tn_)
                tk2 = stt(tmpc[:, 1], lr[:, :, 8:16], -0.5, cu, ALU.mult, ALU.add)
                stt(rw[:, :, 0:8], lr[:, :, 0:8], -0.5, tmpc[:, 0], ALU.mult, ALU.add, tk)
                t_rw = ts(rw[:, :, 8:16], tmpc[:, 1], float(-0.5 * np.log(128.0)), None, ALU.add, None, tk2)
                yield True
                b = bank()
                for t in range(2):
                    tk = pe_turn(P[b][0:16, 128 * t:128 * t + 128], rw[:, t, :], t_rw, pfree[b], sig=(t == 1))
                t_rT = copy(rT[0:16, :], P[b][0:16, 0:256], tk, F)
                pfree[b] = [t_rT]
                yield True
                dused = {}
                for h in range(8):
                    rb = bank()
                    for j in range(2):
                        o = P[rb][:, :].rearrange("p (t a n) -> p t a n", t=2, a=2)[:, :, j, :]
                        l = bc(ident[0:16, h + 8 * j:h + 8 * j + 1], 1, 128)
                        tk = mm(o, l, rT[0:16, :].rearrange("p (t n) -> p t n", t=2), True, t_rT, pfree[rb], sig=(j == 1))
                    dt_ = Dt[h % 2]
                    ts(dt_[:, 0:256], P[rb][:, 0:256], cb[:, h:h + 1], 80.0, ALU.add, ALU.min, tk, gt["t_cb"],
                       dused.get(h % 2), F)
                    ts(dt_[:, 256:512], P[rb][:, 256:512], cb[:, 16 + h:17 + h], 80.0, ALU.add, ALU.min)
                    ta = ts(dt_[:, 512:768], P[rb][:, 256:512], cb[:, 8 + h:9 + h], 80.0, ALU.add, ALU.min)
                    pfree[rb] = [ta]
                    ta = act(dt_, dt_, ACT.Exp, ta)
                    for o_, strict in ((0, 1), (128, 0), (512, 1), (640, 0)):
                        d = dt_[:, o_:o_ + 128]
                        tp3 = op("pool", lambda e, d=d, s=strict: e.affine_select(
                            out=d, in_=d, pattern=[[1, 128]], compare_op=ALU.is_ge, fill=0.0, base=-s,
                            channel_multiplier=-1), ta)
                    if h == 7:
                        table("silu_and_others")
                        gt["silu2"] = True
                    yield True
                    kb = bank()
                    kb2 = bank()
                    for j, src in enumerate((kS, qS)):
                        o = P[kb][:, :].rearrange("p (t a n) -> p t a n", t=2, a=2)[:, :, j, :]
                        mm(o, kS[:, h, 0:128], src[:, h, :].rearrange("p (t n) -> p t n", t=2), True, pfree[kb])
                        tk = mm(P[kb2][:, 128 * j:128 * j + 128], kS[:, h, 128:256], src[:, h, 128:256], True, pfree[kb2],
                                sig=(j == 1))
                    t1 = stt(BA[:, h, 0:512], P[kb][:, :], -1.0, dt_[:, 0:512], ALU.mult, ALU.mult, tk, tp3, F)
                    t2 = stt(BA[:, h, 512:768], P[kb2][:, 0:256], -1.0, dt_[:, 512:768], ALU.mult, ALU.mult)
                    pfree[kb], pfree[kb2] = [t1], [t2]
                    dused[h % 2] = t2
                    gt[("B", h)] = t2
                    gt["kq"] = tk
                    yield True

            beta = keep_tile(16).rearrange("p (t n) -> p t n", t=2)
            cb = keep_tile(24)
            inv_used = {}

            def silus():
                for g in range(2):
                    while ("done", "v", g) not in gt or "silu2" not in gt:
                        yield False
                    tk = act(vS[g], vS[g], ACT.Silu, gt[("vc", g)])
                    yield True
                    for hp in range(2):
                        b = bank()
                        for j in range(2):
                            for t in range(2):
                                tp2 = pe_turn(P[b][:, 256 * j + 128 * t:256 * j + 128 * t + 128],
                                              vS[g][:, 2 * hp + j, 128 * t:128 * t + 128], tk, pfree[b],
                                              sig=(j == 1 and t == 1))
                        h0 = 4 * g + 2 * hp
                        src = P[b][:, :].rearrange("p (j t n) -> p j t n", j=2, t=2)
                        for t in range(2):
                            tv = tt(Vt[:, t, h0:h0 + 2, :], src[:, :, t, :], bc(beta[:, t, h0:h0 + 2].unsqueeze(2), 2, 128),
                                    ALU.mult, tp2, gt["t_beta"], F)
                        pfree[b] = [tv]
                        gt[("v", h0)] = gt[("v", h0 + 1)] = tv
                        yield True
                for g in range(2):
                    while ("z", g) not in gt or ("done", "z", g) not in gt:
                        yield False
                    gt[("zs", g)] = act(zT[:, 4 * g:4 * g + 4, :], zT[:, 4 * g:4 * g + 4, :], ACT.Silu, gt[("z", g)])
                    yield True
                table("natural_log_exp_and_others")
                gt["exp2"] = True

            def invert(g, sl):
                q = [x[:, 1024 * sl + 512 * i:1024 * sl + 512 * i + 512] for x in (oth, otl) for i in range(2)]
                Xb, Yb, Wb, Bb = q
                while ("B", 2 * g + 1) not in gt or (g >= 2 and ("Y", g - 2) not in gt):
                    yield False
                bt = [gt[("B", 2 * g)], gt[("B", 2 * g + 1)], F, inv_used.get(sl), t_idr]
                v4 = lambda a: a.rearrange("p (b n) -> p b n", b=4)
                blk = lambda i: BA[:, 2 * g + i // 2, 512 * (i % 2):512 * (i % 2) + 128]
                sl_ = lambda i: slice(128 * i, 128 * i + 128)
                idb = bc(ident.unsqueeze(1), 1, 4)
                src = BA[:, 2 * g:2 * g + 2, :].rearrange("p h (z n) -> p h z n", z=6)[:, :, 0:5:4, :]

                def level(l, *tokens):
                    m = bc(bc(level_mask[:, l, :].unsqueeze(1), 1, 2).unsqueeze(2), 2, 2)
                    return tt(Bb.rearrange("p (h z n) -> p h z n", h=2, z=2), src, m, ALU.mult, bt, tokens,
                              eng="pool" if l else "dve")

                tb_ = level(0)
                b = bank()
                mm(P[b][:, :], identr, bc(identr.unsqueeze(1), 1, 4), True, pfree[b])
                for i in range(4):
                    tk = mm(P[b][:, sl_(i)], Bb[:, sl_(i)], identr, False, tb_, sig=(i == 3))
                ty = tt(v4(Yb), idb, v4(Bb).bitcast(F32), ALU.add, tb_)
                tx = act(Xb, P[b][:, :], ACT.Copy, tk, bt)
                pfree[b] = [tx]
                tb_ = level(1, ty, tk)
                yield True
                for l in range(1, 7):
                    b = bank()
                    for i in range(4):
                        tk = mm(P[b][:, sl_(i)], Bb[:, sl_(i)], Xb[:, sl_(i)], True, tx, tb_, pfree[b], sig=(i == 3))
                    tw = act(Wb, P[b][:, :], ACT.Copy, tk, bt)
                    pfree[b] = [tw]
                    if l < 6:
                        tb_ = level(l + 1, tk)
                    yield True
                    b = bank()
                    mm(P[b][:, :], identr, Xb, True, tx, pfree[b])
                    for i in range(4):
                        tk2 = mm(P[b][:, sl_(i)], Yb[:, sl_(i)], Wb[:, sl_(i)], False, tw, ty, sig=(i == 3))
                    if l < 6:
                        b2 = bank()
                        mm(P[b2][:, :], identr, Yb, True, pfree[b2])
                        for i in range(4):
                            tk = mm(P[b2][:, sl_(i)], Wb[:, sl_(i)], Yb[:, sl_(i)], False, sig=(i == 3))
                    tx = copy(Xb, P[b][:, :], tk2)
                    pfree[b] = [tx]
                    if l < 6:
                        ty = act(Yb, P[b2][:, :], ACT.Copy, tk)
                        pfree[b2] = [ty]
                    yield True
                Xf = Xb.bitcast(F32)
                b = bank()
                for i in range(4):
                    tk = mm(P[b][:, sl_(i)], blk(i), Xf[:, sl_(i)], True, tx, pfree[b], sig=(i == 3))
                b2 = bank()
                for i in range(4):
                    tk2 = pe_turn(P[b2][:, sl_(i)], Xf[:, sl_(i)], pfree[b2], sig=(i == 3))
                Ys = Ya[:, g, :]
                tr = tt(v4(Ys), idb, v4(Xf), ALU.subtract, tk, gt["kq"])
                tr = tt(Wb, P[b][:, :], Ys, ALU.add, tr)
                pfree[b] = [tr]
                ty = act(Yb, P[b2][:, :], ACT.Copy, tk2)
                pfree[b2] = [ty]
                yield True
                b = bank()
                for i in range(4):
                    tk = mm(P[b][:, sl_(i)], Wb[:, sl_(i)], Yb[:, sl_(i)], True, tr, ty, pfree[b], sig=(i == 3))
                ty = tt(Ys, P[b][:, :], Yb.bitcast(F32), ALU.add, tk)
                pfree[b] = [ty]
                inv_used[sl] = [ty, tk]
                gt[("Y", g)] = ty
                yield True

            sol_used = {}
            Ub = [view(18944 + 256 * i, 256) for i in range(4)]

            def solve(h):
                g, i = h // 2, 2 * (h % 2)
                while ("Y", g) not in gt or ("v", h) not in gt:
                    yield False
                U = Ub[h % 4]
                us = sol_used.get(h % 4)
                Y0, Y1 = Ya[:, g, 128 * i:128 * i + 128], Ya[:, g, 128 * i + 128:128 * i + 256]
                b = bank()
                tk = mm(P[b][:, 0:128], Y0, Vt[:, 0, h, :], True, gt[("Y", g)], gt[("v", h)], pfree[b], sig=True)
                tu = act(U[:, 0:128], P[b][:, 0:128], ACT.Copy, tk, us, gt["kq"])
                pfree[b] = [tu]
                yield True
                b = bank()
                tk = mm(P[b][:, 0:128], BA[:, h, 256:384], U[:, 0:128], True, tu, pfree[b], sig=True)
                tr_ = tt(U[:, 128:256], P[b][:, 0:128], Vt[:, 1, h, :], ALU.add, tk, us)
                pfree[b] = [tr_]
                yield True
                b = bank()
                tk = mm(P[b][:, 0:128], Y1, U[:, 128:256], True, tr_, pfree[b], sig=True)
                tu1 = act(U[:, 128:256], P[b][:, 0:128], ACT.Copy, tk)
                pfree[b] = [tu1]
                yield True
                b = bank()
                mm(P[b][:, 0:128], BA[:, h, 128:256], U[:, 0:128], True, tu, pfree[b])
                mm(P[b][:, 128:256], BA[:, h, 384:512], U[:, 0:128], True)
                tk = mm(P[b][:, 128:256], BA[:, h, 640:768], U[:, 128:256], False, tu1, sig=True)
                sol_used[h % 4] = tk
                ta = act(BA[:, h, 0:256], P[b][:, 0:256], ACT.Copy, tk, scale=-1.0)
                pfree[b] = [ta]
                gt[("o", h)] = ta
                yield True

            xfree = []

            def gdn_out():
                for h0 in range(0, 8, 2):
                    while not (("o", h0) in gt and ("o", h0 + 1) in gt and "exp2" in gt):
                        yield False
                    tko = [gt[("o", h0)], gt[("o", h0 + 1)]]
                    i = h0 // 2 % 2
                    sq5 = pre[i].rearrange("p (h n) -> p h n", h=2)
                    ss4 = small_tile(4)
                    ta = act(sq5, BA[:, h0:h0 + 2, 0:256], ACT.Square, *tko, preu.get(i))
                    tv = op("dve", lambda e, ss4=ss4, i=i: e.reduce_sum(
                        ss4, pre[i].rearrange("p (a n) -> p a n", a=4), AX), ta)
                    preu[i] = tv
                    r4, tr4 = rsqrt(ss4, 4, 1.0 / 128, tv)
                    for j in range(2):
                        o2 = BA[:, h0 + j, 0:256].rearrange("p (t n) -> p t n", t=2)
                        tk = tt(o2, o2, bc(r4[:, 2 * j:2 * j + 2].unsqueeze(2), 2, 128), ALU.mult, tr4, ta)
                    yield True
                    b = bank()
                    for j in range(2):
                        for t in range(2):
                            tq = pe_turn(P[b][:, 256 * j + 128 * t:256 * j + 128 * t + 128],
                                         BA[:, h0 + j, 128 * t:128 * t + 128], tk, pfree[b], sig=(j == 1 and t == 1))
                    dz = zT[:, h0:h0 + 2, :]
                    tz = stt(dz, P[b][:, :].rearrange("p (h n) -> p h n", h=2), C("gdno"), dz, ALU.mult, ALU.mult, tq,
                             gt[("zs", 0)], gt[("zs", 1)])
                    pfree[b] = [tz]
                    ta = act(xh[:, h0:h0 + 2, :], dz, ACT.Copy, tz, xfree)
                    tv = tt(xl[:, h0:h0 + 2, :], dz, xh[:, h0:h0 + 2, :], ALU.subtract, ta, xfree)
                    ot_t[h0] = ot_t[h0 + 1] = [ta, tv]
                    yield True

            def mark():
                xfree.append((done["pe"], count["pe"]))
                return
                yield

            order = [("k", 0), ("q", 0), ("k", 1), ("q", 1), ("v", 0), ("v", 1), ("z", 0), ("z", 1)]
            vfree = []

            def vmark():
                while ("done", "q", 1) not in gt:
                    yield False
                vfree.extend([accu[i] for i in accu])

            main = chain(*[gdn_proj(nm, g, 2 * (i % 2)) for i, (nm, g) in enumerate(order)], mark(),
                         o_product(lambda k, t: xh[:, k, 128 * t:128 * t + 128],
                                   lambda k, t: xl[:, k, 128 * t:128 * t + 128]))
            convs = chain(*[gdn_conv(nm, g) for nm, g in order[:4]], vmark(), *[gdn_conv(nm, g) for nm, g in order[4:]])
            table("silu_and_others")
            s_main = [main, (convs, 1), (gdn_stats(), 1), (silus(), 1), (chain(invert(0, 0), invert(2, 0)), 1),
                      (chain(invert(1, 1), invert(3, 1)), 1),
                      (chain(*[solve(h) for h in (0, 4)]), 1), (chain(*[solve(h) for h in (1, 5)]), 1),
                      (chain(*[solve(h) for h in (2, 6)]), 1), (chain(*[solve(h) for h in (3, 7)]), 1),
                      (gdn_out(), 1)]
            weave(*s_main)
            gn, t_gn = post_row("gdn_post_norm_2", 17408, fence())
            tX = post_norm(final, gn, t_gn, 0, fence())

        if stop >= 6:
            F = stage()
            evac.clear()
            V = view(0, 2048, "p (t n) -> p t n", t=2)
            kT = view(2048, 2048, "p (h n) -> p h n", h=8)
            qT = view(4096, 2048, "p (h n) -> p h n", h=8)
            bufs = {"q": view(6144, 1024, "p (t n) -> p t n", t=2), "k": view(7168, 1024, "p (t n) -> p t n", t=2)}
            zT = view(8192, 2048, "p (h n) -> p h n", h=8)
            sqs = [view(10240 + 512 * i, 512) for i in range(2)]
            rq = view(11264, 16, "p (t h) -> p t h", t=2)
            bb = [view(13984 + 384 * i, 384) for i in range(4)]
            gz = [view(15520 + 256 * i, 256) for i in range(2)]
            cT_ = view(16032, 256)
            rbc = view(16288, 256)
            junk = view(18432, 1024)
            xh2 = oth[:, :].rearrange("p (k n) -> p k n", k=8)
            xl2 = otl[:, :].rearrange("p (k n) -> p k n", k=8)
            gnf, t_gnf = post_row("fox_post_norm_2", 17000, F)
            sq_used.clear()
            sq_used.update({0: F, 1: F})
            xt2, xt = transposed(tX, ("foxpre", xh2, xl2), ("kvn", xh, xl), free=F)
            ss, tk = mean_squares(junk, tX, F)
            r1 = rsqrt(ss, 2, 1.0 / D, tk, F, out_=keep_tile(2))
            gf = keep_tile(1)
            t_gf = tt(gf, C("foxq"), C("foxk"), ALU.mult, IN, F)
            fx, lf = (keep_tile(16).rearrange("p (t n) -> p t n", t=2) for _ in range(2))
            cc, cn = keep_tile(16), keep_tile(16)
            fs = {}

            def fox_z():
                for g in range(2):
                    toks = {}
                    yield from proj_w(2 * g, xh2, xl2, xt2, toks)
                    if g == 0:
                        fs["rbc"] = across(r1[0], rbc, r1[1], F)
                    for half in range(2):
                        b = 2 * g + half
                        d = zT[:, 4 * g + 2 * half:4 * g + 2 * half + 2, :]
                        tk = tt(d, P[b][:, :].rearrange("p (m n) -> p m n", m=2), bc(rbc.unsqueeze(1), 1, 2), ALU.mult,
                                toks[half], fs["rbc"], F)
                        pfree[b] = [tk]
                    fs["z", g] = tk
                    if g == 0:
                        table("silu_and_others")
                    tz = act(zT[:, 4 * g:4 * g + 4, :], zT[:, 4 * g:4 * g + 4, :], ACT.Silu, tk)
                    fs["zs"] = tz
                table("natural_log_exp_and_others")

            def fox_f():
                tok = proj_few(8, xh, xl, xt)
                e0, e1, e2 = (small_tile(16).rearrange("p (t n) -> p t n", t=2) for _ in range(3))
                for t in range(2):
                    tk = stt(fx[:, t, :], P[t][:, 0:8], r1[0][:, t:t + 1], RW("fbias"), ALU.mult, ALU.add, tok, IN, F)
                    pfree[t] = [tk]
                ta = act(e0, fx, ACT.Abs, tk)
                ta = act(e1, e0, ACT.Exp, ta, scale=-1.0)
                table("natural_log")
                ta = act(e2, e1, ACT.Ln, ta, bias=1.0)
                table("natural_log_exp_and_others")
                fs["lf"] = stt(lf, fx, 0.0, e2, ALU.min, ALU.subtract, ta)
                yield True

            def fox_c():
                while "lf" not in fs:
                    yield False
                b = bank()
                mm(P[b][:, 0:8], K("tri"), lf[:, 0, :], True, fs["lf"], pfree[b])
                mm(P[b][:, 8:16], K("ones"), lf[:, 0, :], True)
                tk = mm(P[b][:, 8:16], K("tri"), lf[:, 1, :], False, sig=True)
                copy(cc, P[b][:, 0:16], tk, F)
                t_c = ts(cn, P[b][:, 0:16], -1.0, None, ALU.mult, None, tk)
                pfree[b] = [t_c]
                yield True
                b = bank()
                for t in range(2):
                    tk = pe_turn(P[b][0:8, 128 * t:128 * t + 128], cn[:, 8 * t:8 * t + 8], t_c, pfree[b], sig=(t == 1))
                t_cT = copy(cT_[0:8, :], P[b][0:8, 0:256], tk, F)
                pfree[b] = [t_cT]
                fs["cT"] = t_cT
                yield True
                for h in range(8):
                    while h >= 4 and h - 4 not in fb_used:
                        yield False
                    b = bank()
                    tk = mm(P[b][:, 0:256], bc(ident[0:8, h:h + 1], 1, 128), cT_[0:8, :], True, t_cT, pfree[b], sig=True)
                    d = bb[h % 4]
                    m = K("mask")
                    stt(d[:, 0:128], P[b][:, 0:128], cc[:, h:h + 1], m[:, 0:128], ALU.add, ALU.add, tk, F, fb_used.get(h - 4))
                    tk = stt(d[:, 128:384], P[b][:, 0:256], cc[:, 8 + h:9 + h], m[:, 128:384], ALU.add, ALU.add)
                    pfree[b] = [tk]
                    fb[h] = (d, tk, lambda t_, h=h: fb_used.__setitem__(h, t_))
                    yield True

            fb, fb_used, gz_used = {}, {}, {}

            def fox_keep(h, b, tk):
                g_ = gz[h % 2]
                tv0 = tt(g_, P[b][:, 0:256], zT[:, h, :], ALU.mult, tk, fs["zs"], gz_used.get(h % 2), F)
                qd = evac[("pe", "q", 1)]
                ta = act(xh2[:, h, :], g_, ACT.Copy, tv0, qd)
                tv = tt(xl2[:, h, :], g_, xh2[:, h, :], ALU.subtract, ta, qd)
                gz_used[h % 2] = tv
                ot_t[h] = [ta, tv]
                return [tv0]

            bufF = [F, t_gf]
            seq = [(0, "k"), (0, "v"), (0, "q"), (1, "q"), (1, "k"), (1, "v")]
            main = chain(fox_z(), fox_f(), *[
                heads_main(g, w_, 2 * (i_ % 2), xh2 if w_ == "q" else xh, xl2 if w_ == "q" else xl,
                           xt2 if w_ == "q" else xt, r1, bufs, V, bufF) for i_, (g, w_) in enumerate(seq)], o_product())
            post = chain(*[heads_post(g, w_, bufs, qT, kT, gf, rq, sqs, bufF) for g, w_ in seq if w_ != "v"])

            def fox_gate():
                while ("pe", "q", 1) not in evac:
                    yield False
                yield from when_ready(0)
                yield from when_ready(1)

            attn = attention(range(8), lambda h: qT[:, h, :], lambda h: kT[:, h, :],
                             lambda h, t: V[:, t, 128 * h:128 * h + 128],
                             lambda h: ([rq[:, t, h:h + 1] for t in range(2)], ready[("rq", h // 4)]),
                             lambda h: fb[h], 11296, fox_keep, after=F)
            weave(main, (post, 1), (fox_c(), 1), (fox_gate(), 1), (attn, 2))
            tX = post_norm(final, gnf, t_gnf, 0, fence())
        finish(tX)

        block = ctx.enter_context(nc.Block())

        def play(eng, entries):
            for kind, a, b, *n in entries:
                if kind == "wait":
                    eng.wait_ge(a, b)
                else:
                    ins = a(eng)
                    if b is not None:
                        ins.then_inc(b, n[0])

        @block.sync
        def _(eng):
            play(eng, queue["sp"])

        @block.scalar
        def _(eng):
            play(eng, queue["act"])

        @block.vector
        def _(eng):
            play(eng, queue["dve"])

        @block.gpsimd
        def _(eng):
            play(eng, queue["pool"])

        @block.tensor
        def _(eng):
            play(eng, queue["pe"])


def constants():
    c = np.zeros((128, NCST), np.float32)
    p = np.arange(128)
    c[:, 0:128] = np.eye(128, dtype=np.float32)
    causal = np.where(p[None, :] <= p[:, None], 0.0, NEG)
    c[:, 128:256] = causal
    c[:, 384:512] = causal
    c[:, 512:640] = p[:, None] <= p[None, :]
    c[:, 640:768] = 1.0
    limits = [-1.0e9] + list(range(1, 17)) + [21, 27, 35, 46, 59, 77, 99, 128, 166, 216, 280, 363, 470, 609, 790]
    c[:, 768] = np.tile(np.array(limits, np.float32), 4)
    pred = np.zeros((128, 7, 128), np.float32)
    for l in range(7):
        s = 1 << l
        m = ((p[:, None] // (2 * s)) == (p[None, :] // (2 * s))) & ((p[:, None] // s) % 2 == 0) & ((p[None, :] // s) % 2 == 1)
        pred[:, l] = m
    return c, pred.reshape(128, 896)


def kernel(**inputs):
    import numpy as _np
    import concourse.bacc as _bacc
    from concourse import mybir as _mybir
    from concourse.bass_utils import run_bass_kernel_spmd as _run

    a = {k: _np.ascontiguousarray(v) for k, v in inputs.items()}
    col = lambda v: v.reshape(-1, 128).T
    cols = _np.ascontiguousarray(_np.concatenate([
        col(a["attn_norm"][0]), col(a["attn_norm"][1]), col(a["mlp_norm"][0]), col(a["mlp_norm"][1]),
        col(a["gdn_pre_norm_2"][0]), col(a["kv_norm_2"]), col(a["fox_pre_norm_2"][0]), col(a["mla_q_a_norm"][0]),
        col(a["mla_kv_a_norm"][0]), col(a["mla_q_nope_norm"][0]), col(a["mla_k_nope_norm"][0]),
        col(a["moba_q_norm"][0]), col(a["moba_k_norm"][0]), col(a["kv_k_norm_2"]), col(a["fox_q_norm_2"][0]),
        col(a["gdn_o_norm_2"][0]),
        a["gdn_conv_w_2"][0].reshape(4, 24, 128).transpose(2, 1, 0).reshape(128, 96)], axis=1))
    invf = _np.float32(10000.0) ** (-_np.arange(0, 64, 2, dtype=_np.float32) / _np.float32(64))
    rows = _np.concatenate([a["mla_q_rope_norm"][0], a["mla_k_rope_norm"][0], a["gdn_a_log_2"][0],
                            a["gdn_dt_bias_2"][0], a["kv_forget_bias_2"], invf.astype(_np.float32)])
    cst, pred = constants()
    arrays = {
        "x": a["x"][0], "positions": a["positions"], "rel_bias_table": a["rel_bias_table"],
        "mla_w_in": a["mla_w_in"][0], "mla_w_uq": a["mla_w_uq"][0], "mla_w_ukv": a["mla_w_ukv"][0],
        "mla_w_o": a["mla_w_o"][0], "moba_w_qkv": a["moba_w_qkv"][0], "moba_w_o": a["moba_w_o"][0],
        "mlp_w_in": a["mlp_w_in"], "mlp_w_out": a["mlp_w_out"], "gdn_w_in": a["gdn_w_in_2"][0],
        "gdn_w_out": a["gdn_w_out_2"][0], "kv_w": a["kv_w_2"], "fox_w_in": a["fox_w_in_2"][0],
        "fox_w_out": a["fox_w_out_2"][0], "gdn_post_norm_2": a["gdn_post_norm_2"][0],
        "fox_post_norm_2": a["fox_post_norm_2"][0],
        "c_cols": cols, "c_rows": rows, "c_cst": cst, "c_pred": pred,
        "c_posT": _np.ascontiguousarray(a["positions"].reshape(2, 128).T),
    }
    arrays = {k + "_dram": _np.ascontiguousarray(v) for k, v in arrays.items()}
    nc = _bacc.Bacc("TRN2", target_bir_lowering=False, num_devices=1)
    aps = {k[:-5]: nc.dram_tensor(k, v.shape, _mybir.dt.from_np(v.dtype), kind="ExternalInput").ap()
           for k, v in arrays.items()}
    out = nc.dram_tensor("out_dram", (256, 1024), _mybir.dt.float32, kind="ExternalOutput").ap()
    bass_two_blocks(nc, aps, out)
    r = _run(nc, [arrays], core_ids=[0])
    return r.results[0]["out_dram"].reshape(1, 256, 1024)
```

```python
import numpy as np
import concourse.bass as bass
import concourse.mybir as mybir
from contextlib import ExitStack

F32 = mybir.dt.float32
F32R = mybir.dt.float32r
BF16 = mybir.dt.bfloat16
I32 = mybir.dt.int32
ALU = mybir.AluOpType
ACT = mybir.ActivationFunctionType
AX = mybir.AxisListType.X

T = 256
D = 1024
NEG = -1.0e30
EPS = 1e-6
RAW = 3
SPLIT = 3
CH = 2048

COLS = {}
_at = 0
for _n, _w in (("attn0", 8), ("attn1", 8), ("mlp0", 8), ("mlp1", 8), ("gdnpre", 8), ("kvn", 8), ("foxpre", 8),
               ("qa", 3), ("kva", 2), ("mlaqn", 1), ("mlakn", 1), ("mobaq", 1), ("mobak", 1), ("foxk", 1), ("foxq", 1),
               ("gdno", 1), ("conv", 96)):
    COLS[_n] = (_at, _w)
    _at += _w
NCOLS = _at
ROWS = {"ropeq": (0, 64), "ropek": (64, 64), "alog": (128, 8), "dt": (136, 8), "fbias": (144, 8), "invf": (152, 32)}
NROWS = 184
CST = {"ident": (0, 128), "mask": (128, 384), "tri": (512, 128), "ones": (640, 128), "tb": (768, 1),
       "negid": (769, 128)}
NCST = 897


def bc(ap, dim, n):
    shape = list(ap.shape)
    shape[dim] = n
    return ap.broadcast_to(shape)


def bass_two_blocks(nc, A, out, stop=99):
    ctx = ExitStack()
    with ctx:
        def sb(name, shape, dt=F32):
            return ctx.enter_context(nc.sbuf_tensor(name, shape, dt))

        def sem(name):
            return ctx.enter_context(nc.semaphore(name))

        queue = {e: [] for e in ("pe", "act", "dve", "pool", "sp")}
        done = {e: sem("s_" + e) for e in ("pe", "act", "dve", "pool")}
        count = {e: 0 for e in done}
        waited = {}

        clock = {e: 0.0 for e in queue}
        when = {}

        def eta(*tokens):
            m = 0.0
            for t in tokens:
                if t is None:
                    continue
                if len(t) == 2 and isinstance(t[1], int):
                    m = max(m, when.get((id(t[0]), t[1]), 0.0))
                else:
                    m = max(m, eta(*t))
            return m

        def width(a):
            n = 1
            for d in list(a.shape)[1:]:
                n *= d
            return n

        def wait(eng, tokens):
            for t in tokens:
                if t is None:
                    continue
                if not (len(t) == 2 and isinstance(t[1], int)):
                    wait(eng, t)
                    continue
                s, v = t
                if waited.get((eng, id(s)), 0) < v:
                    waited[(eng, id(s))] = v
                    queue[eng].append(("wait", s, v))

        last = [0.0]

        def op(eng, fn, *tokens, sig=True, cost=200.0):
            clock[eng] = max(clock[eng], eta(*tokens)) + cost
            wait(eng, tokens)
            if sig:
                count[eng] += 1
                last[0] = when[id(done[eng]), count[eng]] = clock[eng] + 60.0 + (150.0 if eng == "act" else 40.0)
                queue[eng].append(("run", fn, done[eng], 1))
                return (done[eng], count[eng])
            queue[eng].append(("run", fn, None, 0))
            return None

        arrived = {}

        def dma(fn, s, *tokens, cost=300.0):
            wait("sp", tokens)
            clock["sp"] = max(clock["sp"], eta(*tokens)) + cost
            arrived[id(s)] = arrived.get(id(s), 0) + 16
            when[id(s), arrived[id(s)]] = clock["sp"] + 2000.0
            queue["sp"].append(("run", fn, s, 16))

        def act(o, i, func, *tokens, bias=0.0, scale=1.0, accum=None):
            return op("act", lambda e: e.activation(o, i, func, bias=bias, scale=scale, accum_out=accum)
                      if accum is not None else e.activation(o, i, func, bias=bias, scale=scale), *tokens, cost=75 + 0.83 * width(i))

        def table(name):
            queue["act"].append(("run", lambda e: e.preload_act_table_set(name), None, 0))

        def tt(o, a, b, f, *tokens, eng="dve"):
            return op(eng, lambda e: e.tensor_tensor(o, a, b, f), *tokens,
                      cost=85 + (1.04 if eng == "dve" else 2.4) * width(o))

        def ts(o, a, s1, s2, f1, f2, *tokens, eng="dve"):
            return op(eng, lambda e: e.tensor_scalar(o, a, s1, s2, f1, f2) if f2 is not None
                      else e.tensor_scalar(o, a, s1, None, f1), *tokens, cost=85 + 0.8 * width(o))

        def stt(o, a, s, b, f1, f2, *tokens):
            return op("dve", lambda e: e.scalar_tensor_tensor(out=o, in0=a, scalar=s, in1=b, op0=f1, op1=f2), *tokens,
                      cost=85 + 1.04 * width(o))

        def copy(o, a, *tokens, eng="dve"):
            return op(eng, lambda e: e.tensor_copy(o, a), *tokens,
                      cost=85 + (0.8 if eng == "dve" else 2.4) * width(o))

        def mm(o, l, r, start, *tokens, sig=False):
            return op("pe", lambda e: e.matmul(o, l, r, start=start, stop=True, skip_group_check=True), *tokens, sig=sig,
                      cost=width(r) / 2.4 * (1 if r.dtype == F32R or r.dtype == BF16 else 4))

        def mm3(o, lh, ll, rh, rl, start, *tokens, sig=False):
            mm(o, lh, rh, start, *tokens)
            mm(o, lh, rl, False)
            return mm(o, ll, rh, False, sig=sig)

        cst = sb("cst", [128, NCST])
        cols = sb("cols", [128, NCOLS])
        rows = sb("rows", [128, NROWS])
        level_mask = sb("level_mask", [128, 7, 128], BF16)[:, :, :]
        identr = sb("identr", [128, 128], F32R)[:, :]
        X = sb("X", [128, 2, D])
        xh = sb("xh", [128, 8, T], F32R)
        xl = sb("xl", [128, 8, T], F32R)
        raw = [sb(f"raw{i}", [128, CH]) for i in range(RAW)]
        whi = [sb(f"whi{i}", [128, CH], F32R) for i in range(SPLIT)]
        wlo = [sb(f"wlo{i}", [128, CH], F32R) for i in range(SPLIT)]
        oth = sb("oth", [128, 2048], F32R)
        otl = sb("otl", [128, 2048], F32R)
        st = sb("st", [128, 1024])
        pint = sb("pint", [128, 384])
        AR = 20600
        arena = sb("arena", [128, AR])

        P = [ctx.enter_context(nc.psum_tensor(f"ps{i}", [128, 512], F32)) for i in range(8)]
        pfree = [[] for _ in range(8)]
        ring = [4]

        spare = [4, 5, 6, 7]

        def bank():
            if len(spare) == 4:
                b = ring[0]
                ring[0] = 4 + (b - 3) % 4
                return b
            b = min((x for x in spare if x != ring[0]), key=lambda x: eta(pfree[x]))
            ring[0] = b
            return b

        def C(name, j=None):
            a, w = COLS[name]
            return cols[:, a:a + w] if j is None else cols[:, a + j:a + j + 1]

        def K(name):
            a, w = CST[name]
            return cst[:, a:a + w]

        def RW(name):
            a, w = ROWS[name]
            return rows[:, a:a + w]

        ident = K("ident")

        s_in = sem("s_in")
        s_x = sem("s_x")
        s_out = sem("s_out")
        n_in = [0]

        def small(o, i):
            dma(lambda e: e.dma_start(o, i), s_in)
            n_in[0] += 16

        dma(lambda e: e.dma_start(X[:, :, :], A["x"].rearrange("(t p) d -> p t d", p=128)), s_x)
        dma(lambda e: e.dma_start(cst[:, :], A["c_cst"]), s_x)
        dma(lambda e: e.dma_start(cols[:, :], A["c_cols"]), s_x)
        INX = (s_x, 48)
        posT = st[:, 1020:1022].bitcast(I32)
        pqi = pint[:, 0:256].bitcast(I32)
        pki = pint[:, 256:320].bitcast(I32)
        tab = pint[:, 320:352]
        tabs = pint[:, 352:384]
        z0 = op("dve", lambda e: e.memset(pint[:, 320:384], 0.0))
        t_idr = op("dve", lambda e: e.tensor_copy(identr, ident), INX)

        specs = []

        def add(src, a, b):
            specs.append((src, a, b))
            return len(specs) - 1

        def kslab(w, k0, nk, c0, nc_):
            return add(w[128 * k0:128 * (k0 + nk), c0:c0 + nc_].rearrange("(k p) n -> p k n", p=128), nk, nc_)

        def columns(w, *starts):
            for c0 in starts:
                for hk in range(2):
                    kslab(w, 4 * hk, 4, c0, 512)

        def down(w):
            for k in range(0, 8, 2):
                kslab(w, k, 2, 0, 1024)

        for k in range(0, 8, 2):
            kslab(A["mla_w_in"], k, 2, 0, 704)
        for g in range(2):
            kslab(A["mla_w_ukv"], 0, 2, 1024 * g, 1024)
            for i in range(2):
                kslab(A["mla_w_uq"], 0, 3, 768 * g + 384 * i, 384)
        down(A["mla_w_o"])

        def mlp_specs(i):
            for g in range(9):
                if g < 8:
                    columns(A["mlp_w_in"][i], 512 * g)
                if g > 0:
                    for k in range(4 * (g - 1), 4 * g, 2):
                        kslab(A["mlp_w_out"][i], k, 2, 0, 1024)

        mlp_specs(0)
        columns(A["moba_w_qkv"], 0, 1024, 2048, 512, 1536, 2560)
        down(A["moba_w_o"])
        mlp_specs(1)
        kslab(A["gdn_w_in"], 0, 8, 4096, 16)
        columns(A["gdn_w_in"], 1024, 0, 1536, 512, 2048, 2560, 3072, 3584)
        down(A["gdn_w_out"])
        columns(A["fox_w_in"], 1024, 1536)
        kslab(A["kv_w"], 0, 8, 2048, 8)
        columns(A["kv_w"], 0, 1024)
        columns(A["fox_w_in"], 0, 512)
        columns(A["kv_w"], 512, 1536)
        down(A["fox_w_out"])

        s_raw = [sem(f"s_raw{i}") for i in range(RAW)]
        loaded = [0]
        nsplit = [0]
        split_at = {}
        released = {}

        def load():
            c = loaded[0]
            if c >= len(specs):
                return
            loaded[0] += 1
            src, a, b = specs[c]
            dst = raw[c % RAW][:, 0:a * b].rearrange("p (k n) -> p k n", k=a)
            dma(lambda e: e.dma_start(dst, src), s_raw[c % RAW], *(split_at[c - RAW] if c >= RAW else ()),
                cost=1.45 * a * b)

        def split():
            c = nsplit[0]
            if c >= len(specs):
                return
            nsplit[0] += 1
            if loaded[0] <= c:
                load()
            _, a, b = specs[c]
            n = a * b
            r, h, l = raw[c % RAW][:, 0:n], whi[c % SPLIT][:, 0:n], wlo[c % SPLIT][:, 0:n]
            free = released.get(c - SPLIT)
            t1 = op("act", lambda e: e.activation(h, r, ACT.Copy), (s_raw[c % RAW], 16 * (c // RAW + 1)), free,
                    cost=75 + 0.83 * n)
            t2 = tt(l, r, h, ALU.subtract, t1, free, eng="dve" if eager[0] or c % 2 or n < CH else "pool")
            split_at[c] = (t1, t2)
            load()

        for _ in range(RAW):
            load()
        small(posT, A["c_posT"])
        small(rows[:, :], bc(A["c_rows"].rearrange("(a d) -> a d", a=1), 0, 128))
        small(pqi, bc(A["positions"], 0, 128))
        for kk in range(4):
            small(pki[32 * kk:32 * kk + 32, :], bc(A["positions"][:, 64 * kk:64 * kk + 64], 0, 32))
        wait("sp", [z0])
        for kk in range(4):
            small(tab[32 * kk:32 * kk + 32, 8 * kk:8 * kk + 8], A["rel_bias_table"])
            small(tabs[32 * kk + 1:32 * kk + 32, 8 * kk:8 * kk + 8], A["rel_bias_table"][0:31, :])
        IN = (s_in, n_in[0])
        cur = [-1]

        eager = [True]

        def pump(now):
            while nsplit[0] < min(cur[0] + 1 + SPLIT, len(specs)):
                c = nsplit[0]
                free = released.get(c - SPLIT)
                if c >= SPLIT and free is None or eta((s_raw[c % RAW], 16 * (c // RAW + 1)), free) > now:
                    break
                split()

        def next_chunk():
            c = cur[0] + 1
            return eta(split_at[c]) if c in split_at else 0.0

        def use():
            cur[0] += 1
            c = cur[0]
            top = min(c + (SPLIT if eager[0] else 1), len(specs))
            while nsplit[0] < top and (nsplit[0] - SPLIT < 0 or (nsplit[0] - SPLIT) in released):
                split()
            _, a, b = specs[c]
            v = [w[c % SPLIT][:, 0:a * b].rearrange("p (k n) -> p k n", k=a) for w in (whi, wlo)]
            return c, v[0], v[1], split_at[c]

        def release(c, tok):
            released[c] = tok

        at = {"turn": 0, "keep": 512}

        def small_tile(n):
            if at["turn"] + n > 512:
                at["turn"] = 0
            a = at["turn"]
            at["turn"] += n
            return st[:, a:a + n]

        def keep_tile(n):
            a = at["keep"]
            at["keep"] += n
            assert at["keep"] <= 1024
            return st[:, a:a + n]

        def rsqrt(ss, n, scale, *tokens, eps=EPS, out_=None):
            m, l, r, u, v = (small_tile(n) for _ in range(5))
            w = small_tile(n) if out_ is None else out_
            t = ts(m, ss, scale, eps, ALU.mult, ALU.add, *tokens)
            t = act(l, m, ACT.Ln, t)
            t = act(r, l, ACT.Exp, t, scale=-0.5)
            t = stt(u, r, -0.5, m, ALU.mult, ALU.mult, t)
            t = tt(v, u, r, ALU.mult, t)
            t = stt(w, v, 1.5, r, ALU.add, ALU.mult, t)
            return w, t

        def pe_turn(o, i, *tokens, sig=False):
            return op("pe", lambda e: e.transpose(o, i, ident), *tokens, sig=sig, cost=128 / 2.4 * 4)

        def transposed(tX, *sets, free=()):
            banks, res = [], []
            for j2 in range(4):
                b = bank()
                for j in (2 * j2, 2 * j2 + 1):
                    for t in range(2):
                        a = 256 * (j % 2) + 128 * t
                        tk = pe_turn(P[b][:, a:a + 128], X[:, t, 128 * j:128 * j + 128], INX, tX[j2 // 2], pfree[b],
                                     sig=(j % 2 == 1 and t == 1))
                banks.append((b, tk))
            for gain, h, l in sets:
                toks = []
                for j2, (b, tk) in enumerate(banks):
                    for j in (2 * j2, 2 * j2 + 1):
                        ta = act(h[:, j, :], P[b][:, 256 * (j % 2):256 * (j % 2) + 256], ACT.Copy, tk, INX, free,
                                 pfree[b] if toks is None else None, scale=C(gain, j))
                    for j in (2 * j2, 2 * j2 + 1):
                        tv = stt(l[:, j, :], P[b][:, 256 * (j % 2):256 * (j % 2) + 256], C(gain, j), h[:, j, :],
                                 ALU.mult, ALU.subtract, ta, INX, free)
                    banks[j2] = (b, tv)
                    pfree[b] = [ta, tv]
                    toks.append(tv)
                res.append(toks)
            return res

        def mean_squares(junk, *tokens):
            ss = small_tile(2)
            for t in range(2):
                tk = act(junk, X[:, t, :], ACT.Square, *tokens, accum=ss[:, t:t + 1])
                tokens = (tk,)
            return ss, tk

        def proj_x(pair, th, tl, xt, done_):
            for hk in range(2):
                c, wh, wl, tk = use()
                for t in range(2):
                    s = slice(128 * t, 128 * t + 128)
                    for k in range(4):
                        kk = 4 * hk + k
                        tok = mm3(P[pair + t][:, :], th[:, kk, s], tl[:, kk, s], wh[:, k, :], wl[:, k, :], kk == 0, tk,
                                  xt[kk // 2], pfree[pair + t], sig=(k == 3))
                        if k == 1:
                            yield True
                    done_[t] = tok
                    if t == 1:
                        release(c, tok)
                    yield True if t == 0 else next_chunk()

        def proj_w(pair, th, tl, xt, done_):
            for hk in range(2):
                c, wh, wl, tk = use()
                for half in range(2):
                    for m in (2 * half, 2 * half + 1):
                        o = P[pair + half][:, 256 * (m % 2):256 * (m % 2) + 256]
                        s = slice(128 * m, 128 * m + 128)
                        for k in range(4):
                            kk = 4 * hk + k
                            mm(o, wh[:, k, s], th[:, kk, :], kk == 0 and m % 2 == 0, tk, xt[kk // 2], pfree[pair + half])
                            mm(o, wh[:, k, s], tl[:, kk, :], False)
                            tok = mm(o, wl[:, k, s], th[:, kk, :], False, sig=(k == 3 and m % 2 == 1))
                        if m % 2 == 0:
                            yield True
                    done_[half] = tok
                    if half == 1:
                        release(c, tok)
                    yield True if half == 0 else next_chunk()

        def proj_few(n, th, tl, xt):
            c, wh, wl, tk = use()
            for t in range(2):
                s = slice(128 * t, 128 * t + 128)
                for k in range(8):
                    tok = mm3(P[t][:, 0:n], th[:, k, s], tl[:, k, s], wh[:, k, :], wl[:, k, :], k == 0, tk, xt[k // 2],
                              pfree[t], sig=(k == 7))
            release(c, tok)
            return tok

        def back(k0, hh, hl, first, toks, *tokens):
            c, wh, wl, tk = use()
            for ch in range(2):
                for t in range(2):
                    b = 2 * t + ch
                    for k in range(2):
                        tok = mm3(P[b][:, :], hh(k0 + k, t), hl(k0 + k, t), wh[:, k, 512 * ch:512 * ch + 512],
                                  wl[:, k, 512 * ch:512 * ch + 512], first and k == 0, tk, tokens, pfree[b],
                                  sig=(k == 1))
                    toks[b] = tok
                    if t == 0:
                        yield True
                if ch == 1:
                    release(c, tok)
                yield True if ch == 0 else next_chunk()

        def residual(toks, scale=None):
            res = []
            for ch in range(2):
                for t in range(2):
                    b = 2 * t + ch
                    xs = X[:, t, 512 * ch:512 * ch + 512]
                    if scale is None:
                        tk = tt(xs, P[b][:, :], xs, ALU.add, toks[b])
                    else:
                        tk = stt(xs, P[b][:, :], scale[0][:, t:t + 1], xs, ALU.mult, ALU.add, toks[b], scale[1])
                    pfree[b] = [tk]
                res.append(tk)
            return res

        def weave(main, *sides, whole=True):
            live = [[main, 0.0, 99]] + [[g_, 0.0, r_] for g_, r_ in sides]
            eager[0] = False
            idle = 0
            while live:
                now = clock["pe"]
                pump(now)
                busy = clock["dve"] - 3000.0
                at_ = [max(x[1], busy) if 5 <= x[2] < 99 else x[1] for x in live]
                order = [x[-1] for x in sorted([(0, x[2], r_, i, x) if r_ <= now else (1, 0, r_, i, x)
                                                for i, (x, r_) in enumerate(zip(live, at_))])]
                for entry in order:
                    r = next(entry[0], "end")
                    if r == "end":
                        live.remove(entry)
                        if entry[0] is main and not whole:
                            live = []
                        break
                    if r is False:
                        continue
                    if r is True:
                        entry[1] = last[0] if entry[0] is not main else 0.0
                    else:
                        entry[1] = r
                    break
                else:
                    idle += 1
                    assert idle < 3, "no step can be queued"
                    continue
                idle = 0
            eager[0] = True

        def chain(*gens):
            for g_ in gens:
                yield from g_

        def fence():
            return [(done[e], count[e]) for e in done]

        ready, ot_t, final = {}, {}, {}

        def attention(heads, qT, kT, V, scale, bias, a0, emit, extra=None, after=()):
            Sx = [view(a0 + 384 * i, 384) for i in range(2)]
            Pn = [view(a0 + 768 + 384 * i, 384) for i in range(3)]
            PT = [view(a0 + 1920 + 384 * i, 384) for i in range(2)]
            used, sums, prob, turned = {}, {}, {}, {}

            def score(j, h):
                b = bank()
                S, Q = Sx[j % 2], Pn[j % 3]
                for t, (c0, n) in enumerate(((0, 128), (128, 256))):
                    s = slice(128 * t, 128 * t + 128)
                    o = P[b][:, c0:c0 + n]
                    tk = mm(o, qT(h)[:, s], kT(h)[:, 0:n], True, pfree[b], ready[h], sig=(extra is None and t == 1))
                    if extra is not None:
                        q2, k2 = extra(h)
                        tk = mm(o, q2[:, s], k2[:, 0:n], False, sig=(t == 1))
                bt = bias(h)
                if isinstance(scale, float):
                    tk = stt(S, P[b][:, 0:384], scale, bt[0], ALU.mult, ALU.add, tk, bt[1], used.get(("S", j % 2)), after)
                else:
                    sc, sct = scale(h)
                    stt(S[:, 0:128], P[b][:, 0:128], sc[0], bt[0][:, 0:128], ALU.mult, ALU.add, tk, bt[1], sct,
                        used.get(("S", j % 2)), after)
                    tk = stt(S[:, 128:384], P[b][:, 128:384], sc[1], bt[0][:, 128:384], ALU.mult, ALU.add)
                if len(bt) > 2:
                    bt[2](tk)
                pfree[b] = [tk]
                mx, ng, su = small_tile(2), small_tile(2), small_tile(2)
                op("dve", lambda e: e.reduce_max(mx[:, 0:1], S[:, 0:128], AX), tk)
                tk = op("dve", lambda e: e.reduce_max(mx[:, 1:2], S[:, 128:384], AX))
                tk = ts(ng, mx, -1.0, None, ALU.mult, None, tk)
                act(Q[:, 0:128], S[:, 0:128], ACT.Exp, tk, used.get(("P", j % 3)), after, bias=ng[:, 0:1],
                    accum=su[:, 0:1])
                tk = act(Q[:, 128:384], S[:, 128:384], ACT.Exp, bias=ng[:, 1:2], accum=su[:, 1:2])
                used[("S", j % 2)] = tk
                sums[j] = (su, tk)

            def divide(j):
                su, tk = sums.pop(j)
                Q = Pn[j % 3]
                rc = small_tile(2)
                tk = op("dve", lambda e: e.reciprocal(rc, su), tk)
                ts(Q[:, 0:128], Q[:, 0:128], rc[:, 0:1], None, ALU.mult, None, tk)
                prob[j] = ts(Q[:, 128:384], Q[:, 128:384], rc[:, 1:2], None, ALU.mult, None)

            def turn(j):
                b = bank()
                for n in range(3):
                    tk = pe_turn(P[b][:, 128 * n:128 * n + 128], Pn[j % 3][:, 128 * n:128 * n + 128], prob[j], pfree[b],
                                 sig=(n == 2))
                used[("P", j % 3)] = tk
                tk = act(PT[j % 2], P[b][:, 0:384], ACT.Copy, tk, used.get(("T", j % 2)), after)
                pfree[b] = [tk]
                turned[j] = tk

            def value(j, h):
                b = bank()
                mm(P[b][:, 0:256], V(h, 0), PT[j % 2][:, 0:256], True, turned[j], pfree[b])
                tk = mm(P[b][:, 128:256], V(h, 1), PT[j % 2][:, 256:384], False, sig=True)
                used[("T", j % 2)] = tk
                pfree[b] = emit(h, b, tk)

            n = len(heads)
            for j in range(n + 3):
                if j < n:
                    while heads[j] not in ready:
                        yield False
                    yield eta(ready[heads[j]])
                    score(j, heads[j])
                if 0 <= j - 1 < n:
                    divide(j - 1)
                if 0 <= j - 2 < n:
                    yield eta(prob[j - 2])
                    turn(j - 2)
                if 0 <= j - 3 < n:
                    yield eta(turned[j - 3])
                    value(j - 3, heads[j - 3])

        def o_split(h, b, tk, *tokens):
            a = act(oth[:, 256 * h:256 * h + 256], P[b][:, 0:256], ACT.Copy, tk, *tokens)
            v = tt(otl[:, 256 * h:256 * h + 256], P[b][:, 0:256], oth[:, 256 * h:256 * h + 256], ALU.subtract, a, *tokens)
            return [a, v]

        def keep_o(h, b, tk):
            ot_t[h] = o_split(h, b, tk)
            return ot_t[h]

        def oh(k, t):
            return oth[:, 256 * k + 128 * t:256 * k + 128 * t + 128]

        def ol(k, t):
            return otl[:, 256 * k + 128 * t:256 * k + 128 * t + 128]

        def view(a, n, s=None, **kw):
            v = arena[:, a:a + n]
            return v.rearrange(s, **kw) if s else v

        def o_product(hh=oh, hl=ol):
            for p_ in range(4):
                while 2 * p_ + 1 not in ot_t:
                    yield False
                yield eta(ot_t[2 * p_], ot_t[2 * p_ + 1])
                yield from back(2 * p_, hh, hl, p_ == 0, final, ot_t[2 * p_], ot_t[2 * p_ + 1])

        def stage():
            at["keep"] = 512
            ready.clear()
            ot_t.clear()
            final.clear()
            qk_used.clear()
            return fence()

        qk_used = {}

        A_PROJ, A_KV, A_Q, A_KT, A_QT, A_QPT, A_KPT, A_SQ, A_AT, A_TR, AB = (
            0, 1408, 5504, 7040, 9088, 11136, 12160, 12416, 13440, 16128, 17528)
        A_IND = A_AT + 640
        projS = view(A_PROJ, 1408, "p (t n) -> p t n", t=2)
        kvtok = view(A_KV, 4096, "p (t h n) -> p t h n", t=2, h=8)
        qtoks = [view(A_Q + 768 * i, 768, "p (t h n) -> p t h n", t=2, h=2) for i in range(2)]
        kT = view(A_KT, 2048, "p (h n) -> p h n", h=8)
        qT = view(A_QT, 2048, "p (h n) -> p h n", h=8)
        qpT = view(A_QPT, 1024, "p (h n) -> p h n", h=4)
        kpT = view(A_KPT, 256)
        sq = [view(A_SQ + 512 * i, 512) for i in range(2)]
        rt = view(A_TR, 448)

        table("silu_and_others")
        posf = keep_tile(2)
        rope_t, t_rope = {}, []

        def rope_tables():
            yield eta(IN)
            tp = copy(posf, posT, IN)
            ang, nn, rr, sn, cs, s2 = (rt[:, 64 * i:64 * i + 64].rearrange("p (t n) -> p t n", t=2) for i in range(6))
            for t in range(2):
                tk = ts(ang[:, t, :], RW("invf"), posf[:, t:t + 1], None, ALU.mult, None, tp)
            MAGIC = 12582912.0
            C1 = 6.28125
            C2 = float(np.float32(2 * np.pi - C1))
            C3 = float(2 * np.pi - C1 - C2)
            tk = ts(nn, ang, float(1 / (2 * np.pi)), MAGIC, ALU.mult, ALU.add, tk)
            tk = ts(nn, nn, MAGIC, None, ALU.subtract, None, tk)
            tk = stt(rr, nn, -C1, ang, ALU.mult, ALU.add, tk)
            tk = stt(rr, nn, -C2, rr, ALU.mult, ALU.add, tk)
            tk = stt(rr, nn, -C3, rr, ALU.mult, ALU.add, tk)
            tk = ts(rr, rr, 3.1415925, -3.1415925, ALU.min, ALU.max, tk)
            tk = act(sn, rr, ACT.Sin, tk)
            tk2 = act(s2, rr, ACT.Sin, scale=0.5)
            tk = tt(s2, s2, s2, ALU.mult, tk2)
            tk = ts(cs, s2, -2.0, 1.0, ALU.mult, ALU.add, tk)
            table("natural_log_exp_and_others")
            for n_, nm in enumerate(("ropeq", "ropek")):
                for j, (src, half) in enumerate(((cs, 0), (sn, 1), (cs, 1), (sn, 0))):
                    d = view(A_TR + 448 + 64 * (4 * n_ + j), 64, "p (t n) -> p t n", t=2)
                    g = bc(RW(nm)[:, 32 * half:32 * half + 32].unsqueeze(1), 1, 2)
                    tk = tt(d, src, g, ALU.mult, tk)
                    rope_t[nm, j] = d
            t_rope.append(tk)
            yield True

        roped = []

        def rope(nm, src, dst, t, nh, tmp, *tokens, eng="dve"):
            x1, x2 = src[:, :, 0:32], src[:, :, 32:64]
            f = [bc(rope_t[nm, j][:, t, :].unsqueeze(1), 1, nh) for j in range(4)]
            ta = tmp.rearrange("p (a h n) -> p a h n", a=4, h=nh)
            tt(ta[:, 0], x1, f[0], ALU.mult, t_rope[0], roped, *tokens, eng=eng)
            tt(ta[:, 1], x2, f[1], ALU.mult, eng=eng)
            tt(ta[:, 2], x2, f[2], ALU.mult, eng=eng)
            tk = tt(ta[:, 3], x1, f[3], ALU.mult, eng=eng)
            tt(dst[:, :, 0:32], ta[:, 0], ta[:, 1], ALU.subtract, tk, eng=eng)
            tk = tt(dst[:, :, 32:64], ta[:, 2], ta[:, 3], ALU.add, eng=eng)
            roped[:] = [tk]
            return tk

        (xT,) = transposed([INX, INX], ("attn0", xh, xl))
        ss, tk = mean_squares(view(A_QT, 1024), INX)
        t_ss0 = tk
        t_in = {}

        def mla_in():
            for c_ in range(4):
                c, wh, wl, tk = use()
                for t in range(2):
                    s = slice(128 * t, 128 * t + 128)
                    for ch, (a, n) in enumerate(((0, 512), (512, 192))):
                        for k in range(2):
                            tok = mm3(P[2 * t + ch][:, 0:n], xh[:, 2 * c_ + k, s], xl[:, 2 * c_ + k, s],
                                      wh[:, k, a:a + n], wl[:, k, a:a + n], c_ == 0 and k == 0, tk, xT[c_],
                                      sig=(k == 1))
                        t_in[t, ch] = tok
                        if t == 1 and ch == 1:
                            release(c, tok)
                            yield next_chunk()
                        else:
                            yield True

        keep_bias = sb("pkf", [128, 64])
        biasM = view(AB, 3072, "p (h n) -> p h n", h=8)
        biasdone, bias_over, t_kp, t_cT = [], [], [], []

        def bias_steps():
            yield eta(IN)
            pq = keep_tile(256)
            pkf = keep_bias[:, :]
            t1 = copy(pq, pqi, IN)
            t1 = ts(pq, pq, K("tb"), None, ALU.subtract, None, t1)
            t2 = copy(pkf, pki, IN)
            tb = pint[:, 0:48].bitcast(BF16).rearrange("p (a n) -> p a n", a=3)
            dd, de = pint[:, 64:96], pint[:, 96:128]
            tk = tt(dd, tab, tabs, ALU.subtract, IN, t1)
            tk = copy(tb[:, 0, :], dd, tk)
            tk = tt(de, dd, tb[:, 0, :], ALU.subtract, tk)
            tk = copy(tb[:, 1, :], de, tk)
            tk = tt(dd, de, tb[:, 1, :], ALU.subtract, tk)
            t_tb = copy(tb[:, 2, :], dd, tk)
            yield True
            ind = [view(a + 512 * i, 512).bitcast(BF16).rearrange("p (g q) -> p g q", g=4)
                   for a in (A_IND, 0) for i in range(2)]
            usedi = {}
            tis, iv_, moved = {}, {}, []

            def make(q_):
                a_ = bc(pq.unsqueeze(1), 1, 4)
                b_ = bc(pkf[:, 4 * q_:4 * q_ + 4].unsqueeze(2), 2, 256)
                if t_kp and not moved:
                    moved.extend([t_kp, t_cT])
                iv_[q_] = ind[q_ % 2 + (2 if moved else 0)]
                tis[q_] = tt(iv_[q_], a_, b_, ALU.is_ge, t1, t2, usedi.get(q_ % 2), moved)

            make(0)
            yield True
            for q_ in range(16):
                iv = iv_[q_]
                if q_ + 1 < 16:
                    make(q_ + 1)
                b = bank()
                for t in range(2):
                    nk = 2 + 2 * t
                    n = 8 * nk
                    for g_ in range(4):
                        for p_ in range(3):
                            a = 128 * t + n * g_
                            tk = mm(P[b][:, a:a + n], iv[0:32 * nk, g_, 128 * t:128 * t + 128], tb[0:32 * nk, p_, 0:n],
                                    p_ == 0, tis[q_], t_tb, pfree[b], sig=(t == 1 and g_ == 3 and p_ == 2))
                usedi[q_ % 2] = tk
                for t in range(2):
                    nk = 2 + 2 * t
                    base = 128 * t
                    d = biasM[:, :, base:base + 64 * nk].rearrange("p h (k g) -> p h k g", k=nk)[:, :, :, 4 * q_:4 * q_ + 4]
                    s_ = P[b][:, base:base + 32 * nk].rearrange("p (g k h) -> p h k g", g=4, k=nk)
                    m_ = K("mask")[:, base:base + 64 * nk].rearrange("p (k g) -> p k g", k=nk)[:, :, 4 * q_:4 * q_ + 4]
                    tv = tt(d, s_, bc(m_.unsqueeze(1), 1, 8), ALU.add, tk)
                pfree[b] = [tv]
                if moved and not bias_over:
                    bias_over.extend(usedi.values())
                yield True
            biasdone.append(tv)
            if not bias_over:
                bias_over.extend(usedi.values())
        def rope_wait():
            while not t_rope:
                yield False

        bias_g = bias_steps()
        weave(chain(mla_in(), rope_wait()), (rope_tables(), 4), (bias_g, 5), whole=False)
        r0, tr0 = rsqrt(ss, 2, 1.0 / D, t_ss0, out_=keep_tile(2))
        t_x = t_in[1, 1]
        ssm = small_tile(6)
        for t in range(2):
            for ch, (a, n) in enumerate(((0, 512), (512, 192))):
                tk = act(projS[:, t, a:a + n], P[2 * t + ch][:, 0:n], ACT.Copy, t_in[t, ch], tr0, scale=r0[:, t:t + 1])
                pfree[2 * t + ch] = [tk]
        t_ps = tk
        for j in (3, 4, 0, 1, 2):
            b = bank()
            for t in range(2):
                tk = pe_turn(P[b][:, 128 * t:128 * t + 128], projS[:, t, 128 * j:128 * j + 128], t_ps, pfree[b],
                             sig=(t == 1))
            g = C("qa", j) if j < 3 else C("kva", j - 3)
            ta = act(xh[:, j, :], P[b][:, 0:256], ACT.Copy, tk, t_x, scale=g)
            tv = stt(xl[:, j, :], P[b][:, 0:256], g, xh[:, j, :], ALU.mult, ALU.subtract, ta, t_x)
            pfree[b] = [ta, tv]
        cT = tv
        for t in range(2):
            for i, (a, n) in enumerate(((0, 384), (384, 256), (640, 64))):
                tk = act(sq[(3 * t + i) % 2][:, 0:n], projS[:, t, a:a + n], ACT.Square, t_ps,
                         accum=ssm[:, 2 * i + t:2 * i + t + 1])
                t_ps = tk
        ssn = small_tile(6)
        for i, n in enumerate((384, 256, 64)):
            t2 = ts(ssn[:, 2 * i:2 * i + 2], ssm[:, 2 * i:2 * i + 2], 1.0 / n, None, ALU.mult, None, tk)
        rm, trm = rsqrt(ssn, 6, 1.0, t2, out_=keep_tile(6))
        t_cT.extend([cT, trm])
        gk = keep_tile(1)
        t_gk = tt(gk, C("mlaqn"), C("mlakn"), ALU.mult, IN)
        sq_used = {}
        sqi = [0]

        def head_rstd(srcs, nh, n, tok, sqs):
            o = small_tile(nh * len(srcs))
            for i, src in enumerate(srcs):
                q_ = sqi[0] % len(sqs)
                sqi[0] += 1
                s_ = sqs[q_][:, 0:nh * n].rearrange("p (h n) -> p h n", h=nh)
                ta = act(s_, src, ACT.Square, tok, sq_used.get(q_))
                tv = op("dve", lambda e, i=i, s_=s_: e.reduce_sum(o[:, nh * i:nh * i + nh], s_, AX), ta)
                sq_used[q_] = tv
            return rsqrt(o, nh * len(srcs), 1.0 / n, tv)

        def heads_T(dst, src, h0, gain, tok, *tokens):
            b = bank()
            for j in range(2):
                for t in range(2):
                    tk = pe_turn(P[b][:, 256 * j + 128 * t:256 * j + 128 * t + 128], src(t, h0 + j), tok, pfree[b],
                                 sig=(j == 1 and t == 1))
            d = dst[:, h0:h0 + 2, :]
            i = P[b][:, :].rearrange("p (h n) -> p h n", h=2)
            if gain is None:
                tk = act(d, i, ACT.Copy, tk, *tokens)
            else:
                tk = act(d, i, ACT.Copy, tk, *tokens, scale=gain)
            pfree[b] = [tk]
            return tk

        kv_t, q_t, kT_t = {}, {}, {}

        def mla_kv(g):
            c, wh, wl, tk = use()
            for ch in range(2):
                for t in range(2):
                    b = 2 * ch + t
                    for k in range(2):
                        s = slice(128 * t, 128 * t + 128)
                        tok = mm3(P[b][:, :], xh[:, 3 + k, s], xl[:, 3 + k, s], wh[:, k, 512 * ch:512 * ch + 512],
                                  wl[:, k, 512 * ch:512 * ch + 512], k == 0, tk, cT, pfree[b], sig=(k == 1))
                    h0 = 4 * g + 2 * ch
                    ta = act(kvtok[:, t, h0:h0 + 2, :], P[b][:, :].rearrange("p (h n) -> p h n", h=2), ACT.Copy, tok, trm,
                             scale=rm[:, 2 + t:3 + t])
                    pfree[b] = [ta]
                    if ch == 1 and t == 1:
                        release(c, tok)
                        kv_t[g] = ta
                    yield True

        def mla_q(i):
            while i >= 2 and 2 * (i - 2) not in ready:
                yield False
            c, wh, wl, tk = use()
            for t in range(2):
                b = t + 2 * (i % 2)
                s = slice(128 * t, 128 * t + 128)
                for k in range(3):
                    tok = mm3(P[b][:, 0:384], xh[:, k, s], xl[:, k, s], wh[:, k, :], wl[:, k, :], k == 0, tk, cT,
                              pfree[b], sig=(k == 2))
                ta = act(qtoks[i % 2][:, t], P[b][:, 0:384].rearrange("p (h n) -> p h n", h=2), ACT.Copy,
                         tok, trm, qk_used.get(("q", i % 2)), scale=rm[:, t:t + 1])
                pfree[b] = [ta]
                if t == 1:
                    release(c, tok)
                    q_t[i] = ta
                yield True

        def mla_kpe():
            kp = view(A_AT, 256, "p (t n) -> p t n", t=2)
            kn = view(A_AT + 256, 128, "p (t n) -> p t n", t=2)
            for t in range(2):
                tk = ts(kn[:, t, :], projS[:, t, 640:704], rm[:, 4 + t:5 + t], None, ALU.mult, None, trm)
            for t in range(2):
                tk = rope("ropek", kn[:, t:t + 1, :], kp[:, t:t + 1, 0:64], t, 1, view(A_AT + 384 + 128 * t, 128), tk)
            tk = copy(kp[:, :, 64:128], kp[:, :, 0:64], tk)
            yield True
            b = bank()
            for t in range(2):
                tk = pe_turn(P[b][:, 128 * t:128 * t + 128], kp[:, t, :], tk, pfree[b], sig=(t == 1))
            tk = copy(kpT, P[b][:, 0:256], tk)
            pfree[b] = [tk]
            t_kp.append(tk)
            yield True

        def mla_kpost(g):
            while g not in kv_t:
                yield False
            ks = [kvtok[:, t, 4 * g:4 * g + 4, 0:128] for t in range(2)]
            r_, tr = head_rstd(ks, 4, 128, kv_t[g], sq)
            for t in range(2):
                tkk = tt(ks[t], ks[t], bc(r_[:, 4 * t:4 * t + 4].unsqueeze(2), 2, 128), ALU.mult, tr)
            yield True
            for h0 in (4 * g, 4 * g + 2):
                kT_t[h0] = heads_T(kT, lambda t, h: kvtok[:, t, h, 0:128], h0, gk, tkk, t_gk)
                yield True

        def mla_qpost(i):
            while i not in q_t or not t_kp:
                yield False
            h0 = 2 * i
            qt = qtoks[i % 2]
            qn = [qt[:, t, :, 0:128] for t in range(2)]
            qp = [qt[:, t, :, 128:192] for t in range(2)]
            r_, tr = head_rstd(qn, 2, 128, q_t[i], sq)
            r2_, tr2 = head_rstd(qp, 2, 64, q_t[i], sq)
            for t in range(2):
                tq = tt(qn[t], qn[t], bc(r_[:, 2 * t:2 * t + 2].unsqueeze(2), 2, 128), ALU.mult, tr)
            yield True
            for t in range(2):
                tp_ = tt(qp[t], qp[t], bc(r2_[:, 2 * t:2 * t + 2].unsqueeze(2), 2, 64), ALU.mult, tr2, eng="pool")
            for t in range(2):
                tp_ = rope("ropeq", qp[t], qp[t], t, 2, view(A_TR + 1016, 256), tp_, eng="pool")
            pr = [view(A_TR + o_, 128) for o_ in ((0, 128), (256, 1272))[i % 2]]
            for t in range(2):
                tp_ = copy(pr[t].rearrange("p (h n) -> p h n", h=2), qp[t], tp_, qk_used.get(("pr", i % 2)), eng="pool")
            yield eta(tq)
            tkq = heads_T(qT, lambda t, h: qt[:, t, h - h0, 0:128], h0, None, tq)
            yield eta(tp_)
            b = bank()
            for t in range(2):
                tk = pe_turn(P[b][:, 128 * t:128 * t + 128], pr[t], tp_, pfree[b], sig=(t == 1))
            qk_used["pr", i % 2] = tk
            qk_used[("q", i % 2)] = [tk, tp_]
            tkp = act(qpT[:, i, :], P[b][:, 0:256], ACT.Copy, tk)
            pfree[b] = [tkp]
            while 2 * i not in kT_t:
                yield False
            ready[h0] = ready[h0 + 1] = [kT_t[h0], tkq, tkp, t_kp[0]]
            yield True

        def mla_extra(h):
            s = slice(64 * (h % 2), 64 * (h % 2) + 64)
            return qpT[s, h // 2, :], kpT[s, :]

        mla_main = chain(mla_kv(0), mla_q(0), mla_q(1), mla_kv(1), mla_q(2), mla_q(3), o_product())
        mla_post = chain(mla_kpe(), mla_kpost(0), mla_kpost(1))
        mla_attn = attention(range(8), lambda h: qT[:, h, :], lambda h: kT[:, h, :],
                             lambda h, t: kvtok[:, t, h, 128:256], float(1.0 / np.sqrt(192.0)),
                             lambda h: (K("mask"), IN), A_AT, keep_o, extra=mla_extra, after=bias_over)

        def after_kpe(gen):
            while not t_kp or not bias_over:
                yield False
            yield from gen

        weave(mla_main, (mla_post, 1), (chain(mla_qpost(0), mla_qpost(2)), 1), (chain(mla_qpost(1), mla_qpost(3)), 1), (after_kpe(mla_attn), 0), (bias_g, 5))
        tX = residual(final)

        s_pr = sem("s_pr")

        def finish(tX):
            for t in range(2):
                dma(lambda e, t=t: e.dma_start(out[128 * t:128 * t + 128, :], X[:, t, :]), s_out, tX)
            wait("sp", [(s_out, 32)])

        def mlp(i, tX):
            F = stage()
            (xt,) = transposed(tX, (f"mlp{i}", xh, xl), free=F[:1])
            ss, tk = mean_squares(view(4096, 1024), tX, F)
            m = small_tile(2)
            r2 = keep_tile(2)
            tk = ts(m, ss, 1.0 / D, EPS, ALU.mult, ALU.add, tk)
            tr2 = op("dve", lambda e: e.reciprocal(r2, m), tk, F)
            if i == 0:
                predf = view(6144, 896)
                dma(lambda e: e.dma_start(predf, A["c_pred"]), s_pr, F)
                copy(level_mask.rearrange("p l n -> p (l n)"), predf, (s_pr, 16))
            rel = [view(2048 * i_, 1024) for i_ in range(2)]
            sqr = [view(2048 * i_ + 1024, 1024) for i_ in range(2)]
            freed, used, hid, toks = {}, {}, {}, {}
            for g in range(9):
                if g < 8:
                    v = g % 2
                    mtok = {}
                    for _ in proj_w(4 + 2 * v, xh, xl, xt, mtok):
                        pass
                    tl_ = []
                    for half in range(2):
                        b = 4 + 2 * v + half
                        hs = slice(512 * half, 512 * half + 512)
                        os_ = slice(1024 * v + 512 * half, 1024 * v + 512 * half + 512)
                        ta = act(rel[v][:, hs], P[b][:, :], ACT.Relu, mtok[half], freed.get((v, half)), F)
                        pfree[b] = [ta]
                        ta = act(sqr[v][:, hs], rel[v][:, hs], ACT.Square, ta)
                        th = copy(oth[:, os_], sqr[v][:, hs], ta, used.get(v), F)
                        tv = tt(otl[:, os_], sqr[v][:, hs], oth[:, os_], ALU.subtract, th)
                        freed[(v, half)] = tv
                        tl_.append(tv)
                    hid[g] = tl_
                if g > 0:
                    v = (g - 1) % 2
                    f = lambda q, k, t, v=v: q[:, 1024 * v + 256 * k + 128 * t:1024 * v + 256 * k + 128 * t + 128]
                    for kk in range(2):
                        for _ in back(2 * kk, lambda k, t: f(oth, k, t), lambda k, t: f(otl, k, t), g == 1 and kk == 0,
                                      toks, hid[g - 1][kk], F):
                            pass
                    used[v] = toks[3]
            ring[0] = 4
            return residual(toks, (r2, tr2))

        if stop >= 2:
            tX = mlp(0, tX)

        def token_major(pair, dst, toks, scale, *tokens):
            for t in range(2):
                ta = act(dst(t), P[pair + t][:, :], ACT.Copy, toks[t], *tokens, scale=scale[:, t:t + 1])
                pfree[pair + t] = [ta]
            return ta

        def heads_main(g, which, pair, th, tl, xt, r, bufs, V, F):
            toks = {}
            yield from proj_x(pair, th, tl, xt, toks)
            while which != "v" and g > 0 and (which, 3) not in ready:
                yield False
            if which == "v":
                evac[("v", g)] = token_major(pair, lambda t: V[:, t, 512 * g:512 * g + 512], toks, r[0], r[1], F)
            else:
                evac[(which, g)] = token_major(pair, lambda t: bufs[which][:, t, :], toks, r[0], r[1], F,
                                               qk_used.get(which))
            evac[("pe", which, g)] = toks[1]

        evac = {}

        def heads_post(g, which, bufs, qT_, kT_, gain, rq, sqs, F):
            while (which, g) not in evac:
                yield False
            buf = bufs[which]
            ta = evac[(which, g)]
            v4 = [buf[:, t, :].rearrange("p (h n) -> p h n", h=4) for t in range(2)]
            r_, tr_ = head_rstd(v4, 4, 128, ta, sqs)
            if which == "k":
                for t in range(2):
                    tk = tt(v4[t], v4[t], bc(r_[:, 4 * t:4 * t + 4].unsqueeze(2), 2, 128), ALU.mult, tr_)
            else:
                tk = ts(rq[:, :, 4 * g:4 * g + 4], r_.rearrange("p (t h) -> p t h", t=2), float(128 ** -0.5), None,
                        ALU.mult, None, tr_, F)
                ready[("rq", g)] = tk
            yield True
            for j in range(2):
                h0 = 4 * g + 2 * j
                src = lambda t, h: buf[:, t, 128 * (h - 4 * g):128 * (h - 4 * g) + 128]
                tk2 = heads_T(kT_ if which == "k" else qT_, src, h0, gain if which == "k" else None,
                              tk if which == "k" else ta, F)
                qk_used[which] = [(done["pe"], count["pe"]), tk2]
                ready[(which, h0)] = ready[(which, h0 + 1)] = tk2
                yield True

        def when_ready(g):
            for j in range(4):
                h = 4 * g + j
                while not all(x in ready for x in (("q", h), ("k", h), ("rq", g))) or ("v", g) not in evac:
                    yield False
                ready[h] = [ready[("q", h)], ready[("k", h)], evac[("v", g)]]
            yield True

        if stop >= 3:
            F = stage()
            evac.clear()
            V = view(0, 2048, "p (t n) -> p t n", t=2)
            kT = view(2048, 2048, "p (h n) -> p h n", h=8)
            qT = view(4096, 2048, "p (h n) -> p h n", h=8)
            bufs = {"q": view(6144, 1024, "p (t n) -> p t n", t=2), "k": view(7168, 1024, "p (t n) -> p t n", t=2)}
            sqs = [view(8192 + 512 * i, 512) for i in range(2)]
            rq = view(9216, 16, "p (t h) -> p t h", t=2)
            (xt,) = transposed(tX, ("attn1", xh, xl), free=F[:1])
            ss, tk = mean_squares(view(10000, 1024), tX, F)
            r1 = rsqrt(ss, 2, 1.0 / D, tk, F, out_=keep_tile(2))
            gm = keep_tile(1)
            t_gm = tt(gm, C("mobaq"), C("mobak"), ALU.mult, IN, F)
            sq_used.clear()
            sq_used.update({0: F, 1: F})
            bufF = [F, t_gm]
            main = chain(*[heads_main(g, w_, 2 * (i_ % 2), xh, xl, xt, r1, bufs, V, bufF)
                           for i_, (g, w_) in enumerate([(g, w_) for g in range(2) for w_ in "qkv"])], o_product())
            post = chain(*[heads_post(g, w_, bufs, qT, kT, gm, rq, sqs, bufF) for g in range(2) for w_ in "qk"])
            gate = chain(when_ready(0), when_ready(1))
            attn = attention(range(8), lambda h: qT[:, h, :], lambda h: kT[:, h, :],
                             lambda h, t: V[:, t, 128 * h:128 * h + 128],
                             lambda h: ([rq[:, t, h:h + 1] for t in range(2)], ready[("rq", h // 4)]),
                             lambda h: (biasM[:, h, :], biasdone[0]), 11024, keep_o, after=F)
            weave(main, (post, 1), (gate, 1), (attn, 0))
            tX = residual(final)
        if stop >= 4:
            tX = mlp(1, tX)

        s_pn = sem("s_pn")
        npn = [0]

        def post_row(name, a, F):
            g = view(a, 1024)
            dma(lambda e: e.dma_start(g, bc(A[name].rearrange("(a d) -> a d", a=1), 0, 128)), s_pn, F)
            npn[0] += 16
            return g, (s_pn, npn[0])

        def post_norm(toks, grow, tg, a, F):
            ss = small_tile(4)
            for b in (0, 2, 1, 3):
                d = view(a + 512 * b, 512)
                g = grow[:, 512 * (b % 2):512 * (b % 2) + 512]
                tg_ = tt(view(a + 2048 + 512 * b, 512), P[b][:, :], g, ALU.mult, toks[b], tg, F)
                tk = act(d, P[b][:, :], ACT.Square, tg_, F, accum=ss[:, b:b + 1])
                pfree[b] = [tk]
            s2_ = small_tile(2)
            sv = ss.rearrange("p (t c) -> p t c", t=2)
            tk = tt(s2_.unsqueeze(2), sv[:, :, 0:1], sv[:, :, 1:2], ALU.add, tk)
            r_, tr = rsqrt(s2_, 2, 1.0 / D, tk)
            res = []
            for ch in range(2):
                for b in (ch, 2 + ch):
                    xs = X[:, b // 2, 512 * ch:512 * ch + 512]
                    tk = stt(xs, view(a + 2048 + 512 * b, 512), r_[:, b // 2:b // 2 + 1], xs, ALU.mult, ALU.add, tr)
                res.append(tk)
            return res

        def across(r, dst, tr, *tokens):
            b = bank()
            for t in range(2):
                tk = pe_turn(P[b][:, 128 * t:128 * t + 128], bc(r[:, t:t + 1], 1, 128), tr, IN, pfree[b], sig=(t == 1))
            tk = copy(dst, P[b][:, 0:256], tk, *tokens)
            pfree[b] = [tk]
            return tk

        if stop >= 5:
            F = stage()
            kS = view(0, 2048, "p (h n) -> p h n", h=8)
            qS = view(2048, 2048, "p (h n) -> p h n", h=8)
            BA = view(4096, 6144, "p (h n) -> p h n", h=8)
            Vt = view(10240, 2048, "p (t h n) -> p t h n", t=2, h=8)
            zT = view(12288, 2048, "p (h n) -> p h n", h=8)
            pre = [view(14336 + 512 * i, 512) for i in range(2)]
            vS = [view(15360 + 1024 * i, 1024, "p (h n) -> p h n", h=4) for i in range(2)]
            acc2 = [view(15360 + 512 * i, 512) for i in range(4)]
            Dt = [view(17408 + 768 * i, 768) for i in range(2)]
            sqp = [view(18944 + 256 * i, 256) for i in range(4)]
            rT = view(19968, 256)
            rbc = view(20224, 256)
            Ya = view(0, 4096, "p (g n) -> p g n", g=8)

            (xt,) = transposed(tX, ("gdnpre", xh, xl), free=F[:1])
            ss, tk = mean_squares(view(0, 1024), tX, F)
            r1, tr1 = rsqrt(ss, 2, 1.0 / D, tk, F, out_=keep_tile(2))
            tok = proj_few(16, xh, xl, xt)
            t_rbc = across(r1, rbc, tr1, F)
            ab_ = keep_tile(32).rearrange("p (t n) -> p t n", t=2)
            for t in range(2):
                tab_ = ts(ab_[:, t, :], P[t][:, 0:16], r1[:, t:t + 1], None, ALU.mult, None, tok, tr1, F)
                pfree[t] = [tab_]
            conv_o = COLS["conv"][0]
            gt, preu, accu = {}, {}, {}
            cnt = {"pre": 0, "acc": 0}

            def gdn_proj(name, g, pair):
                toks = {}
                n_ = order.index((name, g))
                while n_ >= 2 and ("done",) + order[n_ - 2] not in gt:
                    yield False
                yield from proj_w(pair, xh, xl, xt, toks)
                gt[("p", name, g)] = (pair, toks)

            def gdn_conv(name, g):
                while ("p", name, g) not in gt:
                    yield False
                pair, toks = gt[("p", name, g)]
                for half in range(2):
                    b = pair + half
                    rb = bc(rbc.unsqueeze(1), 1, 2)
                    src = P[b][:, :].rearrange("p (m n) -> p m n", m=2)
                    if name == "z":
                        tk = tt(zT[:, 4 * g + 2 * half:4 * g + 2 * half + 2, :], src, rb, ALU.mult, toks[half], t_rbc, F)
                        pfree[b] = [tk]
                        gt[("z", g)] = tk
                        yield True
                        continue
                    i = cnt["pre"] % 2
                    cnt["pre"] += 1
                    px = pre[i].rearrange("p (m n) -> p m n", m=2)
                    t0 = tt(px, src, rb, ALU.mult, toks[half], t_rbc, preu.get(i), F)
                    pfree[b] = [t0]
                    if name == "v":
                        acc = vS[g][:, 2 * half:2 * half + 2, :]
                        free = vfree
                    else:
                        ai = cnt["acc"] % 4
                        cnt["acc"] += 1
                        acc = acc2[ai].rearrange("p (m n) -> p m n", m=2)
                        free = accu.get(ai)
                    m0 = {"q": 0, "k": 8, "v": 16}[name] + 4 * g + 2 * half
                    w = lambda j, tap: cols[:, conv_o + 4 * (m0 + j) + tap:conv_o + 4 * (m0 + j) + tap + 1]
                    tj = [act(acc[:, j, :], px[:, j, :], ACT.Copy, t0, free, F, scale=w(j, 3)) for j in range(2)]
                    for tap in (2, 1, 0):
                        d = 3 - tap
                        tj = [stt(acc[:, j, d:256], px[:, j, 0:256 - d], w(j, tap), acc[:, j, d:256], ALU.mult, ALU.add,
                                  tj[j]) for j in range(2)]
                    preu[i] = tj[1]
                    if name != "v":
                        dst = (kS if name == "k" else qS)[:, 4 * g + 2 * half:4 * g + 2 * half + 2, :]
                        ta = act(dst, acc, ACT.Silu, tj[1], F)
                        accu[ai] = ta
                        gt[(name, g)] = ta
                    else:
                        gt[("vc", g)] = tj[1]
                    yield True
                gt[("done", name, g)] = True

            def gdn_stats():
                lnr = keep_tile(32)
                sst = keep_tile(32)
                sv = sst.rearrange("p (t q h) -> p t q h", t=2, q=2)
                spf = {}
                for h in range(8):
                    while ("done", "k", h // 4) not in gt or ("done", "q", h // 4) not in gt:
                        yield False
                    tq = []
                    for qi, (src, nm) in enumerate(((kS, "k"), (qS, "q"))):
                        i = (2 * h + qi) % 4
                        tq.append(tt(sqp[i], src[:, h, :], src[:, h, :], ALU.mult, gt[(nm, h // 4)], spf.get(i), F,
                                     eng="pool" if qi else "dve"))
                    yield eta(tq)
                    b = bank()
                    for qi in range(2):
                        i = (2 * h + qi) % 4
                        for t in range(2):
                            a = 2 * t + qi
                            tk = mm(P[b][:, a:a + 1], sqp[i][:, 128 * t:128 * t + 128], K("ones")[:, 0:1], True, tq,
                                    pfree[b], sig=(t == 1))
                        spf[i] = tk
                    t_ss = ts(sv[:, :, :, h:h + 1], P[b][:, 0:4].rearrange("p (t q n) -> p t q n", t=2, q=2), EPS, None,
                              ALU.add, None, tk, F)
                    pfree[b] = [t_ss]
                table("natural_log")
                t_ln = act(lnr, sst, ACT.Ln, t_ss, F)
                xx = keep_tile(32).rearrange("p (t n) -> p t n", t=2)
                tt(xx[:, :, 0:8], ab_[:, :, 0:8], bc(RW("dt").unsqueeze(1), 1, 2), ALU.add, IN, tab_, F)
                tk = ts(xx[:, :, 8:16], ab_[:, :, 8:16], -1.0, None, ALU.mult, None)
                e0, e1, e2, sp = (small_tile(32).rearrange("p (t n) -> p t n", t=2) for _ in range(4))
                ta = act(e0, xx, ACT.Abs, tk)
                table("natural_log_exp_and_others")
                ta = act(e1, e0, ACT.Exp, ta, scale=-1.0)
                ta = act(e2, e1, ACT.Ln, ta, bias=1.0)
                yield True
                tk = stt(sp, xx, 0.0, e2, ALU.max, ALU.add, ta)
                ea = keep_tile(8)
                ta = act(ea, RW("alog"), ACT.Exp, IN, F)
                gg = keep_tile(16).rearrange("p (t n) -> p t n", t=2)
                nb_ = keep_tile(16).rearrange("p (t n) -> p t n", t=2)
                tg_ = stt(gg, sp[:, :, 0:8], -1.0, bc(ea.unsqueeze(1), 1, 2), ALU.mult, ALU.mult, ta, tk)
                tn_ = ts(nb_, sp[:, :, 8:16], -1.0, None, ALU.mult, None, tk)
                gt["t_beta"] = act(beta, nb_, ACT.Exp, tn_, F)
                yield True
                b = bank()
                for t in range(2):
                    mm(P[b][:, 8 * t:8 * t + 8], K("tri"), gg[:, t, :], True, tg_, pfree[b])
                tk = mm(P[b][:, 16:24], K("ones"), gg[:, 0, :], True, sig=True)
                cum = keep_tile(24)
                t_cum = copy(cum, P[b][:, 0:24], tk)
                pfree[b] = [t_cum]
                cu = cum[:, 0:16].rearrange("p (t n) -> p t n", t=2)
                lr = lnr.rearrange("p (t n) -> p t n", t=2)
                cbv = cb[:, 0:16].rearrange("p (t n) -> p t n", t=2)
                rw = keep_tile(32).rearrange("p (t n) -> p t n", t=2)
                tmpc = keep_tile(32).rearrange("p (a t n) -> p a t n", a=2, t=2)
                tk = stt(cbv, lr[:, :, 0:8], -0.5, cu, ALU.mult, ALU.subtract, t_cum, t_ln, F)
                gt["t_cb"] = tt(cb[:, 16:24], cb[:, 0:8], cum[:, 16:24], ALU.add, tk)
                tk = tt(tmpc[:, 0], cu, nb_, ALU.add, tn_)
                tk2 = stt(tmpc[:, 1], lr[:, :, 8:16], -0.5, cu, ALU.mult, ALU.add)
                stt(rw[:, :, 0:8], lr[:, :, 0:8], -0.5, tmpc[:, 0], ALU.mult, ALU.add, tk)
                t_rw = ts(rw[:, :, 8:16], tmpc[:, 1], float(-0.5 * np.log(128.0)), None, ALU.add, None, tk2)
                yield True
                b = bank()
                for t in range(2):
                    tk = pe_turn(P[b][0:16, 128 * t:128 * t + 128], rw[:, t, :], t_rw, pfree[b], sig=(t == 1))
                t_rT = copy(rT[0:16, :], P[b][0:16, 0:256], tk, F)
                pfree[b] = [t_rT]
                gt["rT"] = t_rT

            dused = {}

            def gdn_blocks(par):
                while "rT" not in gt:
                    yield False
                yield eta(gt["rT"])
                t_rT = gt["rT"]
                for h in range(par, 8, 2):
                    rb = bank()
                    for j in range(2):
                        o = P[rb][:, :].rearrange("p (t a n) -> p t a n", t=2, a=2)[:, :, j, :]
                        l = bc(ident[0:16, h + 8 * j:h + 8 * j + 1], 1, 128)
                        tk = mm(o, l, rT[0:16, :].rearrange("p (t n) -> p t n", t=2), True, t_rT, pfree[rb], sig=(j == 1))
                    dt_ = Dt[h % 2]
                    ts(dt_[:, 0:256], P[rb][:, 0:256], cb[:, h:h + 1], 80.0, ALU.add, ALU.min, tk, gt["t_cb"],
                       dused.get(h % 2), F)
                    ts(dt_[:, 256:512], P[rb][:, 256:512], cb[:, 16 + h:17 + h], 80.0, ALU.add, ALU.min)
                    ta = ts(dt_[:, 512:768], P[rb][:, 256:512], cb[:, 8 + h:9 + h], 80.0, ALU.add, ALU.min)
                    pfree[rb] = [ta]
                    ta = act(dt_, dt_, ACT.Exp, ta)
                    for o_, strict in ((0, 1), (128, 0), (512, 1), (640, 0)):
                        d = dt_[:, o_:o_ + 128]
                        tp3 = op("pool", lambda e, d=d, s=strict: e.affine_select(
                            out=d, in_=d, pattern=[[1, 128]], compare_op=ALU.is_ge, fill=0.0, base=-s,
                            channel_multiplier=-1), ta)
                    gt[("exp", h)] = True
                    if ("exp", 6) in gt and ("exp", 7) in gt:
                        table("silu_and_others")
                        gt["silu2"] = True
                    yield True
                    kb = bank()
                    kb2 = bank()
                    for j, src in enumerate((kS, qS)):
                        o = P[kb][:, :].rearrange("p (t a n) -> p t a n", t=2, a=2)[:, :, j, :]
                        mm(o, kS[:, h, 0:128], src[:, h, :].rearrange("p (t n) -> p t n", t=2), True, pfree[kb])
                        tk = mm(P[kb2][:, 128 * j:128 * j + 128], kS[:, h, 128:256], src[:, h, 128:256], True, pfree[kb2],
                                sig=(j == 1))
                    t1 = stt(BA[:, h, 0:512], P[kb][:, :], -1.0, dt_[:, 0:512], ALU.mult, ALU.mult, tk, tp3, F)
                    t2 = stt(BA[:, h, 512:768], P[kb2][:, 0:256], -1.0, dt_[:, 512:768], ALU.mult, ALU.mult)
                    pfree[kb], pfree[kb2] = [t1], [t2]
                    dused[h % 2] = t2
                    gt[("B", h)] = t2
                    gt["kq", par] = tk
                    yield True

            beta = keep_tile(16).rearrange("p (t n) -> p t n", t=2)
            cb = keep_tile(24)
            inv_used = {}
            xfree = []

            def silus():
                for g in range(2):
                    while ("done", "v", g) not in gt or "silu2" not in gt:
                        yield False
                    tk = act(vS[g], vS[g], ACT.Silu, gt[("vc", g)])
                    yield True
                    for hp in range(2):
                        b = bank()
                        for j in range(2):
                            for t in range(2):
                                tp2 = pe_turn(P[b][:, 256 * j + 128 * t:256 * j + 128 * t + 128],
                                              vS[g][:, 2 * hp + j, 128 * t:128 * t + 128], tk, pfree[b],
                                              sig=(j == 1 and t == 1))
                        h0 = 4 * g + 2 * hp
                        src = P[b][:, :].rearrange("p (j t n) -> p j t n", j=2, t=2)
                        for t in range(2):
                            tv = tt(Vt[:, t, h0:h0 + 2, :], src[:, :, t, :], bc(beta[:, t, h0:h0 + 2].unsqueeze(2), 2, 128),
                                    ALU.mult, tp2, gt["t_beta"], F)
                        pfree[b] = [tv]
                        gt[("v", h0)] = gt[("v", h0 + 1)] = tv
                        yield True
                for g in range(2):
                    while ("z", g) not in gt or ("done", "z", g) not in gt:
                        yield False
                    gt[("zs", g)] = act(zT[:, 4 * g:4 * g + 4, :], zT[:, 4 * g:4 * g + 4, :], ACT.Silu, gt[("z", g)])
                    yield True
                table("natural_log_exp_and_others")
                gt["exp2"] = True

            def invert(g, sl):
                ops = (oth, otl) if sl < 2 else (xh.rearrange("p k n -> p (k n)"), xl.rearrange("p k n -> p (k n)"))
                q = [x[:, 1024 * (sl % 2) + 512 * i:1024 * (sl % 2) + 512 * i + 512] for x in ops for i in range(2)]
                Xb, Yb, Wb, Bb = q
                while ("B", 2 * g + 1) not in gt or (sl >= 2 and not xfree):
                    yield False
                bt = [gt[("B", 2 * g)], gt[("B", 2 * g + 1)], F, xfree if sl >= 2 else None, t_idr]
                v4 = lambda a: a.rearrange("p (b n) -> p b n", b=4)
                blk = lambda i: BA[:, 2 * g + i // 2, 512 * (i % 2):512 * (i % 2) + 128]
                sl_ = lambda i: slice(128 * i, 128 * i + 128)
                idb = bc(ident.unsqueeze(1), 1, 4)
                src = BA[:, 2 * g:2 * g + 2, :].rearrange("p h (z n) -> p h z n", z=6)[:, :, 0:5:4, :]

                def level(l, *tokens):
                    m = bc(bc(level_mask[:, l, :].unsqueeze(1), 1, 2).unsqueeze(2), 2, 2)
                    return tt(Bb.rearrange("p (h z n) -> p h z n", h=2, z=2), src, m, ALU.mult, bt, tokens,
                              eng="pool" if l else "dve")

                tb_ = level(0)
                yield eta(tb_)
                b = bank()
                mm(P[b][:, :], identr, bc(identr.unsqueeze(1), 1, 4), True, pfree[b])
                for i in range(4):
                    tk = mm(P[b][:, sl_(i)], Bb[:, sl_(i)], identr, False, tb_, sig=(i == 3))
                ty = tt(v4(Yb), idb, v4(Bb).bitcast(F32), ALU.add, tb_)
                tx = act(Xb, P[b][:, :], ACT.Copy, tk, bt)
                pfree[b] = [tx]
                tb_ = level(1, ty, tk)
                yield eta(tx, tb_)
                for l in range(1, 7):
                    b = bank()
                    for i in range(4):
                        tk = mm(P[b][:, sl_(i)], Bb[:, sl_(i)], Xb[:, sl_(i)], True, tx, tb_, pfree[b], sig=(i == 3))
                    tw = act(Wb, P[b][:, :], ACT.Copy, tk, bt)
                    pfree[b] = [tw]
                    if l < 6:
                        tb_ = level(l + 1, tk)
                    yield eta(tw, ty)
                    b = bank()
                    mm(P[b][:, :], identr, Xb, True, tx, pfree[b])
                    for i in range(4):
                        tk2 = mm(P[b][:, sl_(i)], Yb[:, sl_(i)], Wb[:, sl_(i)], False, tw, ty, sig=(i == 3))
                    if l < 6:
                        b2 = bank()
                        mm(P[b2][:, :], identr, Yb, True, pfree[b2])
                        for i in range(4):
                            tk = mm(P[b2][:, sl_(i)], Wb[:, sl_(i)], Yb[:, sl_(i)], False, sig=(i == 3))
                    tx = copy(Xb, P[b][:, :], tk2)
                    pfree[b] = [tx]
                    if l < 6:
                        ty = act(Yb, P[b2][:, :], ACT.Copy, tk)
                        pfree[b2] = [ty]
                    yield eta(tx, tb_ if l < 6 else None)
                while ("B", 6) not in gt or ("B", 7) not in gt:
                    yield False
                Xf = Xb.bitcast(F32)
                b = bank()
                for i in range(4):
                    tk = mm(P[b][:, sl_(i)], blk(i), Xf[:, sl_(i)], True, tx, pfree[b], sig=(i == 3))
                b2 = bank()
                for i in range(4):
                    tk2 = pe_turn(P[b2][:, sl_(i)], Xf[:, sl_(i)], pfree[b2], sig=(i == 3))
                Ys = Ya[:, g, :]
                tr = tt(v4(Ys), idb, v4(Xf), ALU.subtract, tx, gt["kq", 0], gt["kq", 1])
                tr = tt(Wb, P[b][:, :], Ys, ALU.add, tr, tk)
                pfree[b] = [tr]
                ty = act(Yb, P[b2][:, :], ACT.Copy, tk2)
                pfree[b2] = [ty]
                yield eta(tr, ty)
                b = bank()
                for i in range(4):
                    tk = mm(P[b][:, sl_(i)], Wb[:, sl_(i)], Yb[:, sl_(i)], True, tr, ty, pfree[b], sig=(i == 3))
                ty = tt(Ys, P[b][:, :], Yb.bitcast(F32), ALU.add, tk)
                pfree[b] = [ty]
                inv_used[g] = [ty, tk]
                gt[("Y", g)] = ty
                yield True

            sol_used = {}
            Ub = [view(18944 + 256 * i, 256) for i in range(4)]

            def solve(h):
                g, i = h // 2, 2 * (h % 2)
                while ("Y", g) not in gt or ("v", h) not in gt:
                    yield False
                yield eta(gt["Y", g], gt["v", h])
                U = Ub[h % 4]
                us = sol_used.get(h % 4)
                Y0, Y1 = Ya[:, g, 128 * i:128 * i + 128], Ya[:, g, 128 * i + 128:128 * i + 256]
                b = bank()
                tk = mm(P[b][:, 0:128], Y0, Vt[:, 0, h, :], True, gt[("Y", g)], gt[("v", h)], pfree[b], sig=True)
                tu = act(U[:, 0:128], P[b][:, 0:128], ACT.Copy, tk, us, gt["kq", 0], gt["kq", 1])
                pfree[b] = [tu]
                yield True
                b = bank()
                tk = mm(P[b][:, 0:128], BA[:, h, 256:384], U[:, 0:128], True, tu, pfree[b], sig=True)
                tr_ = tt(U[:, 128:256], P[b][:, 0:128], Vt[:, 1, h, :], ALU.add, tk, us)
                pfree[b] = [tr_]
                yield True
                b = bank()
                tk = mm(P[b][:, 0:128], Y1, U[:, 128:256], True, tr_, pfree[b], sig=True)
                tu1 = act(U[:, 128:256], P[b][:, 0:128], ACT.Copy, tk)
                pfree[b] = [tu1]
                yield True
                b = bank()
                mm(P[b][:, 0:128], BA[:, h, 128:256], U[:, 0:128], True, tu, pfree[b])
                mm(P[b][:, 128:256], BA[:, h, 384:512], U[:, 0:128], True)
                tk = mm(P[b][:, 128:256], BA[:, h, 640:768], U[:, 128:256], False, tu1, sig=True)
                sol_used[h % 4] = tk
                ta = act(BA[:, h, 0:256], P[b][:, 0:256], ACT.Copy, tk, scale=-1.0)
                pfree[b] = [ta]
                gt[("o", h)] = ta
                yield True

            def gdn_out():
                for h0 in range(0, 8, 2):
                    while not (("o", h0) in gt and ("o", h0 + 1) in gt and "exp2" in gt and ("Y", 2 + h0 // 4) in gt):
                        yield False
                    tko = [gt[("o", h0)], gt[("o", h0 + 1)]]
                    i = h0 // 2 % 2
                    sq5 = pre[i].rearrange("p (h n) -> p h n", h=2)
                    ss4 = small_tile(4)
                    ta = act(sq5, BA[:, h0:h0 + 2, 0:256], ACT.Square, *tko, preu.get(i))
                    tv = op("dve", lambda e, ss4=ss4, i=i: e.reduce_sum(
                        ss4, pre[i].rearrange("p (a n) -> p a n", a=4), AX), ta)
                    preu[i] = tv
                    r4, tr4 = rsqrt(ss4, 4, 1.0 / 128, tv)
                    for j in range(2):
                        o2 = BA[:, h0 + j, 0:256].rearrange("p (t n) -> p t n", t=2)
                        tk = tt(o2, o2, bc(r4[:, 2 * j:2 * j + 2].unsqueeze(2), 2, 128), ALU.mult, tr4, ta)
                    yield True
                    b = bank()
                    for j in range(2):
                        for t in range(2):
                            tq = pe_turn(P[b][:, 256 * j + 128 * t:256 * j + 128 * t + 128],
                                         BA[:, h0 + j, 128 * t:128 * t + 128], tk, pfree[b], sig=(j == 1 and t == 1))
                    dz = zT[:, h0:h0 + 2, :]
                    tz = stt(dz, P[b][:, :].rearrange("p (h n) -> p h n", h=2), C("gdno"), dz, ALU.mult, ALU.mult, tq,
                             gt[("zs", 0)], gt[("zs", 1)])
                    pfree[b] = [tz]
                    ta = act(xh[:, h0:h0 + 2, :], dz, ACT.Copy, tz, xfree, gt["Y", 2 + h0 // 4], inv_used[2 + h0 // 4])
                    tv = tt(xl[:, h0:h0 + 2, :], dz, xh[:, h0:h0 + 2, :], ALU.subtract, ta, xfree)
                    ot_t[h0] = ot_t[h0 + 1] = [ta, tv]
                    yield True

            def mark():
                xfree.append((done["pe"], count["pe"]))
                while not (("done", "z", 0) in gt and ("done", "z", 1) in gt):
                    yield False
                spare[:] = list(range(8))
                while not (1 in ot_t and ("Y", 3) in gt):
                    yield False
                spare[:] = [4, 5, 6, 7]
                ring[0] = 4

            order = [("k", 0), ("q", 0), ("k", 1), ("q", 1), ("v", 0), ("v", 1), ("z", 0), ("z", 1)]
            vfree = []

            def vmark():
                while ("done", "q", 1) not in gt:
                    yield False
                vfree.extend([accu[i] for i in accu])

            main = chain(*[gdn_proj(nm, g, 2 * (i % 2)) for i, (nm, g) in enumerate(order)], mark(),
                         o_product(lambda k, t: xh[:, k, 128 * t:128 * t + 128],
                                   lambda k, t: xl[:, k, 128 * t:128 * t + 128]))
            convs = chain(*[gdn_conv(nm, g) for nm, g in order[:4]], vmark(), *[gdn_conv(nm, g) for nm, g in order[4:]])
            table("silu_and_others")
            s_main = [main, (convs, 3), (gdn_stats(), 1), (gdn_blocks(0), 1), (gdn_blocks(1), 1), (silus(), 3), (invert(0, 0), 1), (invert(1, 1), 1), (invert(2, 2), 1), (invert(3, 3), 1),
                      (chain(*[solve(h) for h in (0, 4)]), 1), (chain(*[solve(h) for h in (1, 5)]), 1),
                      (chain(*[solve(h) for h in (2, 6)]), 1), (chain(*[solve(h) for h in (3, 7)]), 1),
                      (gdn_out(), 1)]
            weave(*s_main)
            gn, t_gn = post_row("gdn_post_norm_2", 17408, fence())
            tX = post_norm(final, gn, t_gn, 0, fence())

        if stop >= 6:
            F = stage()
            evac.clear()
            V = view(0, 2048, "p (t n) -> p t n", t=2)
            kT = view(2048, 2048, "p (h n) -> p h n", h=8)
            qT = view(4096, 2048, "p (h n) -> p h n", h=8)
            bufs = {"q": view(6144, 1024, "p (t n) -> p t n", t=2), "k": view(7168, 1024, "p (t n) -> p t n", t=2)}
            zT = view(8192, 2048, "p (h n) -> p h n", h=8)
            sqs = [view(10240 + 512 * i, 512) for i in range(2)]
            rq = view(11264, 16, "p (t h) -> p t h", t=2)
            bb = [view(13984 + 384 * i, 384) for i in range(4)]
            gz = [view(15520 + 256 * i, 256) for i in range(2)]
            cT_ = view(16032, 256)
            rbc = view(16288, 256)
            junk = view(18432, 1024)
            xh2 = oth[:, :].rearrange("p (k n) -> p k n", k=8)
            xl2 = otl[:, :].rearrange("p (k n) -> p k n", k=8)
            gnf, t_gnf = post_row("fox_post_norm_2", 17000, F)
            sq_used.clear()
            sq_used.update({0: F, 1: F})
            xt2, xt = transposed(tX, ("foxpre", xh2, xl2), ("kvn", xh, xl), free=F)
            ss, tk = mean_squares(junk, tX, F)
            r1 = rsqrt(ss, 2, 1.0 / D, tk, F, out_=keep_tile(2))
            gf = keep_tile(1)
            t_gf = tt(gf, C("foxq"), C("foxk"), ALU.mult, IN, F)
            fx, lf = (keep_tile(16).rearrange("p (t n) -> p t n", t=2) for _ in range(2))
            cc, cn = keep_tile(16), keep_tile(16)
            fs = {}

            def fox_z():
                for g in range(2):
                    toks = {}
                    yield from proj_w(2 * g, xh2, xl2, xt2, toks)
                    if g == 0:
                        fs["rbc"] = across(r1[0], rbc, r1[1], F)
                    for half in range(2):
                        b = 2 * g + half
                        d = zT[:, 4 * g + 2 * half:4 * g + 2 * half + 2, :]
                        tk = tt(d, P[b][:, :].rearrange("p (m n) -> p m n", m=2), bc(rbc.unsqueeze(1), 1, 2), ALU.mult,
                                toks[half], fs["rbc"], F)
                        pfree[b] = [tk]
                    fs["z", g] = tk
                    if g == 0:
                        table("silu_and_others")
                    tz = act(zT[:, 4 * g:4 * g + 4, :], zT[:, 4 * g:4 * g + 4, :], ACT.Silu, tk)
                    fs["zs"] = tz
                table("natural_log_exp_and_others")

            def fox_f():
                tok = proj_few(8, xh, xl, xt)
                e0, e1, e2 = (small_tile(16).rearrange("p (t n) -> p t n", t=2) for _ in range(3))
                for t in range(2):
                    tk = stt(fx[:, t, :], P[t][:, 0:8], r1[0][:, t:t + 1], RW("fbias"), ALU.mult, ALU.add, tok, IN, F)
                    pfree[t] = [tk]
                ta = act(e0, fx, ACT.Abs, tk)
                ta = act(e1, e0, ACT.Exp, ta, scale=-1.0)
                table("natural_log")
                ta = act(e2, e1, ACT.Ln, ta, bias=1.0)
                table("natural_log_exp_and_others")
                fs["lf"] = stt(lf, fx, 0.0, e2, ALU.min, ALU.subtract, ta)
                yield True

            def fox_c():
                while "lf" not in fs:
                    yield False
                b = bank()
                mm(P[b][:, 0:8], K("tri"), lf[:, 0, :], True, fs["lf"], pfree[b])
                mm(P[b][:, 8:16], K("ones"), lf[:, 0, :], True)
                tk = mm(P[b][:, 8:16], K("tri"), lf[:, 1, :], False, sig=True)
                copy(cc, P[b][:, 0:16], tk, F)
                t_c = ts(cn, P[b][:, 0:16], -1.0, None, ALU.mult, None, tk)
                pfree[b] = [t_c]
                yield True
                b = bank()
                for t in range(2):
                    tk = pe_turn(P[b][0:8, 128 * t:128 * t + 128], cn[:, 8 * t:8 * t + 8], t_c, pfree[b], sig=(t == 1))
                t_cT = copy(cT_[0:8, :], P[b][0:8, 0:256], tk, F)
                pfree[b] = [t_cT]
                fs["cT"] = t_cT
                yield True
                for h in range(8):
                    while h >= 4 and h - 4 not in fb_used:
                        yield False
                    b = bank()
                    tk = mm(P[b][:, 0:256], bc(ident[0:8, h:h + 1], 1, 128), cT_[0:8, :], True, t_cT, pfree[b], sig=True)
                    d = bb[h % 4]
                    m = K("mask")
                    stt(d[:, 0:128], P[b][:, 0:128], cc[:, h:h + 1], m[:, 0:128], ALU.add, ALU.add, tk, F, fb_used.get(h - 4))
                    tk = stt(d[:, 128:384], P[b][:, 0:256], cc[:, 8 + h:9 + h], m[:, 128:384], ALU.add, ALU.add)
                    pfree[b] = [tk]
                    fb[h] = (d, tk, lambda t_, h=h: fb_used.__setitem__(h, t_))
                    yield True

            fb, fb_used, gz_used = {}, {}, {}

            def fox_keep(h, b, tk):
                g_ = gz[h % 2]
                tv0 = tt(g_, P[b][:, 0:256], zT[:, h, :], ALU.mult, tk, fs["zs"], gz_used.get(h % 2), F)
                qd = evac[("pe", "q", 1)]
                ta = act(xh2[:, h, :], g_, ACT.Copy, tv0, qd)
                tv = tt(xl2[:, h, :], g_, xh2[:, h, :], ALU.subtract, ta, qd)
                gz_used[h % 2] = tv
                ot_t[h] = [ta, tv]
                return [tv0]

            bufF = [F, t_gf]
            seq = [(0, "k"), (0, "v"), (0, "q"), (1, "q"), (1, "k"), (1, "v")]
            main = chain(fox_z(), fox_f(), *[
                heads_main(g, w_, 2 * (i_ % 2), xh2 if w_ == "q" else xh, xl2 if w_ == "q" else xl,
                           xt2 if w_ == "q" else xt, r1, bufs, V, bufF) for i_, (g, w_) in enumerate(seq)], o_product())
            post = chain(*[heads_post(g, w_, bufs, qT, kT, gf, rq, sqs, bufF) for g, w_ in seq if w_ != "v"])

            def fox_gate():
                while ("pe", "q", 1) not in evac:
                    yield False
                yield from when_ready(0)
                yield from when_ready(1)

            attn = attention(range(8), lambda h: qT[:, h, :], lambda h: kT[:, h, :],
                             lambda h, t: V[:, t, 128 * h:128 * h + 128],
                             lambda h: ([rq[:, t, h:h + 1] for t in range(2)], ready[("rq", h // 4)]),
                             lambda h: fb[h], 11296, fox_keep, after=F)
            weave(main, (post, 1), (fox_c(), 1), (fox_gate(), 1), (attn, 0))
            tX = post_norm(final, gnf, t_gnf, 0, fence())
        finish(tX)

        block = ctx.enter_context(nc.Block())

        def play(eng, entries):
            for kind, a, b, *n in entries:
                if kind == "wait":
                    eng.wait_ge(a, b)
                else:
                    ins = a(eng)
                    if b is not None:
                        ins.then_inc(b, n[0])

        @block.sync
        def _(eng):
            play(eng, queue["sp"])

        @block.scalar
        def _(eng):
            play(eng, queue["act"])

        @block.vector
        def _(eng):
            play(eng, queue["dve"])

        @block.gpsimd
        def _(eng):
            play(eng, queue["pool"])

        @block.tensor
        def _(eng):
            play(eng, queue["pe"])


def constants():
    c = np.zeros((128, NCST), np.float32)
    p = np.arange(128)
    c[:, 0:128] = np.eye(128, dtype=np.float32)
    causal = np.where(p[None, :] <= p[:, None], 0.0, NEG)
    c[:, 128:256] = causal
    c[:, 384:512] = causal
    c[:, 512:640] = p[:, None] <= p[None, :]
    c[:, 640:768] = 1.0
    limits = [-1.0e9] + list(range(1, 17)) + [21, 27, 35, 46, 59, 77, 99, 128, 166, 216, 280, 363, 470, 609, 790]
    c[:, 768] = np.tile(np.array(limits, np.float32), 4)
    pred = np.zeros((128, 7, 128), np.float32)
    for l in range(7):
        s = 1 << l
        m = ((p[:, None] // (2 * s)) == (p[None, :] // (2 * s))) & ((p[:, None] // s) % 2 == 0) & ((p[None, :] // s) % 2 == 1)
        pred[:, l] = m
    return c, pred.reshape(128, 896)


def kernel(**inputs):
    import numpy as _np
    import concourse.bacc as _bacc
    from concourse import mybir as _mybir
    from concourse.bass_utils import run_bass_kernel_spmd as _run

    a = {k: _np.ascontiguousarray(v) for k, v in inputs.items()}
    col = lambda v: v.reshape(-1, 128).T
    cols = _np.ascontiguousarray(_np.concatenate([
        col(a["attn_norm"][0]), col(a["attn_norm"][1]), col(a["mlp_norm"][0]), col(a["mlp_norm"][1]),
        col(a["gdn_pre_norm_2"][0]), col(a["kv_norm_2"]), col(a["fox_pre_norm_2"][0]), col(a["mla_q_a_norm"][0]),
        col(a["mla_kv_a_norm"][0]), col(a["mla_q_nope_norm"][0]), col(a["mla_k_nope_norm"][0]),
        col(a["moba_q_norm"][0]), col(a["moba_k_norm"][0]), col(a["kv_k_norm_2"]), col(a["fox_q_norm_2"][0]),
        col(a["gdn_o_norm_2"][0]),
        a["gdn_conv_w_2"][0].reshape(4, 24, 128).transpose(2, 1, 0).reshape(128, 96)], axis=1))
    invf = _np.float32(10000.0) ** (-_np.arange(0, 64, 2, dtype=_np.float32) / _np.float32(64))
    rows = _np.concatenate([a["mla_q_rope_norm"][0], a["mla_k_rope_norm"][0], a["gdn_a_log_2"][0],
                            a["gdn_dt_bias_2"][0], a["kv_forget_bias_2"], invf.astype(_np.float32)])
    cst, pred = constants()
    arrays = {
        "x": a["x"][0], "positions": a["positions"], "rel_bias_table": a["rel_bias_table"],
        "mla_w_in": a["mla_w_in"][0], "mla_w_uq": a["mla_w_uq"][0], "mla_w_ukv": a["mla_w_ukv"][0],
        "mla_w_o": a["mla_w_o"][0], "moba_w_qkv": a["moba_w_qkv"][0], "moba_w_o": a["moba_w_o"][0],
        "mlp_w_in": a["mlp_w_in"], "mlp_w_out": a["mlp_w_out"], "gdn_w_in": a["gdn_w_in_2"][0],
        "gdn_w_out": a["gdn_w_out_2"][0], "kv_w": a["kv_w_2"], "fox_w_in": a["fox_w_in_2"][0],
        "fox_w_out": a["fox_w_out_2"][0], "gdn_post_norm_2": a["gdn_post_norm_2"][0],
        "fox_post_norm_2": a["fox_post_norm_2"][0],
        "c_cols": cols, "c_rows": rows, "c_cst": cst, "c_pred": pred,
        "c_posT": _np.ascontiguousarray(a["positions"].reshape(2, 128).T),
    }
    arrays = {k + "_dram": _np.ascontiguousarray(v) for k, v in arrays.items()}
    nc = _bacc.Bacc("TRN2", target_bir_lowering=False, num_devices=1)
    aps = {k[:-5]: nc.dram_tensor(k, v.shape, _mybir.dt.from_np(v.dtype), kind="ExternalInput").ap()
           for k, v in arrays.items()}
    out = nc.dram_tensor("out_dram", (256, 1024), _mybir.dt.float32, kind="ExternalOutput").ap()
    bass_two_blocks(nc, aps, out)
    r = _run(nc, [arrays], core_ids=[0])
    return r.results[0]["out_dram"].reshape(1, 256, 1024)
```
